# Optimizing a Trainium2 kernel written in Bass

```python
import math
import jax, jax.numpy as jnp
from jax import lax
import numpy as np

D_MODEL = 2048
BATCH = 1
SEQ = 256
DEPTH = 1

MIX_WIDTH = D_MODEL
ATTN_HEAD_DIM = 64
ATTN_WIDTH = MIX_WIDTH // 2
ATTN_HEADS = ATTN_WIDTH // ATTN_HEAD_DIM
DILATION_PATTERNS = ((128, 1), (512, 4), (2048, 16))
QBLK = 128
GLA_WIDTH = MIX_WIDTH - ATTN_WIDTH
GLA_HEADS = 4
GLA_KEY_WIDTH = GLA_WIDTH // 2
GLA_HEAD_DK = GLA_KEY_WIDTH // GLA_HEADS
GLA_HEAD_DV = GLA_WIDTH // GLA_HEADS
GLA_GATE_RANK = 16
GLA_GATE_TAU = 16.0
GLA_CHUNK = 64
FFN_HIDDEN = -(-(8 * D_MODEL) // (3 * 256)) * 256
REL_BUCKETS = 32
REL_MAX_DISTANCE = 1024
NORM_EPS = 1e-6
IN_SIZES = (ATTN_WIDTH, ATTN_WIDTH, ATTN_WIDTH,
            GLA_KEY_WIDTH, GLA_KEY_WIDTH, GLA_WIDTH, GLA_WIDTH, 2 * GLA_GATE_RANK)
IN_WIDTH = 3 * ATTN_WIDTH + 2 * GLA_KEY_WIDTH + 2 * GLA_WIDTH + 2 * GLA_GATE_RANK


def rmsnorm(x, w):
    x32 = x.astype(jnp.float32)
    y = x32 * lax.rsqrt(jnp.mean(x32 * x32, axis=-1, keepdims=True) + NORM_EPS)
    return y.astype(x.dtype) * w

def _t5_bucket(rel):
    nb = REL_BUCKETS // 2
    ret = np.where(rel > 0, nb, 0)
    n = np.abs(rel)
    max_exact = nb // 2
    large = max_exact + (np.log(np.maximum(n, 1) / max_exact)
                         / math.log(REL_MAX_DISTANCE / max_exact)
                         * (nb - max_exact)).astype(np.int64)
    large = np.minimum(large, nb - 1)
    return (ret + np.where(n < max_exact, n, large)).astype(np.int32)

def _band_layout(L, radius, dilation):
    nb = -(-L // QBLK)
    span = QBLK + 2 * radius
    key_idx = np.arange(nb)[:, None] * QBLK + np.arange(span)[None, :]
    kpos = key_idx - radius
    qpos = np.arange(nb)[:, None] * QBLK + np.arange(QBLK)[None, :]
    off = kpos[:, None, :] - qpos[:, :, None]
    valid = (np.abs(off) <= radius) & (kpos[:, None, :] >= 0) & (kpos[:, None, :] < L)
    bucket = _t5_bucket(off[0] * dilation)
    return nb, key_idx, valid, bucket

def _from_sub(t, L, S):
    B, H, r = t.shape[:3]
    rest = t.shape[5:]
    t = t.reshape((B, H, r, -1) + rest)[:, :, :, :L]
    t = jnp.swapaxes(t, 2, 3)
    return t.reshape((B, H, S) + rest)

def dilated_window_attention(q, k, v, rel_table, window, dilation):
    B, H, S, Dh = q.shape
    L = S // dilation
    R = (window // 2) // dilation
    nb, key_idx, valid, bucket = _band_layout(L, R, dilation)
    Lp = nb * QBLK

    def to_sub(t):
        return t.reshape(B, H, L, dilation, Dh).transpose(0, 1, 3, 2, 4)

    zpad = ((0, 0), (0, 0), (0, 0))
    qs = jnp.pad(to_sub(q), zpad + ((0, Lp - L), (0, 0)))
    ks = jnp.pad(to_sub(k), zpad + ((R, Lp - L + R), (0, 0)))
    vs = jnp.pad(to_sub(v), zpad + ((R, Lp - L + R), (0, 0)))
    qb = qs.reshape(B, H, dilation, nb, QBLK, Dh)
    kb = ks[:, :, :, key_idx]
    vb = vs[:, :, :, key_idx]

    bias = jnp.transpose(rel_table[bucket].astype(jnp.float32), (2, 0, 1))
    logits = (jnp.einsum('bhrnqd,bhrnkd->bhrnqk', qb, kb).astype(jnp.float32)
              * (Dh ** -0.5) + bias[None, :, None, None])
    logits = jnp.where(valid[None, None, None], logits, -1e30)
    m = jnp.max(logits, axis=-1, keepdims=True)
    p = jnp.exp(logits - m)
    s = jnp.sum(p, axis=-1, keepdims=True)
    o = jnp.einsum('bhrnqk,bhrnkd->bhrnqd', p, vb.astype(jnp.float32)) / s
    lse = (m + jnp.log(s))[..., 0]
    return _from_sub(o, L, S), _from_sub(lse, L, S)

def mixture_of_dilations(q, k, v, rel_table):
    outs, lses = [], []
    for window, dilation in DILATION_PATTERNS:
        o, l = dilated_window_attention(q, k, v, rel_table, window, dilation)
        outs.append(o)
        lses.append(l)
    w = jax.nn.softmax(jnp.stack(lses, axis=0), axis=0)
    out = sum(w[i][..., None] * outs[i] for i in range(len(outs)))
    return out

def gla_causal(q, k, v, log_a):
    B, H, S, Dk = q.shape
    Dv = v.shape[-1]
    n = S // GLA_CHUNK
    qc = q.astype(jnp.float32).reshape(B, H, n, GLA_CHUNK, Dk)
    kc = k.astype(jnp.float32).reshape(B, H, n, GLA_CHUNK, Dk)
    vc = v.astype(jnp.float32).reshape(B, H, n, GLA_CHUNK, Dv)
    G = jnp.cumsum(log_a.astype(jnp.float32).reshape(B, H, n, GLA_CHUNK, Dk), axis=-2)
    q_in = qc * jnp.exp(G)
    k_in = kc * jnp.exp(-G)
    tril = jnp.tril(jnp.ones((GLA_CHUNK, GLA_CHUNK), jnp.float32))
    A = jnp.einsum('bhncd,bhnjd->bhncj', q_in, k_in) * tril
    intra = jnp.einsum('bhncj,bhnjv->bhncv', A, vc)
    G_last = G[..., -1:, :]
    k_end = kc * jnp.exp(G_last - G)
    U = jnp.einsum('bhnjd,bhnjv->bhndv', k_end, vc)
    decay = jnp.exp(G_last[..., 0, :])

    def step(state, inp):
        dec, u = inp
        return state * dec[..., None] + u, state

    _, S_prev = lax.scan(step, jnp.zeros((B, H, Dk, Dv), jnp.float32),
                         (jnp.moveaxis(decay, 2, 0), jnp.moveaxis(U, 2, 0)))
    S_prev = jnp.moveaxis(S_prev, 0, 2)
    inter = jnp.einsum('bhncd,bhndv->bhncv', q_in, S_prev)
    return (intra + inter).reshape(B, H, S, Dv)

def _heads(t, n_heads):
    B, S, W = t.shape
    return t.reshape(B, S, n_heads, W // n_heads).transpose(0, 2, 1, 3)

def _merge_heads(t):
    B, H, S, Dh = t.shape
    return t.transpose(0, 2, 1, 3).reshape(B, S, H * Dh)

def first_inputs(seed: int = 0) -> dict:
    key = jax.random.key(seed)
    ks = jax.random.split(key, 16)
    f32 = jnp.float32
    nrm = lambda k, shape, scale: jax.random.normal(k, shape, f32) * scale
    return {
        "x": nrm(ks[0], (BATCH, SEQ, D_MODEL), 1.0),
        "attn_norm_w": 1.0 + nrm(ks[1], (DEPTH, D_MODEL), 0.02),
        "w_in": nrm(ks[2], (DEPTH, D_MODEL, IN_WIDTH), D_MODEL ** -0.5),
        "rel_bias_table": nrm(ks[3], (REL_BUCKETS, ATTN_HEADS), 0.3),
        "gla_gate_w_fwd": nrm(ks[4], (DEPTH, GLA_GATE_RANK, GLA_KEY_WIDTH), GLA_GATE_RANK ** -0.5),
        "gla_gate_b_fwd": nrm(ks[5], (DEPTH, GLA_KEY_WIDTH), 0.1),
        "gla_gate_w_bwd": nrm(ks[6], (DEPTH, GLA_GATE_RANK, GLA_KEY_WIDTH), GLA_GATE_RANK ** -0.5),
        "gla_gate_b_bwd": nrm(ks[7], (DEPTH, GLA_KEY_WIDTH), 0.1),
        "gla_norm_w": 1.0 + nrm(ks[8], (DEPTH, GLA_WIDTH), 0.02),
        "w_out": nrm(ks[9], (DEPTH, MIX_WIDTH, D_MODEL), MIX_WIDTH ** -0.5),
        "ffn_norm_w": 1.0 + nrm(ks[10], (DEPTH, D_MODEL), 0.02),
        "w_gate": nrm(ks[11], (DEPTH, D_MODEL, FFN_HIDDEN), D_MODEL ** -0.5),
        "w_up": nrm(ks[12], (DEPTH, D_MODEL, FFN_HIDDEN), D_MODEL ** -0.5),
        "w_down": nrm(ks[13], (DEPTH, FFN_HIDDEN, D_MODEL), FFN_HIDDEN ** -0.5),
        "final_norm_w": 1.0 + nrm(ks[14], (D_MODEL,), 0.02),
    }

def first_block(x, attn_norm_w, w_in, rel_bias_table, gla_gate_w_fwd, gla_gate_b_fwd,
              gla_gate_w_bwd, gla_gate_b_bwd, gla_norm_w, w_out, ffn_norm_w,
              w_gate, w_up, w_down, final_norm_w):
    split_idx = []
    acc = 0
    for size in IN_SIZES[:-1]:
        acc += size
        split_idx.append(acc)

    for l in range(DEPTH):
        h = rmsnorm(x, attn_norm_w[l])
        proj = h @ w_in[l]
        aq, ak, av, gq, gk, gv, gr, glr = jnp.split(proj, split_idx, axis=-1)

        attn = mixture_of_dilations(_heads(aq, ATTN_HEADS), _heads(ak, ATTN_HEADS),
                                    _heads(av, ATTN_HEADS), rel_bias_table)
        attn_out = _merge_heads(attn).astype(x.dtype)

        lr_f, lr_b = glr[..., :GLA_GATE_RANK], glr[..., GLA_GATE_RANK:]
        log_a_f = jax.nn.log_sigmoid((lr_f @ gla_gate_w_fwd[l] + gla_gate_b_fwd[l])
                                     .astype(jnp.float32)) / GLA_GATE_TAU
        log_a_b = jax.nn.log_sigmoid((lr_b @ gla_gate_w_bwd[l] + gla_gate_b_bwd[l])
                                     .astype(jnp.float32)) / GLA_GATE_TAU
        qh = _heads(gq, GLA_HEADS) * (GLA_HEAD_DK ** -0.5)
        kh = _heads(gk, GLA_HEADS)
        vh = _heads(gv, GLA_HEADS)
        fwd = gla_causal(qh, kh, vh, _heads(log_a_f, GLA_HEADS))
        flip = lambda t: jnp.flip(t, axis=2)
        bwd = flip(gla_causal(flip(qh), flip(kh), flip(vh), flip(_heads(log_a_b, GLA_HEADS))))
        o = fwd + bwd
        o = o * lax.rsqrt(jnp.mean(o * o, axis=-1, keepdims=True) + NORM_EPS)
        gla_out = (_merge_heads(o).astype(x.dtype) * gla_norm_w[l]) * jax.nn.silu(gr)

        mixed = jnp.concatenate([attn_out, gla_out], axis=-1) @ w_out[l]
        x = x + mixed

        h = rmsnorm(x, ffn_norm_w[l])
        x = x + (jax.nn.silu(h @ w_gate[l]) * (h @ w_up[l])) @ w_down[l]

    return rmsnorm(x, final_norm_w)


RET_HEADS = 4
RET_QK_DIM = 64
RET_V_DIM = 128
RET_WIDTH = RET_HEADS * RET_V_DIM
RET_CHUNK = 128
RET_COLS = 2 * RET_HEADS * RET_QK_DIM + 2 * RET_WIDTH

RWKV_HEADS = 8
RWKV_HEAD_DIM = 64
RWKV_WIDTH = RWKV_HEADS * RWKV_HEAD_DIM
RWKV_DECAY_RANK = 96
RWKV_A_RANK = 96
RWKV_GATE_RANK = 256
RWKV_GN_EPS = 64e-5
RWKV_COLS = 3 * RWKV_WIDTH + RWKV_DECAY_RANK + RWKV_A_RANK + RWKV_GATE_RANK

MOBA_HEADS = 8
MOBA_HEAD_DIM = 128
MOBA_WIDTH = MOBA_HEADS * MOBA_HEAD_DIM
MOBA_BLOCK = 256
MOBA_TOPK = 3
MOBA_Q_CHUNK = 32
MOBA_COLS = 3 * MOBA_WIDTH
NEG_INF = -1e30

MIX_WIDTH_2 = RET_WIDTH + RWKV_WIDTH + MOBA_WIDTH
IN_COLS = RET_COLS + RWKV_COLS + MOBA_COLS

D_FF = 5632
CONV_WIDTH = 3


def rms_norm(x, g):
    xf = x.astype(jnp.float32)
    y = xf * lax.rsqrt(jnp.mean(xf * xf, axis=-1, keepdims=True) + NORM_EPS)
    return (y * g.astype(jnp.float32)).astype(x.dtype)

def token_shift(x):
    return jnp.pad(x, ((0, 0), (1, 0), (0, 0)))[:, :-1]

def retention_chunkwise(q, k, v):
    B, S, H, Dk = q.shape
    Dv = v.shape[-1]
    C = RET_CHUNK
    N = S // C
    f32 = jnp.float32
    log_g = jnp.log1p(-jnp.exp2(-5.0 - jnp.arange(H, dtype=f32)))

    def chunks(a, d):
        return a.astype(f32).reshape(B, N, C, H, d).transpose(1, 0, 3, 2, 4)

    qc_all = chunks(q, Dk)
    kc_all = chunks(k, Dk) * (Dk ** -0.5)
    vc_all = chunks(v, Dv)
    idx = jnp.arange(C, dtype=f32)
    diff = idx[:, None] - idx[None, :]
    inner_decay = jnp.where(diff >= 0, jnp.exp(log_g[:, None, None] * jnp.maximum(diff, 0.0)), 0.0)
    q_decay = jnp.exp(log_g[:, None] * (idx + 1.0))[..., None]
    k_decay = jnp.exp(log_g[:, None] * (C - 1.0 - idx))[..., None]
    chunk_decay = jnp.exp(log_g * C)[:, None, None]

    def step(R, inp):
        qc, kc, vc = inp
        inner = jnp.einsum('bhid,bhjd->bhij', qc, kc) * inner_decay
        o = jnp.einsum('bhij,bhjv->bhiv', inner, vc) + jnp.einsum('bhid,bhdv->bhiv', qc, R) * q_decay
        R = R * chunk_decay + jnp.einsum('bhjd,bhjv->bhdv', kc * k_decay, vc)
        return R, o

    R0 = jnp.zeros((B, H, Dk, Dv), f32)
    _, o = lax.scan(step, R0, (qc_all, kc_all, vc_all))
    return o.transpose(1, 0, 3, 2, 4).reshape(B, S, H, Dv)

def rwkv7_time_mix(r, k, v, wd, wa, wg, w0, w_up, a0, a_up, g_up, k_k, k_a, r_k, ln_w, ln_b):
    B, S, C = r.shape
    H, N = RWKV_HEADS, RWKV_HEAD_DIM
    f32 = jnp.float32
    r, k, v = r.astype(f32), k.astype(f32), v.astype(f32)
    w_log = -jax.nn.softplus(-(w0 + jnp.tanh(wd.astype(f32)) @ w_up)) - 0.5
    decay = jnp.exp(-jnp.exp(w_log))
    a = jax.nn.sigmoid(a0 + wa.astype(f32) @ a_up)
    g = jax.nn.sigmoid(wg.astype(f32)) @ g_up
    kk = (k * k_k).reshape(B, S, H, N)
    kk = kk / jnp.maximum(jnp.sqrt(jnp.sum(kk * kk, axis=-1, keepdims=True)), 1e-12)
    k = k * (1.0 + (a - 1.0) * k_a)

    def heads_tm(z):
        return jnp.moveaxis(z.reshape(B, S, H, N), 1, 0)

    def step(state, inp):
        r_t, w_t, k_t, v_t, kk_t, a_t = inp
        sa = jnp.einsum('bhij,bhj->bhi', state, -kk_t)
        state = (state * w_t[:, :, None, :]
                 + sa[..., None] * (kk_t * a_t)[:, :, None, :]
                 + v_t[..., None] * k_t[:, :, None, :])
        y = jnp.einsum('bhij,bhj->bhi', state, r_t)
        return state, y

    s0 = jnp.zeros((B, H, N, N), f32)
    _, y = lax.scan(step, s0, (heads_tm(r), heads_tm(decay), heads_tm(k), heads_tm(v),
                               jnp.moveaxis(kk, 1, 0), heads_tm(a)))
    y = jnp.moveaxis(y, 0, 1)
    mean = jnp.mean(y, axis=-1, keepdims=True)
    var = jnp.mean((y - mean) ** 2, axis=-1, keepdims=True)
    y = ((y - mean) * lax.rsqrt(var + RWKV_GN_EPS)).reshape(B, S, C) * ln_w + ln_b
    rh, kh, vh = r.reshape(B, S, H, N), k.reshape(B, S, H, N), v.reshape(B, S, H, N)
    bonus = (jnp.sum(rh * kh * r_k, axis=-1, keepdims=True) * vh).reshape(B, S, C)
    return (y + bonus) * g

def moba_attention(q, k, v):
    B, S, H, D = q.shape
    L = MOBA_BLOCK
    NB = -(-S // L)
    P = NB * L
    topk = min(MOBA_TOPK, NB)
    QC = MOBA_Q_CHUNK
    f32 = jnp.float32
    slopes = jnp.exp2(-8.0 * jnp.arange(1, H + 1, dtype=f32) / H)
    qh = q.astype(f32).transpose(0, 2, 1, 3) * (D ** -0.5)
    pad = ((0, 0), (0, 0), (0, P - S), (0, 0))
    kh = jnp.pad(k.astype(f32).transpose(0, 2, 1, 3), pad)
    vh = jnp.pad(v.astype(f32).transpose(0, 2, 1, 3), pad)
    kb = kh.reshape(B, H, NB, L, D)
    vb = vh.reshape(B, H, NB, L, D)
    k_mean = jnp.mean(kb, axis=3)
    gate = jnp.einsum('bhsd,bhnd->bhsn', qh, k_mean)
    q_block = jnp.arange(S) // L
    fully_past = jnp.arange(NB)[None, :] < q_block[:, None]
    gate = jnp.where(fully_past, gate, -jnp.inf)
    _, sel = lax.top_k(gate, topk)
    b_ix = jnp.arange(B)[:, None, None, None]
    h_ix = jnp.arange(H)[None, :, None, None]
    offs = jnp.arange(L)

    def chunk(ci):
        q0 = ci * QC
        qc = lax.dynamic_slice_in_dim(qh, q0, QC, axis=2)
        sc = lax.dynamic_slice_in_dim(sel, q0, QC, axis=2)
        t = q0 + jnp.arange(QC)
        bq = q0 // L
        kg = kb[b_ix, h_ix, sc]
        vg = vb[b_ix, h_ix, sc]
        s_sel = jnp.einsum('bhqd,bhqnld->bhqnl', qc, kg)
        dist_sel = (t[:, None, None] - (sc[..., None] * L + offs)).astype(f32)
        s_sel = jnp.where((sc < bq)[..., None],
                          s_sel - slopes[:, None, None, None] * dist_sel, NEG_INF)
        ko = lax.dynamic_slice_in_dim(kh, bq * L, L, axis=2)
        vo = lax.dynamic_slice_in_dim(vh, bq * L, L, axis=2)
        s_own = jnp.einsum('bhqd,bhld->bhql', qc, ko)
        dist_own = t[:, None] - (bq * L + offs)[None, :]
        s_own = jnp.where(dist_own >= 0,
                          s_own - slopes[:, None, None] * dist_own.astype(f32), NEG_INF)
        scores = jnp.concatenate([s_sel.reshape(B, H, QC, topk * L), s_own], axis=-1)
        p = jax.nn.softmax(scores, axis=-1)
        p_sel = p[..., :topk * L].reshape(B, H, QC, topk, L)
        p_own = p[..., topk * L:]
        return (jnp.einsum('bhqnl,bhqnld->bhqd', p_sel, vg)
                + jnp.einsum('bhql,bhld->bhqd', p_own, vo))

    out = lax.map(chunk, jnp.arange(S // QC))
    return out.transpose(1, 0, 3, 2, 4).reshape(B, S, H * D)

def hybrid_mixer(h, w_in, w_out, mu, w0, w_up, a0, a_up, g_up, k_k, k_a, r_k, ln_w, ln_b):
    B, S, _ = h.shape
    proj = h @ w_in
    o0 = 0
    qk = RET_HEADS * RET_QK_DIM
    rq = proj[..., o0:o0 + qk].reshape(B, S, RET_HEADS, RET_QK_DIM)
    rk = proj[..., o0 + qk:o0 + 2 * qk].reshape(B, S, RET_HEADS, RET_QK_DIM)
    rv = proj[..., o0 + 2 * qk:o0 + 2 * qk + RET_WIDTH].reshape(B, S, RET_HEADS, RET_V_DIM)
    rg = proj[..., o0 + 2 * qk + RET_WIDTH:o0 + RET_COLS].astype(jnp.float32)
    ro = retention_chunkwise(rq, rk, rv)
    ro = ro * lax.rsqrt(jnp.mean(ro * ro, axis=-1, keepdims=True) + NORM_EPS)
    ret_out = ro.reshape(B, S, RET_WIDTH) * jax.nn.silu(rg)
    rw = proj[..., RET_COLS:RET_COLS + RWKV_COLS]
    rw = rw + (token_shift(rw) - rw) * mu
    c1 = RWKV_WIDTH
    c2 = 2 * RWKV_WIDTH
    c3 = 3 * RWKV_WIDTH
    c4 = c3 + RWKV_DECAY_RANK
    c5 = c4 + RWKV_A_RANK
    rwkv_out = rwkv7_time_mix(rw[..., :c1], rw[..., c1:c2], rw[..., c2:c3],
                              rw[..., c3:c4], rw[..., c4:c5], rw[..., c5:],
                              w0, w_up, a0, a_up, g_up, k_k, k_a, r_k, ln_w, ln_b)
    m0 = RET_COLS + RWKV_COLS
    mq = proj[..., m0:m0 + MOBA_WIDTH].reshape(B, S, MOBA_HEADS, MOBA_HEAD_DIM)
    mk = proj[..., m0 + MOBA_WIDTH:m0 + 2 * MOBA_WIDTH].reshape(B, S, MOBA_HEADS, MOBA_HEAD_DIM)
    mv = proj[..., m0 + 2 * MOBA_WIDTH:m0 + 3 * MOBA_WIDTH].reshape(B, S, MOBA_HEADS, MOBA_HEAD_DIM)
    moba_out = moba_attention(mq, mk, mv)
    mixed = jnp.concatenate([ret_out.astype(h.dtype), rwkv_out.astype(h.dtype),
                             moba_out.astype(h.dtype)], axis=-1)
    return mixed @ w_out

def conv_glu_ffn(h, w_up, conv_w, conv_b, w_down):
    S = h.shape[1]
    u = h @ w_up
    up = jnp.pad(u, ((0, 0), (CONV_WIDTH - 1, 0), (0, 0)))
    u = sum(conv_w[j] * up[:, j:j + S] for j in range(CONV_WIDTH)) + conv_b
    val, gate = jnp.split(u, 2, axis=-1)
    return (jax.nn.silu(gate) * val) @ w_down

def second_inputs(seed: int = 0) -> dict:
    key = jax.random.key(seed)
    ks = jax.random.split(key, 24)
    D, L = D_MODEL, DEPTH
    f32 = jnp.float32

    def nrm(k, shape, scale):
        return jax.random.normal(k, shape, f32) * scale

    ratio = (jnp.arange(RWKV_WIDTH, dtype=f32) / (RWKV_WIDTH - 1)) ** 0.85
    return {
        "x": nrm(ks[0], (BATCH, SEQ, D), 1.0),
        "c": nrm(ks[1], (BATCH, D), 1.0),
        "w_in": nrm(ks[2], (L, D, IN_COLS), D ** -0.5),
        "w_out": nrm(ks[3], (L, MIX_WIDTH_2, D), MIX_WIDTH_2 ** -0.5),
        "rwkv_mu": jax.random.uniform(ks[4], (L, RWKV_COLS), f32),
        "rwkv_w0": (-6.5 + 5.0 * ratio)[None, :] + nrm(ks[5], (L, RWKV_WIDTH), 0.1),
        "rwkv_w_up": nrm(ks[6], (L, RWKV_DECAY_RANK, RWKV_WIDTH), 0.1 * RWKV_DECAY_RANK ** -0.5),
        "rwkv_a0": nrm(ks[7], (L, RWKV_WIDTH), 0.1),
        "rwkv_a_up": nrm(ks[8], (L, RWKV_A_RANK, RWKV_WIDTH), RWKV_A_RANK ** -0.5),
        "rwkv_g_up": nrm(ks[9], (L, RWKV_GATE_RANK, RWKV_WIDTH), RWKV_GATE_RANK ** -0.5),
        "rwkv_k_k": 0.85 + nrm(ks[10], (L, RWKV_WIDTH), 0.05),
        "rwkv_k_a": 1.0 + nrm(ks[11], (L, RWKV_WIDTH), 0.05),
        "rwkv_r_k": -0.04 + nrm(ks[12], (L, RWKV_HEADS, RWKV_HEAD_DIM), 0.1),
        "rwkv_ln_w": 1.0 + nrm(ks[13], (L, RWKV_WIDTH), 0.05),
        "rwkv_ln_b": nrm(ks[14], (L, RWKV_WIDTH), 0.02),
        "w_ffn_up": nrm(ks[15], (L, D, 2 * D_FF), D ** -0.5),
        "ffn_conv_w": nrm(ks[16], (L, CONV_WIDTH, 2 * D_FF), CONV_WIDTH ** -0.5),
        "ffn_conv_b": nrm(ks[17], (L, 2 * D_FF), 0.02),
        "w_ffn_down": nrm(ks[18], (L, D_FF, D), D_FF ** -0.5),
        "w_ada": nrm(ks[19], (L, D, 6 * D), 0.5 * D ** -0.5),
        "b_ada": nrm(ks[20], (L, 6 * D), 0.02),
        "norm_mix": 1.0 + nrm(ks[21], (L, D), 0.05),
        "norm_ffn": 1.0 + nrm(ks[22], (L, D), 0.05),
        "norm_final": 1.0 + nrm(ks[23], (D,), 0.05),
    }

def second_block(x, c, w_in, w_out, rwkv_mu, rwkv_w0, rwkv_w_up, rwkv_a0, rwkv_a_up, rwkv_g_up,
              rwkv_k_k, rwkv_k_a, rwkv_r_k, rwkv_ln_w, rwkv_ln_b, w_ffn_up, ffn_conv_w,
              ffn_conv_b, w_ffn_down, w_ada, b_ada, norm_mix, norm_ffn, norm_final):
    c_act = jax.nn.silu(c)
    for l in range(DEPTH):
        mod = (c_act @ w_ada[l] + b_ada[l])[:, None, :]
        sh1, sc1, g1, sh2, sc2, g2 = jnp.split(mod, 6, axis=-1)
        h = rms_norm(x, norm_mix[l]) * (1.0 + sc1) + sh1
        x = x + g1 * hybrid_mixer(h, w_in[l], w_out[l], rwkv_mu[l], rwkv_w0[l], rwkv_w_up[l],
                                  rwkv_a0[l], rwkv_a_up[l], rwkv_g_up[l], rwkv_k_k[l],
                                  rwkv_k_a[l], rwkv_r_k[l], rwkv_ln_w[l], rwkv_ln_b[l])
        h = rms_norm(x, norm_ffn[l]) * (1.0 + sc2) + sh2
        x = x + g2 * conv_glu_ffn(h, w_ffn_up[l], ffn_conv_w[l], ffn_conv_b[l], w_ffn_down[l])
    return rms_norm(x, norm_final)


def setup_inputs(seed=0):
    out = dict(first_inputs(seed))
    for name, value in second_inputs(seed + 1).items():
        if name != "x":
            out[name + "_2"] = value
    return out


def reference(
    x, attn_norm_w, w_in, rel_bias_table, gla_gate_w_fwd, gla_gate_b_fwd, gla_gate_w_bwd,
    gla_gate_b_bwd, gla_norm_w, w_out, ffn_norm_w, w_gate, w_up, w_down, final_norm_w, c_2,
    w_in_2, w_out_2, rwkv_mu_2, rwkv_w0_2, rwkv_w_up_2, rwkv_a0_2, rwkv_a_up_2, rwkv_g_up_2,
    rwkv_k_k_2, rwkv_k_a_2, rwkv_r_k_2, rwkv_ln_w_2, rwkv_ln_b_2, w_ffn_up_2, ffn_conv_w_2,
    ffn_conv_b_2, w_ffn_down_2, w_ada_2, b_ada_2, norm_mix_2, norm_ffn_2, norm_final_2,
):
    x = first_block(
        x, attn_norm_w, w_in, rel_bias_table, gla_gate_w_fwd, gla_gate_b_fwd, gla_gate_w_bwd,
        gla_gate_b_bwd, gla_norm_w, w_out, ffn_norm_w, w_gate, w_up, w_down, final_norm_w,
    )
    return second_block(
        x, c_2, w_in_2, w_out_2, rwkv_mu_2, rwkv_w0_2, rwkv_w_up_2, rwkv_a0_2, rwkv_a_up_2,
        rwkv_g_up_2, rwkv_k_k_2, rwkv_k_a_2, rwkv_r_k_2, rwkv_ln_w_2, rwkv_ln_b_2, w_ffn_up_2,
        ffn_conv_w_2, ffn_conv_b_2, w_ffn_down_2, w_ada_2, b_ada_2, norm_mix_2, norm_ffn_2,
        norm_final_2,
    )


_drawn_inputs = setup_inputs


def setup_inputs(seed=0):
    import zlib

    import numpy as np

    out = dict(_drawn_inputs(seed))
    spreads = {}
    factors = {'attn_norm_w': 2.85,
     'gla_gate_b_fwd': 4.306,
     'gla_gate_b_bwd': 4.354,
     'gla_norm_w': 6.629,
     'ffn_norm_w': 3.98,
     'rwkv_w_up_2': 64.0,
     'rwkv_a0_2': 8.0,
     'rwkv_k_k_2': 200.0,
     'rwkv_k_a_2': 8.0,
     'rwkv_ln_w_2': 64.0,
     'rwkv_ln_b_2': 200.0,
     'ffn_conv_b_2': 31.779,
     'norm_mix_2': 4.142,
     'norm_ffn_2': 12.69}
    for name, (base, spread) in spreads.items():
        noise = np.random.default_rng([zlib.crc32(name.encode()), seed]).standard_normal(out[name].shape)
        drawn = base * np.exp(spread * noise) if base else spread * noise
        out[name] = __import__('jax').numpy.asarray(drawn.astype(out[name].dtype))
    for name, factor in factors.items():
        out[name] = (out[name] * factor).astype(out[name].dtype)
    return out
```

```python
from contextlib import ExitStack
import math

import numpy as np

import concourse.bass as bass
from concourse import mybir

ALU = mybir.AluOpType
ACT = mybir.ActivationFunctionType
AX = mybir.AxisListType.X
F32 = mybir.dt.float32
ds = bass.ds

P = 128
S = 256
ST = S // P
D = 2048
KT = D // P
NORM_EPS = 1e-6
AH, AD = 16, 64
AW = AH * AD
BUCKETS, MAXDIST = 32, 1024
PATTERNS = ((128, 1), (512, 4), (2048, 16))
GH, GK, GV = 4, 128, 256
GCH = 64
GRANK = 16
GTAU = 16.0
F1 = 5632
RH, RK, RV = 4, 64, 128
RWH, RWN = 8, 64
RWW = RWH * RWN
DRANK, ARANK, GGRANK = 96, 96, 256
GN_EPS = 64e-5
MH, MD = 8, 128
F2 = 5632
RCOLS = 2 * RH * RK + 2 * RH * RV
WCOLS = 3 * RWW + DRANK + ARANK + GGRANK
CH = 64
NCH = S // CH

SLOTS = 8
UK, UN = 4, 512

COLS = {}
_n = 0
for _name, _w in (("attn_norm_w", 16), ("ffn_norm_w", 16), ("norm_mix_2", 16), ("norm_ffn_2", 16), ("c_2", 16),
                  ("gla_norm_w", 8), ("mu_rkv", 12), ("rwkv_w0_2", 4), ("rwkv_a0_2", 4), ("rwkv_k_k_2", 4),
                  ("rwkv_k_a_2", 4), ("rwkv_r_k_2", 4), ("rwkv_ln_w_2", 4), ("rwkv_ln_b_2", 4),
                  ("gla_gate_b_fwd", 4), ("gla_gate_b_bwd", 4), ("mu_wd", 1), ("mu_wa", 1), ("mu_wg", 2),
                  ("conv_w0", 88), ("conv_w1", 88), ("conv_w2", 88), ("conv_b", 88)):
    COLS[_name] = _n
    _n += _w
NCOLS = _n


def t5_bucket(rel):
    nb = BUCKETS // 2
    n = np.abs(rel)
    exact = nb // 2
    large = exact + (np.log(np.maximum(n, 1) / exact) / math.log(MAXDIST / exact) * (nb - exact)).astype(np.int64)
    return np.where(rel > 0, nb, 0) + np.where(n < exact, n, np.minimum(large, nb - 1))


def constants():
    i = np.arange(P)
    r, c = i[:, None], i[None, :]
    same = (r // CH) == (c // CH)
    parts = [("ident", r == c), ("ones", np.ones((P, P))), ("headsum", same), ("flip", r + c == P - 1),
             ("incl", same & (r <= c)), ("strict", same & (r < c)), ("anti", same & (r >= c))]
    b = 1
    while b < CH:
        lvl = (r // (2 * b) == c // (2 * b)) & (r % (2 * b) < b) & (c % (2 * b) >= b)
        parts.append((f"lvlT{b}", lvl))
        if b == 1:
            parts.append(("lvl1", lvl.T))
        b *= 2
    tok = np.arange(S)
    off = tok[None, :] - tok[:, None]
    count = sum(((off % dil == 0) & (np.abs(off) <= win // 2)).astype(np.float64) for win, dil in PATTERNS)
    parts.append(("carry", np.broadcast_to(np.tile(tok % CH != 0, 4), (P, 4 * S))))
    lnc = np.where(count > 0, np.log(np.maximum(count, 1)), -1e30)
    parts.append(("lncount", lnc.reshape(ST, P, S).transpose(1, 0, 2).reshape(P, -1)))
    g = np.log1p(-np.exp2(-5.0 - np.arange(RH)))
    d = tok[None, :] - i[:, None]
    ret = np.where(d[:, None, :] >= 0, np.exp(g[None, :, None] * np.maximum(d, 0)[:, None, :]), 0.0) * RK ** -0.5
    parts.append(("retdecay", ret.reshape(P, -1)))
    dist = np.where(off <= 0, -off, 1e34)
    parts.append(("distance", dist.reshape(ST, P, S).transpose(1, 0, 2).reshape(P, -1)))
    hot = np.zeros((P, 2 * S))
    m = np.arange(2 * S - 1)
    hot[t5_bucket(m - (S - 1)), m] = 1
    parts.append(("onehot", hot))
    at, n = {}, 0
    for name, a in parts:
        at[name] = (n, n + a.shape[1])
        n += a.shape[1]
    return np.concatenate([np.asarray(a, np.float32) for _, a in parts], axis=1), at


class Kit:

    def __init__(self, nc, ctx, ins, at):
        self.nc, self.ins, self.at = nc, ins, at
        self.ctx = ctx
        self.units = 0
        self.pairs = [0, 0]
        self.loads_done = 0
        self.norms = 0
        self.dve_steps = 0
        self.act_steps = 0
        sb = self.sb
        self.x = sb("x_rows", [P, ST, D])
        self.hT = sb("h_T", [P, KT, S])
        self.ring = sb("ring", [P, SLOTS, UK * UN])
        self.resident = at["carry"][1]
        self.cst = sb("cst", [P, self.resident])
        self.col = sb("col", [P, NCOLS])
        self.stat = sb("stat", [P, 64])
        self.modT = sb("modT", [P, 2 * KT])
        self.modcols = sb("modcols", [P, 6 * D // P])
        self.ps = ctx.enter_context(nc.psum_tensor("ps", [P, 8, 512], F32))
        self.weights_in = [self.sem(f"weights_in{i}") for i in range(SLOTS)]
        self.weights_used = self.sem("weights_used")
        self.pair_free = [self.sem(f"pair_free{i}") for i in range(2)]
        self.dve_order = self.sem("dve_order")
        self.act_order = self.sem("act_order")
        self.loaded = self.sem("loaded")
        self.spreads = 0
        self.spread = [self.sem("gate_row_" + n) for n in ("diag", "spread", "copied")]
        self.n_sumsq = self.sem("norm_sumsq")
        self.n_mean = self.sem("norm_mean")
        self.n_rms = self.sem("norm_rms")
        self.n_rstd = self.sem("norm_rstd")
        self.n_scaled = self.sem("norm_scaled")
        self.n_turned = self.sem("norm_turned")
        self.n_out = [self.sem("norm_out_dve"), self.sem("norm_out_act")]

    def loads(self, n):
        self.loads_done = self.loads_done + 16 * n
        return self.loads_done

    def sb(self, name, shape, ctx=None):
        return (ctx or self.ctx).enter_context(self.nc.sbuf_tensor(name, shape, F32))

    def sem(self, name):
        return self.ctx.enter_context(self.nc.semaphore(name))

    def const_src(self, name):
        a, b = self.at[name]
        return self.ins["consts"][:, a:b]

    def c(self, name):
        a, b = self.at[name]
        return self.cst[:, a:b]

    def cols(self, name, k):
        return self.col[:, COLS[name] + k:COLS[name] + k + 1]

    def dve(self, ins):
        self.dve_steps += 1
        ins.then_inc(self.dve_order, 1)
        self.nc.vector.wait_ge(self.dve_order, self.dve_steps)

    def act(self, ins):
        self.act_steps += 1
        ins.then_inc(self.act_order, 1)
        self.nc.scalar.wait_ge(self.act_order, self.act_steps)


def flat(ap):
    return ap.rearrange("p a b -> p (a b)")


def unit_src(w, k0, col, n=UN):
    return w[k0 * UK * P:(k0 + 1) * UK * P, ds(col, n)].rearrange("(k p) n -> p k n", p=P)


def load_pair(kit, sp, first, i, srcs, wait):
    for j in range(2):
        for u in range(4):
            n = first + 4 * j + u
            slot = n % SLOTS
            if wait:
                sp.wait_ge(kit.weights_used, n - SLOTS + 1 + 8 * i)
            w, col = srcs(i, j)
            sp.dma_start(kit.ring[:, slot, :].rearrange("p (k n) -> p k n", k=UK),
                         unit_src(w, u, col)).then_inc(kit.weights_in[slot], 16)


def load_wide(kit, sp, n, i, w, row):
    slot = n % SLOTS
    sp.wait_ge(kit.weights_used, n - SLOTS + 1 + 8 * i)
    sp.dma_start(kit.ring[:, slot, :], w[ds(row, P), :]).then_inc(kit.weights_in[slot], 16)


def multiply_pair(kit, pe, form, first, i, xT, uses, mid=None):
    nc = kit.nc
    for j in range(2):
        pe.wait_ge(kit.pair_free[j], uses[j] + 1 + i)
        for u in range(4):
            n = first + 4 * j + u
            slot = n % SLOTS
            pe.wait_ge(kit.weights_in[slot], 16 * (n // SLOTS + 1) + 16 * i)
            for kk in range(UK):
                k = UK * u + kk
                for q in range(2 if form == "rows" else 4):
                    if form == "rows":
                        ins = nc.tensor.matmul(kit.ps[:, 2 * j + q, :], lhsT=xT[:, k, q * P:(q + 1) * P],
                                               rhs=kit.ring[:, slot, kk * UN:(kk + 1) * UN],
                                               start=(k == 0), stop=(k == KT - 1))
                    else:
                        ins = nc.tensor.matmul(kit.ps[:, 2 * j + q // 2, (q % 2) * S:(q % 2 + 1) * S],
                                               lhsT=kit.ring[:, slot, kk * UN + q * P:kk * UN + (q + 1) * P],
                                               rhs=xT[:, k, :], start=(k == 0 and q % 2 == 0),
                                               stop=(k == KT - 1), skip_group_check=True)
            ins.then_inc(kit.weights_used, 1)
            if mid and (j, u) == (0, 0):
                mid()


class Part:

    def __init__(self, form, turns, srcs, dst, scale=1.0):
        self.form, self.turns, self.srcs, self.dst, self.scale = form, turns, srcs, dst, scale


def run_turns(eng, start, turns, body):
    if turns - start > 1:
        with eng.Fori(start, turns) as i:
            body(i)
    elif turns - start == 1:
        body(start)


def stage_product(kit, parts, xT, head_next, extra_pe=None, extra_act=None, extra_sync=None, extra_dve=None):
    nc = kit.nc
    first = kit.units
    starts, n = [], first
    for part in parts:
        starts.append(n)
        n += 8 * part.turns
    uses = list(kit.pairs)

    with nc.Block() as block:
        @block.sync
        def _(sp):
            if extra_sync:
                extra_sync(sp)
            for p, part in enumerate(parts):
                run_turns(sp, 1 if p == 0 else 0, part.turns,
                          lambda i: load_pair(kit, sp, starts[p], i, part.srcs, True))
            head_next(sp, n)

        @block.tensor
        def _(pe):
            done = 0
            for p, part in enumerate(parts):
                u = [uses[0] + done, uses[1] + done]
                run_turns(pe, 0, part.turns,
                          lambda i: multiply_pair(kit, pe, part.form, starts[p], i, xT, u))
                done += part.turns
            if extra_pe:
                extra_pe(pe)

        @block.scalar
        def _(act):
            for p, part in enumerate(parts):
                def body(i):
                    for j in range(2):
                        act.wait_ge(kit.weights_used, starts[p] + 4 * (j + 1) + 8 * i)
                        src = kit.ps[:, 2 * j:2 * j + 2, :]
                        dst = part.dst(i, j)
                        if part.form == "T":
                            src = flat(src)
                        nc.scalar.activation(dst, src, ACT.Copy, scale=part.scale).then_inc(kit.pair_free[j], 1)
                run_turns(act, 0, part.turns, body)
            if extra_act:
                extra_act(act)

        if extra_dve:
            @block.vector
            def _(dve):
                extra_dve(dve)

    kit.units = n
    for j in range(2):
        kit.pairs[j] += sum(part.turns for part in parts)


def stage_down(kit, w, w_tiles, actT, out, head_next, gate=None):
    nc = kit.nc
    first = kit.units
    lead = w_tiles % SLOTS
    turns = w_tiles // SLOTS

    with nc.Block() as block:
        @block.sync
        def _(sp):
            for n in range(SLOTS, w_tiles % SLOTS + SLOTS):
                load_wide(kit, sp, first + n, 0, w, P * n)

            def body(i):
                for u in range(SLOTS):
                    load_wide(kit, sp, first + lead + SLOTS + u, i, w, P * (lead + SLOTS + u) + P * SLOTS * i)
            run_turns(sp, 0, turns - 1, body)
            head_next(sp, first + w_tiles)

        @block.tensor
        def _(pe):
            def tile(n, k, i, start, stop):
                slot = n % SLOTS
                pe.wait_ge(kit.weights_in[slot], 16 * (n // SLOTS + 1) + 16 * i)
                for t in range(ST):
                    lhsT = k if not isinstance(k, int) else actT[:, k, t * P:(t + 1) * P]
                    for q in range(4):
                        ins = nc.tensor.matmul(kit.ps[:, 4 * t + q, :], lhsT=lhsT,
                                               rhs=kit.ring[:, slot, q * UN:(q + 1) * UN], start=start, stop=stop,
                                               skip_group_check=True)
                ins.then_inc(kit.weights_used, 1)
            for k in range(w_tiles):
                tile(first + k, k, 0, k == 0, k == w_tiles - 1)

        @block.vector
        def _(dve):
            dve.wait_ge(kit.weights_used, first + w_tiles)
            for t in range(ST):
                sums = flat(kit.ps[:, 4 * t:4 * t + 4, :])
                if gate is not None:
                    kit.dve(nc.vector.tensor_tensor(sums, sums, gate[:, :], ALU.mult))
                kit.dve(nc.vector.tensor_tensor(out[:, t, :], sums, out[:, t, :], ALU.add))
    kit.units = first + w_tiles


def norm_steps(kit, x, tiles, with_T, wcol, bcol, row_w):
    nc = kit.nc
    r = kit.norms
    kit.norms += 1
    turns = kit.turns
    width = KT

    with ExitStack() as st:
        xn = kit.sb(f"xn{r}", [P, ST, D], st) if with_T else None
        with nc.Block() as block:
            @block.scalar
            def _(act):
                for t in range(ST):
                    nc.scalar.activation(flat(kit.ps[:, 0:4, :]), x[:, t, :], ACT.Square,
                                         accum_out=kit.stat[:, t:t + 1]).then_inc(kit.n_sumsq, 1)
                    act.wait_ge(kit.n_sumsq, ST * r + t + 1)
                act.wait_ge(kit.n_mean, r + 1)
                nc.scalar.activation(kit.stat[:, 4:6], kit.stat[:, 2:4], ACT.Sqrt).then_inc(kit.n_rms, 1)
                if with_T:
                    for k in range(1, width, 2):
                        act.wait_ge(kit.n_turned, width * turns + k + 1)
                        nc.scalar.activation(kit.hT[:, k, :], kit.ps[:, 4 + k % 4, 0:S], ACT.Identity,
                                             scale=wcol(k), bias=bcol(k) if bcol else 0.0
                                             ).then_inc(kit.n_out[1], 1)

            @block.vector
            def _(dve):
                dve.wait_ge(kit.n_sumsq, ST * (r + 1))
                nc.vector.tensor_scalar(kit.stat[:, 2:4], kit.stat[:, 0:2], 1.0 / D, NORM_EPS, ALU.mult,
                                        ALU.add).then_inc(kit.n_mean, 1)
                dve.wait_ge(kit.n_rms, r + 1)
                nc.vector.reciprocal(kit.stat[:, 6:8], kit.stat[:, 4:6]).then_inc(kit.n_rstd, 1)
                dve.wait_ge(kit.n_rstd, r + 1)
                for t in range(ST):
                    nc.vector.tensor_scalar(xn[:, t, :] if with_T else x[:, t, :], x[:, t, :],
                                            kit.stat[:, 6 + t:7 + t], None, ALU.mult).then_inc(kit.n_scaled, 1)
                if with_T:
                    for k in range(0, width, 2):
                        dve.wait_ge(kit.n_turned, width * turns + k + 1)
                        if bcol:
                            ins = nc.vector.tensor_scalar(kit.hT[:, k, :], kit.ps[:, 4 + k % 4, 0:S], wcol(k),
                                                          bcol(k), ALU.mult, ALU.add)
                        else:
                            ins = nc.vector.tensor_scalar(kit.hT[:, k, :], kit.ps[:, 4 + k % 4, 0:S], wcol(k),
                                                          None, ALU.mult)
                        ins.then_inc(kit.n_out[0], 1)
                else:
                    dve.wait_ge(kit.n_scaled, ST * (r + 1))
                    for t in range(ST):
                        kit.dve(nc.vector.tensor_tensor(x[:, t, :], x[:, t, :], row_w[:, :], ALU.mult))

            if with_T:
                @block.tensor
                def _(pe):
                    pe.wait_ge(kit.n_scaled, ST * (r + 1))
                    for k in range(width):
                        if k >= 4:
                            pe.wait_ge(kit.n_out[k % 2], width // 2 * turns + (k - 4) // 2 + 1)
                        for t in range(ST):
                            ins = nc.tensor.transpose(kit.ps[:, 4 + k % 4, t * P:(t + 1) * P],
                                                      xn[:, t, k * P:(k + 1) * P], kit.c("ident"))
                        ins.then_inc(kit.n_turned, 1)
    if with_T:
        kit.turns += 1


def stage_setup(kit, mem, head):
    nc, ins = kit.nc, kit.ins
    rows = [("attn_norm_w", 0), ("ffn_norm_w", 0), ("norm_mix_2", 0), ("norm_ffn_2", 0), ("c_2", 0),
            ("gla_norm_w", 0), ("mu_rkv", 0), ("rwkv_w0_2", 0), ("rwkv_a0_2", 0), ("rwkv_k_k_2", 0),
            ("rwkv_k_a_2", 0), ("rwkv_r_k_2", 0), ("rwkv_ln_w_2", 0), ("rwkv_ln_b_2", 0)]
    names = list(COLS)
    width = {n: (COLS[names[i + 1]] if i + 1 < len(names) else NCOLS) - COLS[n] for i, n in enumerate(names)}
    mu = ins["rwkv_mu_2"]
    c3 = 3 * RWW

    def src(name):
        if name == "mu_rkv":
            return mu[0:1, 0:c3].rearrange("a (r f) -> (a r) f", f=P)
        if name == "mu_wg":
            return mu[0:1, c3 + DRANK + ARANK:WCOLS].rearrange("a (r f) -> (a r) f", f=P)
        if name == "rwkv_r_k_2":
            return ins[name].rearrange("a (r h) n -> (a r) (h n)", h=2)
        if name.startswith("conv_w"):
            j = int(name[-1])
            return ins["ffn_conv_w_2"][0, j:j + 1, :].rearrange("a (r f) -> (a r) f", f=P)
        if name == "conv_b":
            return ins["ffn_conv_b_2"].rearrange("a (r f) -> (a r) f", f=P)
        return ins[name].rearrange("a (r f) -> (a r) f", f=P)

    packs = [names[0:14], names[14:19], ["conv_w0"], ["conv_w1"], ["conv_w2"], ["conv_b"]]
    s_zero, s_rows, s_turn, s_col = (kit.sem(n) for n in ("pack_zeroed", "pack_loaded", "pack_turned", "pack_out"))
    s_bias, s_biasrow, s_biasout = (kit.sem(n) for n in ("bias_rows", "bias_rows_copied", "bias_rows_stored"))
    loads = sum(len(p) for p in packs)
    setup_loads = kit.loads(4)

    with ExitStack() as st:
        pack = kit.sb("pack", [P, len(packs), P], st)
        table = kit.sb("table", [BUCKETS, AH], st)
        hot = kit.sb("onehot", [BUCKETS, 2 * S], st)
        brow = kit.sb("brow", [AH, 2 * S], st)
        with nc.Block() as block:
            @block.sync
            def _(sp):
                sp.dma_start(kit.x[:, :, :], ins["x"].rearrange("b (t p) d -> p (b t) d", p=P)
                             ).then_inc(kit.loaded, 16)
                sp.dma_start(kit.cst[:, :], ins["consts"][:, 0:kit.resident]).then_inc(kit.loaded, 16)
                sp.dma_start(table[:, :], ins["rel_bias_table"]).then_inc(kit.loaded, 16)
                sp.dma_start(hot[:, :], kit.const_src("onehot")[0:BUCKETS, :]).then_inc(kit.loaded, 16)
                sp.wait_ge(s_zero, 1)
                for n, names_ in enumerate(packs):
                    at = 0
                    for name in names_:
                        w = width[name]
                        if name in ("mu_wd", "mu_wa"):
                            a = c3 + (DRANK if name == "mu_wa" else 0)
                            sp.dma_start(pack[at:at + 1, n, 0:DRANK], mu[0:1, a:a + DRANK]).then_inc(s_rows, 16)
                        else:
                            sp.dma_start(pack[at:at + w, n, :], src(name)).then_inc(s_rows, 16)
                        at += w
                head(sp)
                sp.wait_ge(s_biasrow, 1)
                sp.dma_start(mem["bias_dram"].ap(), brow[:, :]).then_inc(s_biasout, 16)
                sp.wait_ge(s_biasout, 16)

            @block.vector
            def _(dve):
                nc.vector.memset(pack[:, 1, :], 0.0).then_inc(s_zero, 1)
                for j in range(2):
                    nc.vector.memset(kit.ps[:, 2 * j, 0:8], 0.0).then_inc(kit.pair_free[j], 1)
                at = 0
                for n, names_ in enumerate(packs):
                    w = sum(width[x] for x in names_)
                    dve.wait_ge(s_turn, n + 1)
                    nc.vector.tensor_copy(kit.col[:, at:at + w], kit.ps[:, 4 + n % 2, 0:w]).then_inc(s_col, 1)
                    at += w
                dve.wait_ge(s_bias, 1)
                nc.vector.tensor_copy(brow[:, :], kit.ps[0:AH, 7, :]).then_inc(s_biasrow, 1)

            @block.scalar
            def _(act):
                act.wait_ge(s_col, 1)
                a = COLS["c_2"]
                kit.act(nc.scalar.activation(kit.col[:, a:a + KT], kit.col[:, a:a + KT], ACT.Silu))

            @block.tensor
            def _(pe):
                pe.wait_ge(kit.loaded, setup_loads)
                nc.tensor.matmul(kit.ps[0:AH, 7, :], lhsT=table[:, :], rhs=hot[:, :],
                                 start=True, stop=True).then_inc(s_bias, 1)
                pe.wait_ge(s_rows, 16 * loads)
                for n, names_ in enumerate(packs):
                    w = sum(width[x] for x in names_)
                    if n >= 2:
                        pe.wait_ge(s_col, n - 1)
                    nc.tensor.transpose(kit.ps[:, 4 + n % 2, 0:w], pack[0:w, n, :], kit.c("ident")[0:w, 0:w]
                                        ).then_inc(s_turn, 1)


def stage_attention(kit, qT, kT, v, bias_dram, outT):
    nc = kit.nc
    (s_logits, s_biased, s_max, s_neg, s_exp, s_recip, s_p, s_turned, s_pT, s_out, s_done) = (
        kit.sem("attn_" + n) for n in ("logits", "biased", "max", "negmax", "exp", "recip", "probs",
                                       "turned", "probsT", "out", "stored"))
    tables_ready = kit.loads(AH + 1)
    with ExitStack() as st:
        hank = kit.sb("hankel", [P, AH, 3 * P], st)
        L = kit.sb("logits", [P, 2, ST, S], st)
        E = kit.sb("expd", [P, 2, ST, S], st)
        ET = kit.sb("probsT", [P, 2, ST, S], st)
        lncount = kit.sb("lncount", [P, ST * S], st)
        sc = kit.sb("attn_sc", [P, 2, 4, ST], st)
        mx, neg, tot, rec = (sc[:, :, n, :] for n in range(4))
        ps = kit.ps
        with nc.Block() as block:
            @block.sync
            def _(sp):
                src = bias_dram.ap()
                sp.dma_start(lncount[:, :], kit.const_src("lncount")).then_inc(kit.loaded, 16)
                for h in range(AH):
                    sp.dma_start(hank[:, h, :], bass.AP(tensor=src.tensor, offset=h * 2 * S,
                                                        ap=[[1, P], [1, 3 * P]])).then_inc(kit.loaded, 16)

            @block.tensor
            def _(pe):
                def logits(h):
                    hb, tile, b = AD * (h % 2), h // 2, h % 2
                    if h == 0:
                        pe.wait_ge(kit.loaded, tables_ready)
                    if h >= 2:
                        pe.wait_ge(s_biased, h - 1)
                    for t in range(ST):
                        nc.tensor.matmul(ps[:, b, t * S:(t + 1) * S], lhsT=qT[hb:hb + AD, tile, t * P:(t + 1) * P],
                                         rhs=kT[hb:hb + AD, tile, :], start=True, stop=False)
                        ins = nc.tensor.matmul(ps[:, b, t * S:(t + 1) * S], lhsT=kit.c("flip"),
                                               rhs=hank[:, h, P - t * P:P - t * P + S], start=False, stop=True)
                    ins.then_inc(s_logits, 1)

                logits(0)
                for h in range(AH):
                    if h + 1 < AH:
                        logits(h + 1)
                    b = h % 2
                    pe.wait_ge(s_p, ST * (h + 1))
                    if h >= 2:
                        pe.wait_ge(s_pT, h - 1)
                    for jt in range(ST):
                        for t in range(ST):
                            ins = nc.tensor.transpose(ps[:, 2 + b, jt * S + t * P:jt * S + (t + 1) * P],
                                                      E[:, b, t, jt * P:(jt + 1) * P], kit.c("ident"))
                    ins.then_inc(s_turned, 1)
                    pe.wait_ge(s_pT, h + 1)
                    if h % 2 == 0 and h >= 4:
                        pe.wait_ge(s_done, h // 2 - 1)
                    hb = AD * (h % 2)
                    for jt in range(ST):
                        ins = nc.tensor.matmul(ps[hb:hb + AD, 4 + (h // 2) % 2, 0:S],
                                               lhsT=v[:, jt, h * AD:(h + 1) * AD], rhs=ET[:, b, jt, :],
                                               start=(jt == 0), stop=(jt == ST - 1))
                    ins.then_inc(s_out, 1)

            @block.vector
            def _(dve):
                dve.wait_ge(kit.loaded, tables_ready)
                for h in range(AH + 2):
                    if h < AH:
                        b = h % 2
                        dve.wait_ge(s_logits, h + 1)
                        if h >= 2:
                            dve.wait_ge(s_exp, ST * (h - 1))
                        nc.vector.tensor_tensor(flat(L[:, b, :, :]), ps[:, b, :], lncount[:, :],
                                                ALU.add).then_inc(s_biased, 1)
                        dve.wait_ge(s_biased, h + 1)
                        nc.vector.tensor_reduce(mx[:, b, :], L[:, b, :, :], AX, ALU.max).then_inc(s_max, 1)
                        dve.wait_ge(s_max, h + 1)
                        nc.vector.tensor_scalar(neg[:, b, :], mx[:, b, :], -1.0, None, ALU.mult).then_inc(s_neg, 1)
                    if 1 <= h <= AH:
                        g = h - 1
                        b = g % 2
                        dve.wait_ge(s_exp, ST * (g + 1))
                        nc.vector.reciprocal(rec[:, b, :], tot[:, b, :]).then_inc(s_recip, 1)
                        dve.wait_ge(s_recip, g + 1)
                        for t in range(ST):
                            nc.vector.tensor_scalar(E[:, b, t, :], E[:, b, t, :], rec[:, b, t:t + 1], None,
                                                    ALU.mult).then_inc(s_p, 1)
                    if h >= 3 and h % 2 == 1:
                        pair = (h - 3) // 2
                        dve.wait_ge(s_out, 2 * pair + 2)
                        nc.vector.tensor_copy(outT[:, pair, :], ps[:, 4 + pair % 2, 0:S]).then_inc(s_done, 1)

            @block.scalar
            def _(act):
                for h in range(AH + 1):
                    if h < AH:
                        b = h % 2
                        act.wait_ge(s_neg, h + 1)
                        if h >= 2:
                            act.wait_ge(s_turned, h - 1)
                        for t in range(ST):
                            nc.scalar.activation(E[:, b, t, :], L[:, b, t, :], ACT.Exp, bias=neg[:, b, t:t + 1],
                                                 accum_out=tot[:, b, t:t + 1]).then_inc(s_exp, 1)
                    if h >= 1:
                        g = h - 1
                        act.wait_ge(s_turned, g + 1)
                        if g >= 2:
                            act.wait_ge(s_out, g - 1)
                        nc.scalar.activation(flat(ET[:, g % 2, :, :]), ps[:, 2 + g % 2, :], ACT.Copy
                                             ).then_inc(s_pT, 1)


def stage_gla(kit, gqk, gv, gr, glr, outT, ctx_name="gla"):
    nc, ps, ins = kit.nc, kit.ps, kit.ins
    W = GH * S
    G16 = 1.0 / GTAU
    sem = lambda n: kit.sem("gla_" + n)
    w_ready = kit.loads(2)
    with ExitStack() as st:
        gw = kit.sb("gate_w", [GRANK, 2, GH * GK], st)
        A = kit.sb("gla_a", [P, 2, W], st)
        B = kit.sb("gla_b", [P, 2, W], st)
        G = kit.sb("gla_g", [P, 2, W], st)
        E = kit.sb("gla_e", [P, 2, W], st)
        q_in = kit.sb("gla_qin", [P, 2, W], st)
        k_in = kit.sb("gla_kin", [P, 2, W], st)
        k_end = B
        last = kit.sb("gla_last", [P, 2, GH * NCH], st)
        dec = kit.sb("gla_dec", [P, 2, GH * NCH], st)
        AT = kit.sb("gla_AT", [P, 2, ST, P], st)
        tmp = kit.sb("gla_tmp", [P, 2, S], st)

        s_z, s_s, s_ln, s_G, s_D, s_eq, s_ek, s_ee = (
            sem(n) for n in ("gate", "biased", "softplus", "sums", "to_end", "exp_q", "exp_k", "exp_end"))
        with nc.Block() as block:
            @block.sync
            def _(sp):
                sp.dma_start(gw[:, 0, :], ins["gla_gate_w_fwd"][0]).then_inc(kit.loaded, 16)
                sp.dma_start(gw[:, 1, :], ins["gla_gate_w_bwd"][0]).then_inc(kit.loaded, 16)

            @block.tensor
            def _(pe):
                pe.wait_ge(kit.loaded, w_ready)
                for d in range(2):
                    for m in range(GH):
                        i_ = nc.tensor.matmul(ps[:, 2 * d + m // 2, (m % 2) * S:(m % 2 + 1) * S],
                                              lhsT=gw[:, d, m * P:(m + 1) * P], rhs=glr[:, d, :], start=True,
                                              stop=True)
                    i_.then_inc(s_z, 1)

            @block.vector
            def _(dve):
                for d, name in enumerate(("gla_gate_b_fwd", "gla_gate_b_bwd")):
                    dve.wait_ge(s_z, d + 1)
                    for m in range(GH):
                        nc.vector.tensor_scalar(A[:, d, m * S:(m + 1) * S],
                                                ps[:, 2 * d + m // 2, (m % 2) * S:(m % 2 + 1) * S],
                                                kit.cols(name, m), None, ALU.add).then_inc(s_s, 1)
                dve.wait_ge(s_s, 2 * GH)
                dve.wait_ge(s_ln, 1)
                kit.dve(nc.vector.scalar_tensor_tensor(flat(A[:, :, :]), flat(A[:, :, :]), 0.0, flat(B[:, :, :]),
                                                       ALU.min, ALU.subtract))
                for d in range(2):
                    kit.dve(nc.vector.tensor_tensor_scan(G[:, d, :], kit.c("carry"), A[:, d, :], 0.0, ALU.mult,
                                                         ALU.add))
                chunks = lambda t: t.rearrange("p (g c) -> p g c", c=GCH)
                for d in range(2):
                    kit.dve(nc.vector.tensor_copy(last[:, d, :], chunks(G[:, d, :])[:, :, GCH - 1]))
                kit.dve(nc.vector.tensor_tensor(B[:, 1, :], A[:, 1, :], G[:, 1, :], ALU.subtract))
                lastb = lambda d: last[:, d, :].unsqueeze(2).broadcast_to([P, GH * NCH, GCH])
                nc.vector.tensor_tensor(chunks(G[:, 1, :]), chunks(B[:, 1, :]), lastb(1), ALU.add).then_inc(s_G, 1)
                dve.wait_ge(s_G, 1)
                for d in range(2):
                    nc.vector.tensor_tensor(chunks(B[:, d, :]), lastb(d), chunks(G[:, d, :]),
                                            ALU.subtract).then_inc(s_D, 1)
                qk = flat(gqk[:, :, :])
                dve.wait_ge(s_eq, 1)
                for d in range(2):
                    kit.dve(nc.vector.scalar_tensor_tensor(q_in[:, d, :], qk[:, 0:W], GK ** -0.5, E[:, d, :],
                                                           ALU.mult, ALU.mult))
                dve.wait_ge(s_ek, 1)
                for d in range(2):
                    kit.dve(nc.vector.tensor_tensor(k_in[:, d, :], qk[:, W:2 * W], A[:, d, :], ALU.mult))
                dve.wait_ge(s_ee, 1)
                for d in range(2):
                    kit.dve(nc.vector.tensor_tensor(k_end[:, d, :], qk[:, W:2 * W], B[:, d, :], ALU.mult))

            @block.scalar
            def _(act):
                act.wait_ge(s_s, 2 * GH)
                kit.act(nc.scalar.activation(flat(B[:, :, :]), flat(A[:, :, :]), ACT.Abs))
                kit.act(nc.scalar.activation(flat(E[:, :, :]), flat(B[:, :, :]), ACT.Exp, scale=-1.0))
                nc.scalar.activation(flat(B[:, :, :]), flat(E[:, :, :]), ACT.Ln, bias=1.0).then_inc(s_ln, 1)
                act.wait_ge(s_G, 1)
                nc.scalar.activation(flat(E[:, :, :]), flat(G[:, :, :]), ACT.Exp, scale=G16).then_inc(s_eq, 1)
                nc.scalar.activation(flat(A[:, :, :]), flat(G[:, :, :]), ACT.Exp, scale=-G16).then_inc(s_ek, 1)
                act.wait_ge(s_D, 2)
                nc.scalar.activation(flat(B[:, :, :]), flat(B[:, :, :]), ACT.Exp, scale=G16).then_inc(s_ee, 1)
                kit.act(nc.scalar.activation(flat(dec[:, :, :]), flat(last[:, :, :]), ACT.Exp, scale=G16))

        krow = A[:, :, :].rearrange("p d (t f) -> p d t f", t=ST)
        states = flat(G[:, :, :])[:, 0:6 * GV].rearrange("p (d c v) -> p d c v", d=2, c=3)
        orow = flat(E[:, :, :]).rearrange("p (t f) -> p t f", t=ST)

        def update(d, n):
            bank, half = {(0, 0): (2, 0), (0, 2): (2, 1), (1, 1): (3, 0),
                          (0, 1): (4, 0), (1, 0): (4, 1), (1, 2): (7, 0)}[d, n]
            return ps[:, bank, half * GV:(half + 1) * GV]

        s_kt, s_kr, s_A, s_AT, s_U, s_st, s_O, s_oo = (
            sem(n) for n in ("kend_turned", "kend_rows", "products", "masked", "updates", "states", "out", "out_rows"))
        with nc.Block() as block:
            @block.tensor
            def _(pe):
                for g in range(4):
                    d, t = g // 2, g % 2
                    for h in range(GH):
                        i_ = nc.tensor.transpose(ps[:, g, h * P:(h + 1) * P],
                                                 k_end[:, d, h * S + t * P:h * S + (t + 1) * P], kit.c("ident"))
                    i_.then_inc(s_kt, 1)
                pe.wait_ge(s_kr, 4)

                def products(h):
                    if h >= 2:
                        pe.wait_ge(s_AT, h - 1)
                    for d in range(2):
                        for t in range(ST):
                            a = h * S + t * P
                            i_ = nc.tensor.matmul(ps[:, h % 2, d * S + t * P:d * S + (t + 1) * P],
                                                  lhsT=k_in[:, d, a:a + P], rhs=q_in[:, d, a:a + P], start=True,
                                                  stop=True)
                    i_.then_inc(s_A, 1)

                def updates(h):
                    if h >= 1:
                        pe.wait_ge(s_st, h)
                    for d in range(2):
                        for n in range(3):
                            c = n if d == 0 else NCH - 1 - n
                            t, pb = c // 2, CH * (c % 2)
                            i_ = nc.tensor.matmul(update(d, n),
                                                  lhsT=krow[pb:pb + CH, d, t, h * GK:(h + 1) * GK],
                                                  rhs=gv[pb:pb + CH, t, h * GV:(h + 1) * GV], start=True, stop=True)
                    i_.then_inc(s_U, 1)

                products(0)
                updates(0)
                for h in range(GH):
                    if h + 1 < GH:
                        products(h + 1)
                    pe.wait_ge(s_AT, h + 1)
                    pe.wait_ge(s_st, h + 1)
                    if h >= 2:
                        pe.wait_ge(s_oo, h - 1)
                    for t in range(ST):
                        o = ps[:, 5 + h % 2, t * GV:(t + 1) * GV]
                        i_ = nc.tensor.matmul(o, lhsT=AT[:, h % 2, t, :], rhs=gv[:, t, h * GV:(h + 1) * GV],
                                              start=True, stop=False, skip_group_check=True)
                        for c in range(2 * t, 2 * t + 2):
                            pb = CH * (c % 2)
                            for d, n in ((0, c - 1), (1, NCH - 2 - c)):
                                if n >= 0:
                                    i_ = nc.tensor.matmul(o[pb:pb + CH, :],
                                                          lhsT=q_in[:, d, h * S + c * CH:h * S + (c + 1) * CH],
                                                          rhs=states[:, d, n, :], start=False, stop=False,
                                                          skip_group_check=True)
                    i_.then_inc(s_O, 1)
                    if h + 1 < GH:
                        updates(h + 1)

            @block.vector
            def _(dve):
                for h in range(GH):
                    dve.wait_ge(s_A, h + 1)
                    if h >= 2:
                        dve.wait_ge(s_O, h - 1)
                    for d, mask in enumerate(("incl", "anti")):
                        kit.dve(nc.vector.tensor_tensor(
                            tmp[:, d, :].rearrange("p (t c) -> p t c", t=ST),
                            ps[:, h % 2, d * S:(d + 1) * S].rearrange("p (t c) -> p t c", t=ST),
                            kit.c(mask).unsqueeze(1).broadcast_to([P, ST, P]), ALU.mult))
                    nc.vector.tensor_tensor(flat(AT[:, h % 2, :, :]), tmp[:, 0, :], tmp[:, 1, :],
                                            ALU.add).then_inc(s_AT, 1)
                    dve.wait_ge(s_U, h + 1)
                    if h >= 1:
                        dve.wait_ge(s_O, h)
                    for n in range(3):
                        for d in range(2):
                            c = n if d == 0 else NCH - 1 - n
                            u = update(d, n)
                            if n == 0:
                                kit.dve(nc.vector.tensor_copy(states[:, d, 0, :], u))
                            else:
                                step = nc.vector.scalar_tensor_tensor(states[:, d, n, :], states[:, d, n - 1, :],
                                                                      dec[:, d, h * NCH + c:h * NCH + c + 1], u,
                                                                      ALU.mult, ALU.add)
                                if (n, d) == (2, 1):
                                    step.then_inc(s_st, 1)
                                else:
                                    kit.dve(step)

            @block.scalar
            def _(act):
                for g in range(4):
                    act.wait_ge(s_kt, g + 1)
                    nc.scalar.activation(krow[:, g // 2, g % 2, :], ps[:, g, :], ACT.Copy).then_inc(s_kr, 1)
                for h in range(GH):
                    act.wait_ge(s_O, h + 1)
                    nc.scalar.activation(orow[:, :, h * GV:(h + 1) * GV],
                                         ps[:, 5 + h % 2, :].rearrange("p (t v) -> p t v", t=ST), ACT.Copy
                                         ).then_inc(s_oo, 1)
        gated_norm(kit, "gla", orow, gr, GH, GV, outT, lambda k: kit.cols("gla_norm_w", k))


def gated_norm(kit, name, orow, gate, heads, width, outT, wcol):
    nc, ps = kit.nc, kit.ps
    tiles = heads * width // P
    n = heads * ST
    s_sq, s_mean, s_rms, s_silu, s_rows, s_turn, s_od, s_oa = (
        kit.sem(f"{name}_{x}") for x in ("sumsq", "mean", "rms", "silu", "normed", "turned", "out_dve", "out_act"))
    stat = kit.stat
    with nc.Block() as block:
        @block.scalar
        def _(act):
            for t in range(ST):
                for h in range(heads):
                    j = t * heads + h
                    kit.act(nc.scalar.activation(ps[:, 0, 0:width], orow[:, t, h * width:(h + 1) * width], ACT.Square,
                                                 accum_out=stat[:, 8 + j:9 + j]))
            nc.scalar.activation(stat[:, 32:33], stat[:, 8:9], ACT.Copy).then_inc(s_sq, 1)
            act.wait_ge(s_mean, 1)
            nc.scalar.activation(stat[:, 24:24 + n], stat[:, 16:16 + n], ACT.Sqrt).then_inc(s_rms, 1)
            nc.scalar.activation(gate[:, :, :], gate[:, :, :], ACT.Silu).then_inc(s_silu, 1)
            for k in range(1, tiles, 2):
                act.wait_ge(s_turn, k + 1)
                nc.scalar.activation(outT[:, k, :], ps[:, 4 + k % 4, 0:S], ACT.Identity,
                                     scale=wcol(k) if wcol else 1.0).then_inc(s_oa, 1)

        @block.vector
        def _(dve):
            dve.wait_ge(s_sq, 1)
            nc.vector.tensor_scalar(stat[:, 16:16 + n], stat[:, 8:8 + n], 1.0 / width, NORM_EPS, ALU.mult,
                                    ALU.add).then_inc(s_mean, 1)
            dve.wait_ge(s_rms, 1)
            kit.dve(nc.vector.reciprocal(stat[:, 8:8 + n], stat[:, 24:24 + n]))
            dve.wait_ge(s_silu, 1)
            for t in range(ST):
                for h in range(heads):
                    a, b = h * width, (h + 1) * width
                    j = 8 + t * heads + h
                    nc.vector.scalar_tensor_tensor(orow[:, t, a:b], orow[:, t, a:b], stat[:, j:j + 1],
                                                   gate[:, t, a:b], ALU.mult, ALU.mult).then_inc(s_rows, 1)
            for k in range(0, tiles, 2):
                dve.wait_ge(s_turn, k + 1)
                if wcol:
                    i_ = nc.vector.tensor_scalar(outT[:, k, :], ps[:, 4 + k % 4, 0:S], wcol(k), None, ALU.mult)
                else:
                    i_ = nc.vector.tensor_copy(outT[:, k, :], ps[:, 4 + k % 4, 0:S])
                i_.then_inc(s_od, 1)

        @block.tensor
        def _(pe):
            pe.wait_ge(s_rows, n)
            for k in range(tiles):
                if k >= 4:
                    pe.wait_ge(s_oa if k % 2 else s_od, (k - 4) // 2 + 1)
                for t in range(ST):
                    i_ = nc.tensor.transpose(ps[:, 4 + k % 4, t * P:(t + 1) * P], orow[:, t, k * P:(k + 1) * P],
                                             kit.c("ident"))
                i_.then_inc(s_turn, 1)


class Ada:

    def __init__(self, kit, ctx):
        self.kit = kit
        self.w = kit.sb("ada_w", [P, 2, 2, 2 * UN], ctx)
        self.acc = kit.sb("ada_acc", [P, 2 * UN], ctx)
        self.b = kit.sb("ada_b", [1, 2 * UN], ctx)
        self.out = kit.modcols
        self.s_w = [kit.sem("ada_w0"), kit.sem("ada_w1")]
        self.s_b = kit.sem("ada_b_loaded")
        self.s_acc = kit.sem("ada_acc")
        self.s_sum = kit.sem("ada_sum")
        self.s_out = kit.sem("ada_out")

    def load(self, sp, lead, i, m, col):
        kit = self.kit
        a = 8 * lead + m
        if a >= 2:
            sp.wait_ge(self.s_acc, 2 * (a - 1) + 16 * i)
        w = kit.ins["w_ada_2"][0]
        sp.dma_start(self.w[:, m % 2, :, :], w[2 * m * P:2 * (m + 1) * P, ds(col, 2 * UN)]
                     .rearrange("(k p) n -> p k n", p=P)).then_inc(self.s_w[m % 2], 16)

    def load_bias(self, sp, lead, i, col):
        if lead:
            sp.wait_ge(self.s_sum, lead + i)
        sp.dma_start(self.b[:, :], self.kit.ins["b_ada_2"][:, ds(col, 2 * UN)]).then_inc(self.s_b, 16)

    def products(self, dve, lead, i):
        nc, kit = self.kit.nc, self.kit
        if lead:
            dve.wait_ge(self.s_sum, lead + i)
        for m in range(8):
            dve.wait_ge(self.s_w[m % 2], 64 * lead + 64 * i + 16 * (m // 2 + 1))
            for k in range(2):
                w, c = self.w[:, m % 2, k, :], kit.cols("c_2", 2 * m + k)
                n = 16 * lead + 2 * m + k
                if m or k:
                    dve.wait_ge(self.s_acc, n + 16 * i)
                    step = nc.vector.scalar_tensor_tensor(self.acc[:, :], w, c, self.acc[:, :], ALU.mult, ALU.add)
                else:
                    step = nc.vector.tensor_scalar(self.acc[:, :], w, c, None, ALU.mult)
                step.then_inc(self.s_acc, 1)

    def sums(self, pe, lead, i):
        nc, kit = self.kit.nc, self.kit
        pe.wait_ge(self.s_acc, 16 * lead + 16 * i)
        pe.wait_ge(self.s_b, 16 * lead + 16 * i)
        if lead > 1:
            pe.wait_ge(self.s_out, lead - 1 + i)
        ones = kit.c("ones")
        for q in range(8):
            nc.tensor.matmul(kit.ps[:, 6, q:q + 1], lhsT=self.acc[:, q * P:(q + 1) * P], rhs=ones[:, 0:1],
                             start=True, stop=False)
            step = nc.tensor.matmul(kit.ps[:, 6, q:q + 1], lhsT=self.b[:, q * P:(q + 1) * P], rhs=ones[0:1, 0:1],
                                    start=False, stop=True)
        step.then_inc(self.s_sum, 1)

    def copy(self, dve, lead, i):
        dve.wait_ge(self.s_sum, lead + i)
        self.kit.nc.vector.tensor_copy(self.out[:, ds(8 * (lead - 1) + 8 * i, 8)],
                                       self.kit.ps[:, 6, 0:8]).then_inc(self.s_out, 1)


def stage_glu(kit, ada, act_out, tmp, w_gate, w_up, head_next):
    nc = kit.nc
    first = kit.units
    uses = list(kit.pairs)
    turns = F1 // UN
    s_silu, s_glu = kit.sem("glu_silu"), kit.sem("glu_out")
    srcs = lambda i, j: ((w_gate, w_up)[j], UN * i)
    outf = flat(act_out)
    with nc.Block() as block:
        @block.sync
        def _(sp):
            def body(i):
                for m in range(8):
                    ada.load(sp, 1, i, m, 2 * UN * i)
                    if m == 2:
                        ada.load_bias(sp, 1, i, 2 * UN * i)
                    j, u = m // 4, m % 4
                    n = first + 8 + m
                    sp.wait_ge(kit.weights_used, n - SLOTS + 1 + 8 * i)
                    w = (w_gate, w_up)[j]
                    sp.dma_start(kit.ring[:, n % SLOTS, :].rearrange("p (k n) -> p k n", k=UK),
                                 unit_src(w, u, UN * i + UN)).then_inc(kit.weights_in[n % SLOTS], 16)
            run_turns(sp, 0, turns - 1, body)
            for m in range(8):
                ada.load(sp, turns, 0, m, 2 * UN * (turns - 1))
                if m == 2:
                    ada.load_bias(sp, turns, 0, 2 * UN * (turns - 1))
            head_next(sp, first + 8 * turns)

        @block.tensor
        def _(pe):
            run_turns(pe, 0, turns, lambda i: multiply_pair(kit, pe, "T", first, i, kit.hT, uses,
                                                            mid=lambda: ada.sums(pe, 1, i)))
            ada.sums(pe, turns + 1, 0)

        @block.scalar
        def _(act):
            def body(i):
                act.wait_ge(kit.weights_used, first + 4 + 8 * i)
                act.wait_ge(s_glu, 1 + i)
                nc.scalar.activation(tmp, flat(kit.ps[:, 0:2, :]), ACT.Silu).then_inc(kit.pair_free[0], 1)
            run_turns(act, 0, turns, body)

        @block.vector
        def _(dve):
            nc.vector.memset(kit.stat[:, 63:64], 0.0).then_inc(s_glu, 1)

            def body(i):
                ada.copy(dve, 1, i)
                ada.products(dve, 1, i)
                dve.wait_ge(kit.pair_free[0], uses[0] + 2 + i)
                dve.wait_ge(kit.weights_used, first + 8 + 8 * i)
                dve.wait_ge(kit.pair_free[1], uses[1] + 1 + i)
                nc.vector.tensor_tensor(outf[:, ds(4 * S * i, 4 * S)], tmp, flat(kit.ps[:, 2:4, :]),
                                        ALU.mult).then_inc(s_glu, 1)
                dve.wait_ge(s_glu, 2 + i)
                nc.vector.memset(kit.stat[:, 62:63], 0.0).then_inc(kit.pair_free[1], 1)
            run_turns(dve, 0, turns, body)
            ada.copy(dve, turns + 1, 0)
    kit.units = first + 8 * turns
    kit.pairs = [u + turns for u in uses]


def stage_project(kit, w, ada, with_ada, mixed, next_head):
    w_src = lambda i, j: (w, UN * j + 2 * UN * i)
    nc = kit.nc
    first = kit.units
    uses = list(kit.pairs)
    group = 11
    with nc.Block() as block:
        @block.sync
        def _(sp):
            for m in range(8):
                if with_ada:
                    ada.load(sp, 0, 0, m, 2 * UN * group)
                    if m == 0:
                        ada.load_bias(sp, 0, 0, 2 * UN * group)
                j, u = m // 4, m % 4
                n = first + 8 + m
                sp.wait_ge(kit.weights_used, n - SLOTS + 1)
                sp.dma_start(kit.ring[:, n % SLOTS, :].rearrange("p (k n) -> p k n", k=UK),
                             unit_src(w, u, UN * j + 2 * UN)).then_inc(kit.weights_in[n % SLOTS], 16)
            next_head(sp, first + 16)

        @block.tensor
        def _(pe):
            for i in range(2):
                multiply_pair(kit, pe, "rows", first, i, kit.hT, uses)

        @block.scalar
        def _(act):
            for i in range(2):
                for j in range(2):
                    act.wait_ge(kit.weights_used, first + 4 * (j + 1) + 8 * i)
                    a = UN * (2 * i + j)
                    nc.scalar.activation(mixed[:, :, a:a + UN], kit.ps[:, 2 * j:2 * j + 2, :], ACT.Copy
                                         ).then_inc(kit.pair_free[j], 1)

        if with_ada:
            @block.vector
            def _(dve):
                ada.products(dve, 0, 0)
    kit.units = first + 16
    kit.pairs = [u + 2 for u in uses]


def stage_add(kit, mixed, gate_row):
    nc = kit.nc
    with nc.Block() as block:
        @block.vector
        def _(dve):
            for t in range(ST):
                if gate_row is not None:
                    kit.dve(nc.vector.tensor_tensor(mixed[:, t, :], mixed[:, t, :], gate_row, ALU.mult))
                kit.dve(nc.vector.tensor_tensor(kit.x[:, t, :], kit.x[:, t, :], mixed[:, t, :], ALU.add))

def stage_modulation(kit, modcols):
    nc = kit.nc
    with nc.Block() as block:
        @block.vector
        def _(dve):
            for n, (scale, w) in enumerate(((24, "norm_mix_2"), (72, "norm_ffn_2"))):
                a = COLS[w]
                kit.dve(nc.vector.scalar_tensor_tensor(kit.modT[:, KT * n:KT * (n + 1)], modcols[:, scale:scale + KT],
                                                       1.0, kit.col[:, a:a + KT], ALU.add, ALU.mult))


def stage_gate_row(kit, name, modcols, at, row):
    nc = kit.nc
    s_diag, s_row, s_out = kit.spread
    n0 = KT * kit.spreads
    kit.spreads += 1
    with ExitStack() as st:
        diag = kit.sb(f"{name}_diag", [P, KT, P], st)
        with nc.Block() as block:
            @block.vector
            def _(dve):
                for k in range(KT):
                    nc.vector.tensor_scalar(diag[:, k, :], kit.c("ident"), modcols[:, at(k):at(k) + 1], None,
                                            ALU.mult).then_inc(s_diag, 1)

            @block.tensor
            def _(pe):
                for k in range(KT):
                    pe.wait_ge(s_diag, n0 + k + 1)
                    nc.tensor.matmul(kit.ps[:, 4 + k // 4, (k % 4) * P:(k % 4 + 1) * P], lhsT=kit.c("ones"),
                                     rhs=diag[:, k, :], start=True, stop=True).then_inc(s_row, 1)

            @block.scalar
            def _(act):
                for q in range(4):
                    act.wait_ge(s_row, n0 + 4 * (q + 1))
                    nc.scalar.activation(row[:, q * UN:(q + 1) * UN], kit.ps[:, 4 + q, :], ACT.Copy
                                         ).then_inc(s_out, 1)


def stage_retention(kit, rqk, rvg, outT):
    nc, ps = kit.nc, kit.ps
    table_ready = kit.loads(1)
    s_S, s_PT, s_O, s_oo = (kit.sem("ret_" + n) for n in ("products", "decayed", "out", "rows"))
    with ExitStack() as st:
        decay = kit.sb("ret_decay", [P, RH, S], st)
        PT = kit.sb("ret_PT", [P, 2, 3 * P], st)
        orow = kit.sb("ret_rows", [P, ST, RH * RV], st)
        with nc.Block() as block:
            @block.sync
            def _(sp):
                sp.dma_start(flat(decay[:, :, :]), kit.const_src("retdecay")).then_inc(kit.loaded, 16)

            @block.tensor
            def _(pe):
                def products(h):
                    hb, tile, b = RK * (h % 2), h // 2, h % 2
                    if h >= 2:
                        pe.wait_ge(s_PT, h - 1)
                    for jt in range(ST):
                        a = jt * P
                        ins = nc.tensor.matmul(ps[:, b, jt * S:jt * S + S - a],
                                               lhsT=rqk[hb:hb + RK, 2 + tile, a:a + P],
                                               rhs=rqk[hb:hb + RK, tile, a:S], start=True, stop=True)
                    ins.then_inc(s_S, 1)

                products(0)
                for h in range(RH):
                    if h + 1 < RH:
                        products(h + 1)
                    pe.wait_ge(s_PT, h + 1)
                    if h >= 2:
                        pe.wait_ge(s_oo, h - 1)
                    v = lambda jt: rvg[:, jt, h * RV:(h + 1) * RV]
                    b = h % 2
                    nc.tensor.matmul(ps[:, 2 + b, 0:RV], lhsT=PT[:, b, 0:P], rhs=v(0), start=True, stop=True)
                    nc.tensor.matmul(ps[:, 2 + b, RV:2 * RV], lhsT=PT[:, b, P:2 * P], rhs=v(0), start=True,
                                     stop=False)
                    nc.tensor.matmul(ps[:, 2 + b, RV:2 * RV], lhsT=PT[:, b, 2 * P:3 * P], rhs=v(1), start=False,
                                     stop=True).then_inc(s_O, 1)

            @block.vector
            def _(dve):
                dve.wait_ge(kit.loaded, table_ready)
                for h in range(RH):
                    dve.wait_ge(s_S, h + 1)
                    if h >= 2:
                        dve.wait_ge(s_O, h - 1)
                    kit.dve(nc.vector.tensor_tensor(PT[:, h % 2, 0:S], ps[:, h % 2, 0:S], decay[:, h, :], ALU.mult))
                    nc.vector.tensor_tensor(PT[:, h % 2, S:S + P], ps[:, h % 2, S:S + P], decay[:, h, 0:P],
                                            ALU.mult).then_inc(s_PT, 1)

            @block.scalar
            def _(act):
                for h in range(RH):
                    act.wait_ge(s_O, h + 1)
                    nc.scalar.activation(orow[:, :, h * RV:(h + 1) * RV],
                                         ps[:, 2 + h % 2, 0:2 * RV].rearrange("p (t v) -> p t v", t=ST), ACT.Copy
                                         ).then_inc(s_oo, 1)
        gated_norm(kit, "ret", orow, rvg[:, :, RH * RV:], RH, RV, outT, None)


def stage_moba(kit, mqk, mv, outT):
    nc, ps = kit.nc, kit.ps
    (s_logits, s_biased, s_max, s_neg, s_exp, s_recip, s_p, s_turned, s_pT, s_out, s_done) = (
        kit.sem("moba_" + n) for n in ("logits", "biased", "max", "negmax", "exp", "recip", "probs",
                                       "turned", "probsT", "out", "stored"))
    table_ready = kit.loads(1)
    span = ((0, P), (P, P + S))
    with ExitStack() as st:
        dist = kit.sb("distance", [P, ST, S], st)
        L = kit.sb("moba_logits", [P, 2, 3 * P], st)
        E = kit.sb("moba_exp", [P, 2, 3 * P], st)
        ET = kit.sb("moba_probsT", [P, 2, 3 * P], st)
        sc = kit.sb("moba_sc", [P, 2, 4, ST], st)
        mx, neg, tot, rec = (sc[:, :, n, :] for n in range(4))
        with nc.Block() as block:
            @block.sync
            def _(sp):
                sp.dma_start(flat(dist[:, :, :]), kit.const_src("distance")).then_inc(kit.loaded, 16)

            @block.tensor
            def _(pe):
                def logits(h):
                    if h >= 2:
                        pe.wait_ge(s_biased, ST * (h - 1))
                    for t in range(ST):
                        a, b = span[t]
                        ins = nc.tensor.matmul(ps[:, h % 2, a:b], lhsT=mqk[:, h, t * P:(t + 1) * P],
                                               rhs=mqk[:, MH + h, 0:b - a], start=True, stop=True)
                    ins.then_inc(s_logits, 1)

                logits(0)
                for h in range(MH):
                    if h + 1 < MH:
                        logits(h + 1)
                    b = h % 2
                    pe.wait_ge(s_p, ST * (h + 1))
                    if h >= 2:
                        pe.wait_ge(s_pT, h - 1)
                    for n in range(3):
                        ins = nc.tensor.transpose(ps[:, 2 + b, n * P:(n + 1) * P], E[:, b, n * P:(n + 1) * P],
                                                  kit.c("ident"))
                    ins.then_inc(s_turned, 1)
                    pe.wait_ge(s_pT, h + 1)
                    if h >= 2:
                        pe.wait_ge(s_done, h - 1)
                    nc.tensor.matmul(ps[:, 4 + b, 0:S], lhsT=mv[:, 0, h * MD:(h + 1) * MD], rhs=ET[:, b, 0:S],
                                     start=True, stop=False)
                    nc.tensor.matmul(ps[:, 4 + b, P:S], lhsT=mv[:, 1, h * MD:(h + 1) * MD], rhs=ET[:, b, S:S + P],
                                     start=False, stop=True).then_inc(s_out, 1)

            @block.vector
            def _(dve):
                dve.wait_ge(kit.loaded, table_ready)
                for h in range(MH + 2):
                    if h < MH:
                        b = h % 2
                        slope = 2.0 ** (-8.0 * (h + 1) / MH)
                        dve.wait_ge(s_logits, h + 1)
                        if h >= 2:
                            dve.wait_ge(s_exp, ST * (h - 1))
                        for t in range(ST):
                            x, y = span[t]
                            nc.vector.scalar_tensor_tensor(L[:, b, x:y], dist[:, t, 0:y - x], -slope, ps[:, b, x:y],
                                                           ALU.mult, ALU.add).then_inc(s_biased, 1)
                        dve.wait_ge(s_biased, ST * (h + 1))
                        for t in range(ST):
                            x, y = span[t]
                            nc.vector.tensor_reduce(mx[:, b, t:t + 1], L[:, b, x:y], AX, ALU.max).then_inc(s_max, 1)
                        dve.wait_ge(s_max, ST * (h + 1))
                        nc.vector.tensor_scalar(neg[:, b, :], mx[:, b, :], -1.0, None, ALU.mult).then_inc(s_neg, 1)
                    if 1 <= h <= MH:
                        g = h - 1
                        b = g % 2
                        dve.wait_ge(s_exp, ST * (g + 1))
                        nc.vector.reciprocal(rec[:, b, :], tot[:, b, :]).then_inc(s_recip, 1)
                        dve.wait_ge(s_recip, g + 1)
                        for t in range(ST):
                            x, y = span[t]
                            nc.vector.tensor_scalar(E[:, b, x:y], E[:, b, x:y], rec[:, b, t:t + 1], None,
                                                    ALU.mult).then_inc(s_p, 1)
                    if h >= 2:
                        g = h - 2
                        dve.wait_ge(s_out, g + 1)
                        nc.vector.tensor_copy(outT[:, g, :], ps[:, 4 + g % 2, 0:S]).then_inc(s_done, 1)

            @block.scalar
            def _(act):
                for h in range(MH + 1):
                    if h < MH:
                        b = h % 2
                        act.wait_ge(s_neg, h + 1)
                        if h >= 2:
                            act.wait_ge(s_turned, h - 1)
                        for t in range(ST):
                            x, y = span[t]
                            nc.scalar.activation(E[:, b, x:y], L[:, b, x:y], ACT.Exp, bias=neg[:, b, t:t + 1],
                                                 accum_out=tot[:, b, t:t + 1]).then_inc(s_exp, 1)
                    if h >= 1:
                        g = h - 1
                        act.wait_ge(s_turned, g + 1)
                        if g >= 2:
                            act.wait_ge(s_out, g - 1)
                        nc.scalar.activation(ET[:, g % 2, :], ps[:, 2 + g % 2, 0:3 * P], ACT.Copy).then_inc(s_pT, 1)


def stage_rwkv(kit, rw, low, outT):
    nc, ps, ins = kit.nc, kit.ps, kit.ins
    NT = RWW // P
    W = NT * S
    sem = lambda n: kit.sem("rw_" + n)
    c3 = 3 * NT
    with ExitStack() as st:
        sb = lambda n, shape: kit.sb("rw_" + n, shape, st)
        kap, bet, kt, rt = (sb(n, [P, NT, S]) for n in ("kap", "bet", "kt", "rt"))
        bonus, gate = sb("bonus", [P, NT, S]), sb("gate", [P, NT, S])
        endG = sb("end_decay", [P, NT, NCH])
        gp = sb("gp", [P, NT, S])

        inner = ExitStack()
        new = kit.sb("rw_new", [P, c3, S], inner)
        lnew = kit.sb("rw_lnew", [P, 4, S], inner)
        wup = kit.sb("rw_wup", [DRANK, RWW], inner)
        aup = kit.sb("rw_aup", [ARANK, RWW], inner)
        gup = kit.sb("rw_gup", [P, 2, RWW], inner)
        t1, t2 = kit.sb("rw_t1", [P, NT, S], inner), kit.sb("rw_t2", [P, NT, S], inner)
        up_ready = kit.loads(3)
        s_shift, s_code, s_z, s_sw, s_sa = (
            sem(n) for n in ("shifted", "codes", "low_products", "decay_gate", "a_gate"))

        def bank_tile(m, base):
            return ps[:, base + m // 2, (m % 2) * S:(m % 2 + 1) * S]

        with nc.Block() as block:
            @block.sync
            def _(sp):
                sp.dma_start(wup[:, :], ins["rwkv_w_up_2"][0]).then_inc(kit.loaded, 16)
                sp.dma_start(aup[:, :], ins["rwkv_a_up_2"][0]).then_inc(kit.loaded, 16)
                sp.dma_start(gup[:, :, :], ins["rwkv_g_up_2"][0].rearrange("(k p) n -> p k n", p=P)
                             ).then_inc(kit.loaded, 16)

            @block.vector
            def _(dve):
                lows = ((DRANK, 0, 1), (ARANK, 1, 2), (P, 2, 4))
                for m, a, b in lows:
                    nc.vector.tensor_tensor(lnew[0:m, a:b, 1:S], low[0:m, a:b, 0:S - 1], low[0:m, a:b, 1:S],
                                            ALU.subtract)
                    kit.dve(nc.vector.tensor_scalar(lnew[0:m, a:b, 0:1], low[0:m, a:b, 0:1], -1.0, None, ALU.mult))
                for q, (m, name, k) in enumerate(((DRANK, "mu_wd", 0), (ARANK, "mu_wa", 0), (P, "mu_wg", 0),
                                                  (P, "mu_wg", 1))):
                    nc.vector.scalar_tensor_tensor(lnew[0:m, q, :], lnew[0:m, q, :], kit.cols(name, k)[0:m, :],
                                                   low[0:m, q, :], ALU.mult, ALU.add).then_inc(s_shift, 1)
                nc.vector.tensor_tensor(new[:, :, 1:S], rw[:, :, 0:S - 1], rw[:, :, 1:S], ALU.subtract)
                kit.dve(nc.vector.tensor_scalar(new[:, :, 0:1], rw[:, :, 0:1], -1.0, None, ALU.mult))
                for q in range(c3):
                    kit.dve(nc.vector.scalar_tensor_tensor(new[:, q, :], new[:, q, :], kit.cols("mu_rkv", q),
                                                           rw[:, q, :], ALU.mult, ALU.add))

            @block.scalar
            def _(act):
                act.wait_ge(s_shift, 4)
                nc.scalar.activation(lnew[0:DRANK, 0, :], lnew[0:DRANK, 0, :], ACT.Tanh).then_inc(s_code, 1)
                nc.scalar.activation(lnew[:, 2:4, :], lnew[:, 2:4, :], ACT.Sigmoid).then_inc(s_code, 1)
                act.wait_ge(s_z, 1)
                for m in range(NT):
                    nc.scalar.activation(t1[:, m, :], bank_tile(m, 0), ACT.Sigmoid, bias=kit.cols("rwkv_w0_2", m)
                                         ).then_inc(s_sw, 1)
                act.wait_ge(s_z, 2)
                for m in range(NT):
                    nc.scalar.activation(t2[:, m, :], bank_tile(m, 2), ACT.Sigmoid, bias=kit.cols("rwkv_a0_2", m)
                                         ).then_inc(s_sa, 1)
                act.wait_ge(s_z, 3)
                kit.act(nc.scalar.activation(flat(gate[:, :, :]), flat(ps[:, 4:6, :]), ACT.Copy))

            @block.tensor
            def _(pe):
                pe.wait_ge(kit.loaded, up_ready)
                pe.wait_ge(s_code, 2)
                for base, w, r, q in ((0, wup, DRANK, 0), (2, aup, ARANK, 1)):
                    for m in range(NT):
                        i_ = nc.tensor.matmul(bank_tile(m, base), lhsT=w[:, m * P:(m + 1) * P], rhs=lnew[0:r, q, :],
                                              start=True, stop=True)
                    i_.then_inc(s_z, 1)
                for m in range(NT):
                    for k in range(2):
                        i_ = nc.tensor.matmul(bank_tile(m, 4), lhsT=gup[:, k, m * P:(m + 1) * P],
                                              rhs=lnew[:, 2 + k, :], start=(k == 0), stop=(k == 1))
                i_.then_inc(s_z, 1)

        r, k, v = (new[:, n * NT:(n + 1) * NT, :] for n in range(3))
        G = bonus
        s_G, s_Gm, s_eG, s_enG, s_eGm, s_sq, s_ss, s_max, s_nrm, s_rkk, s_sum = (
            sem(n) for n in ("G", "G_before", "exp_G", "exp_minus_G", "exp_G_before", "kk_sq", "kk_sumsq", "kk_max",
                             "kk_norm", "rk_products", "rk_sums"))
        two = lambda ap: ap.rearrange("p (b a) s -> p b (a s)", b=2)
        with nc.Block() as block:
            @block.vector
            def _(dve):
                kit.dve(nc.vector.tensor_scalar(flat(t1[:, :, :]), flat(t1[:, :, :]), -math.exp(-0.5), None, ALU.mult))
                nc.vector.tensor_tensor_scan(flat(G[:, :, :]), kit.c("carry"), flat(t1[:, :, :]), 0.0, ALU.mult, ALU.add
                                             ).then_inc(s_G, 1)
                dve.wait_ge(s_G, 1)
                dve.wait_ge(s_enG, 1)
                nc.vector.tensor_tensor(flat(t1[:, :, :]), flat(G[:, :, :]), flat(t1[:, :, :]), ALU.subtract).then_inc(s_Gm, 1)
                for m in range(NT):
                    kit.dve(nc.vector.tensor_scalar(kap[:, m, :], k[:, m, :], kit.cols("rwkv_k_k_2", m), None,
                                                    ALU.mult))
                nc.vector.tensor_tensor(flat(bet[:, :, :]), flat(kap[:, :, :]), flat(kap[:, :, :]), ALU.mult).then_inc(s_sq, 1)
                dve.wait_ge(s_ss, 1)
                nc.vector.tensor_scalar(two(bet[:, :, :]), ps[:, 0:2, :], 1e-24, None, ALU.max).then_inc(s_max, 1)
                for m in range(NT):
                    kit.dve(nc.vector.tensor_scalar(gp[:, m, :], t2[:, m, :], -1.0, kit.cols("rwkv_k_a_2", m),
                                                    ALU.add, ALU.mult))
                kit.dve(nc.vector.scalar_tensor_tensor(flat(k), flat(gp[:, :, :]), 1.0, flat(k), ALU.add, ALU.mult))
                dve.wait_ge(s_nrm, 1)
                kit.dve(nc.vector.reciprocal(flat(bet[:, :, :]), flat(bet[:, :, :])))
                kit.dve(nc.vector.tensor_tensor(flat(kap[:, :, :]), flat(kap[:, :, :]), flat(bet[:, :, :]), ALU.mult))
                kit.dve(nc.vector.tensor_tensor(flat(gp[:, :, :]), flat(r), flat(k), ALU.mult))
                for m in range(NT):
                    nc.vector.tensor_scalar(gp[:, m, :], gp[:, m, :], kit.cols("rwkv_r_k_2", m), None,
                                            ALU.mult).then_inc(s_rkk, 1)
                dve.wait_ge(s_enG, 1)
                kit.dve(nc.vector.tensor_tensor(flat(bet[:, :, :]), flat(kap[:, :, :]), flat(t2[:, :, :]), ALU.mult))
                kit.dve(nc.vector.tensor_tensor(flat(bet[:, :, :]), flat(bet[:, :, :]), flat(kt[:, :, :]), ALU.mult))
                kit.dve(nc.vector.tensor_tensor(flat(kt[:, :, :]), flat(k), flat(kt[:, :, :]), ALU.mult))
                dve.wait_ge(s_eG, 1)
                kit.dve(nc.vector.tensor_copy(endG[:, :, :], rt[:, :, :].rearrange("p m (c s) -> p m c s", s=CH)
                                              [:, :, :, CH - 1]))
                kit.dve(nc.vector.tensor_tensor(flat(rt[:, :, :]), flat(r), flat(rt[:, :, :]), ALU.mult))
                dve.wait_ge(s_eGm, 1)
                kit.dve(nc.vector.tensor_tensor(flat(kap[:, :, :]), flat(kap[:, :, :]), flat(t1[:, :, :]), ALU.mult))
                dve.wait_ge(s_sum, 1)
                kit.dve(nc.vector.tensor_tensor(two(bonus[:, :, :]), ps[:, 2:4, :], two(v), ALU.mult))

            @block.scalar
            def _(act):
                act.wait_ge(s_G, 1)
                nc.scalar.activation(flat(rt[:, :, :]), flat(G[:, :, :]), ACT.Exp).then_inc(s_eG, 1)
                nc.scalar.activation(flat(kt[:, :, :]), flat(G[:, :, :]), ACT.Exp, scale=-1.0).then_inc(s_enG, 1)
                act.wait_ge(s_Gm, 1)
                nc.scalar.activation(flat(t1[:, :, :]), flat(t1[:, :, :]), ACT.Exp).then_inc(s_eGm, 1)
                act.wait_ge(s_max, 1)
                nc.scalar.activation(flat(bet[:, :, :]), flat(bet[:, :, :]), ACT.Sqrt).then_inc(s_nrm, 1)

            @block.tensor
            def _(pe):
                for need, count, src, base, done in ((s_sq, 1, bet, 0, s_ss), (s_rkk, NT, gp, 2, s_sum)):
                    pe.wait_ge(need, count)
                    for b in range(2):
                        i_ = nc.tensor.matmul(ps[:, base + b, :], lhsT=kit.c("headsum"),
                                              rhs=two(src[:, :, :])[:, b, :], start=True, stop=True)
                    i_.then_inc(done, 1)

        srcs = (kap, bet, kt, v)
        kap_r, bet_r, kt_r, v_r = (rw[:, n * NT:(n + 1) * NT, :] if n < 3 else gp for n in range(4))
        kap_r, bet_r, kt_r, v_r = (x.rearrange("p m s -> p (m s)").rearrange("p (t f) -> p t f", t=ST)
                                   for x in (kap_r, bet_r, kt_r, v_r[:, :, :]))
        dsts = (kap_r, bet_r, kt_r, v_r)
        s_tr, s_rows = sem("turned"), sem("rows")
        with nc.Block() as block:
            @block.tensor
            def _(pe):
                for n in range(8):
                    src, t = srcs[n // 2], n % 2
                    for m in range(NT):
                        i_ = nc.tensor.transpose(ps[:, n, m * P:(m + 1) * P], src[:, m, t * P:(t + 1) * P],
                                                 kit.c("ident"))
                    i_.then_inc(s_tr, 1)

            @block.scalar
            def _(act):
                for n in range(8):
                    act.wait_ge(s_tr, n + 1)
                    nc.scalar.activation(dsts[n // 2][:, n % 2, :], ps[:, n, :], ACT.Copy).then_inc(s_rows, 1)
        inner.close()

        RB, RKm = sb("RB_T", [P, ST, 2, 4 * P]), sb("RK_T", [P, ST, 2, 4 * P])
        KxT = sb("Kx_T", [P, NT, S])
        Z = sb("Z", [P, ST, RWW])
        solve = ExitStack()
        AT, X, XT, BT, P1, Off = (kit.sb("rw_" + n, [P, 2, 4 * P], solve) for n in ("A_T", "X", "X_T", "B_T", "P1",
                                                                                    "off"))
        bv = Off[:, 0, :]
        blocks = [2 ** n for n in range(1, int(math.log2(CH)))]
        s_pr, s_ev, s_off, s_p1, s_p1c, s_m, s_x, s_bv, s_bvc, s_zk, s_zkc = (
            sem(n) for n in ("products", "masked", "between", "offX", "offX_copied", "XoffX", "X_updated", "BV",
                             "BV_copied", "Z_Kx", "Z_Kx_copied"))
        heads4 = lambda ap: ap.rearrange("p (h c) -> p h c", h=4)
        mask4 = lambda name: kit.c(name).unsqueeze(1).broadcast_to([P, 4, P])
        for t in range(ST):
            a = t * P
            NL = len(blocks)
            with nc.Block() as block:
                @block.tensor
                def _(pe):
                    n = 0
                    for lhs, rhs in ((bet, kap), (kap, bet), (kt, kap), (bet, rt), (kt, rt)):
                        for par in range(2):
                            hb = RWN * par
                            if n >= 8:
                                pe.wait_ge(s_ev, 10 * t + n - 7)
                            for m in range(NT):
                                i_ = nc.tensor.matmul(ps[:, n % 8, m * P:(m + 1) * P],
                                                      lhsT=lhs[hb:hb + RWN, m, a:a + P],
                                                      rhs=rhs[hb:hb + RWN, m, a:a + P], start=True, stop=True)
                            i_.then_inc(s_pr, 1)
                            n += 1
                    pe.wait_ge(s_ev, 10 * (t + 1))
                    for l in range(NL):
                        for g in range(2):
                            lv = 2 * (t * NL + l) + g
                            pe.wait_ge(s_off, lv + 1)
                            pe.wait_ge(s_x, lv - 1) if lv >= 2 else None
                            for m in range(4):
                                q = slice(m * P, (m + 1) * P)
                                i_ = nc.tensor.matmul(ps[:, g, q], lhsT=Off[:, g, q], rhs=X[:, g, q], start=True,
                                                      stop=True)
                            i_.then_inc(s_p1, 1)
                        for g in range(2):
                            lv = 2 * (t * NL + l) + g
                            pe.wait_ge(s_p1c, lv + 1)
                            for m in range(4):
                                q = slice(m * P, (m + 1) * P)
                                nc.tensor.matmul(ps[:, 2 + 2 * g, q], lhsT=XT[:, g, q], rhs=P1[:, g, q], start=True,
                                                 stop=True)
                            for m in range(4):
                                q = slice(m * P, (m + 1) * P)
                                i_ = nc.tensor.matmul(ps[:, 3 + 2 * g, q], lhsT=P1[:, g, q], rhs=XT[:, g, q],
                                                      start=True, stop=True)
                            i_.then_inc(s_m, 1)
                    pe.wait_ge(s_x, 2 * NL * (t + 1))
                    for h in range(RWH):
                        q = slice((h // 2) * P, (h // 2 + 1) * P)
                        f = slice(h * RWN, (h + 1) * RWN)
                        i_ = nc.tensor.matmul(ps[:, 6, f], lhsT=BT[:, h % 2, q], rhs=v_r[:, t, f], start=True,
                                              stop=True)
                    i_.then_inc(s_bv, 1)
                    for h in range(RWH):
                        q = slice((h // 2) * P, (h // 2 + 1) * P)
                        f = slice(h * RWN, (h + 1) * RWN)
                        hb = RWN * (h % 2)
                        i_ = nc.tensor.matmul(ps[hb:hb + RWN, 7, q], lhsT=kap_r[:, t, f], rhs=XT[:, h % 2, q],
                                              start=True, stop=True)
                    i_.then_inc(s_zk, 1)
                    pe.wait_ge(s_bvc, t + 1)
                    for h in range(RWH):
                        q = slice((h // 2) * P, (h // 2 + 1) * P)
                        f = slice(h * RWN, (h + 1) * RWN)
                        i_ = nc.tensor.matmul(ps[:, 0, f], lhsT=XT[:, h % 2, q], rhs=bv[:, f], start=True, stop=True)
                    i_.then_inc(s_zk, 1)

                @block.vector
                def _(dve):
                    n = 0
                    for kind in range(5):
                        for par in range(2):
                            dve.wait_ge(s_pr, 10 * t + n + 1)
                            src = ps[:, n % 8, :]
                            if kind == 0:
                                kit.dve(nc.vector.tensor_copy(AT[:, par, :], src))
                                kit.dve(nc.vector.tensor_tensor(heads4(XT[:, par, :]), heads4(AT[:, par, :]),
                                                                mask4("lvlT1"), ALU.mult))
                                i_ = nc.vector.tensor_tensor(heads4(XT[:, par, :]), mask4("ident"),
                                                             heads4(XT[:, par, :]), ALU.subtract)
                            elif kind == 1:
                                kit.dve(nc.vector.tensor_tensor(heads4(X[:, par, :]), heads4(src), mask4("lvl1"),
                                                                ALU.mult))
                                i_ = nc.vector.tensor_tensor(heads4(X[:, par, :]), mask4("ident"),
                                                             heads4(X[:, par, :]), ALU.subtract)
                            else:
                                dst, mask = {2: (BT[:, par, :], "strict"), 3: (RB[:, t, par, :], "incl"),
                                             4: (RKm[:, t, par, :], "incl")}[kind]
                                i_ = nc.vector.tensor_tensor(heads4(dst), heads4(src), mask4(mask), ALU.mult)
                            i_.then_inc(s_ev, 1)
                            n += 1
                    dve.wait_ge(s_ev, 10 * (t + 1))
                    for l, b in enumerate(blocks):
                        for g in range(2):
                            lv = 2 * (t * NL + l) + g
                            if lv >= 2:
                                dve.wait_ge(s_p1, lv - 1)
                            nc.vector.tensor_tensor(heads4(Off[:, g, :]), heads4(AT[:, g, :]), mask4(f"lvlT{b}"),
                                                    ALU.mult).then_inc(s_off, 1)
                        for g in range(2):
                            lv = 2 * (t * NL + l) + g
                            dve.wait_ge(s_m, lv + 1)
                            if l < NL - 1:
                                nc.vector.tensor_tensor(X[:, g, :], X[:, g, :], ps[:, 2 + 2 * g, :], ALU.subtract)
                            nc.vector.tensor_tensor(XT[:, g, :], XT[:, g, :], ps[:, 3 + 2 * g, :],
                                                    ALU.subtract).then_inc(s_x, 1)

                @block.scalar
                def _(act):
                    for l in range(NL):
                        for g in range(2):
                            lv = 2 * (t * NL + l) + g
                            act.wait_ge(s_p1, lv + 1)
                            nc.scalar.activation(P1[:, g, :], ps[:, g, :], ACT.Copy).then_inc(s_p1c, 1)
                    act.wait_ge(s_bv, t + 1)
                    nc.scalar.activation(bv, ps[:, 6, :], ACT.Copy).then_inc(s_bvc, 1)
                    act.wait_ge(s_zk, 2 * t + 1)
                    nc.scalar.activation(KxT[:, :, a:a + P], heads4(ps[:, 7, :]), ACT.Copy).then_inc(s_zkc, 1)
                    act.wait_ge(s_zk, 2 * t + 2)
                    nc.scalar.activation(Z[:, t, :], ps[:, 0, :], ACT.Copy).then_inc(s_zkc, 1)
        solve.close()

        U, M, YT = sb("U", [P, ST, RWW]), sb("M", [P, NT, RWN]), sb("Y_T", [P, NT, S])
        s_pu, s_u, s_y2, s_y1, s_pm, s_M, s_y2c, s_y = (
            sem(n) for n in ("U_products", "U", "Y_chunk", "Y_state", "M_products", "M", "Y_copied", "Y"))
        pairs = lambda ap: ap.rearrange("p (m two n) -> p m two n", two=2, n=RWN)
        with nc.Block() as block:
            @block.tensor
            def _(pe):
                for c in range(NCH):
                    t, pb, b = c // 2, CH * (c % 2), c % 2
                    rows_ = slice(pb, pb + CH)
                    cs = slice(c * CH, (c + 1) * CH)
                    if c:
                        pe.wait_ge(s_M, c)
                        for h in range(RWH):
                            hb, m = RWN * (h % 2), h // 2
                            i_ = nc.tensor.matmul(ps[rows_, h % 2, m * RWN:(m + 1) * RWN],
                                                  lhsT=KxT[hb:hb + RWN, m, cs], rhs=M[hb:hb + RWN, m, :],
                                                  start=True, stop=True)
                        i_.then_inc(s_pu, 1)
                        if c >= 3:
                            pe.wait_ge(s_y, c - 2)
                        for h in range(RWH):
                            hb, m = RWN * (h % 2), h // 2
                            i_ = nc.tensor.matmul(ps[hb:hb + RWN, 4 + b, m * CH:(m + 1) * CH],
                                                  lhsT=M[hb:hb + RWN, m, :], rhs=rt[hb:hb + RWN, m, cs],
                                                  start=True, stop=True)
                        i_.then_inc(s_y1, 1)
                    pe.wait_ge(s_u, c + 1)
                    for h in range(RWH):
                        hb, m = RWN * (h % 2), h // 2
                        f = slice(h * RWN, (h + 1) * RWN)
                        o = ps[hb:hb + RWN, 6 + b, m * RWN:(m + 1) * RWN]
                        nc.tensor.matmul(o, lhsT=bet_r[rows_, t, f], rhs=U[rows_, t, f], start=True, stop=False)
                        i_ = nc.tensor.matmul(o, lhsT=kt_r[rows_, t, f], rhs=v_r[rows_, t, f], start=False,
                                              stop=True)
                    i_.then_inc(s_pm, 1)
                    if c >= 2:
                        pe.wait_ge(s_y2c, c - 1)
                    for h in range(RWH):
                        hb, m = RWN * (h % 2), h // 2
                        f = slice(h * RWN, (h + 1) * RWN)
                        q = slice(m * P + pb, m * P + pb + CH)
                        o = ps[hb:hb + RWN, 2 + b, m * CH:(m + 1) * CH]
                        nc.tensor.matmul(o, lhsT=U[rows_, t, f], rhs=RB[rows_, t, h % 2, q], start=True, stop=False)
                        i_ = nc.tensor.matmul(o, lhsT=v_r[rows_, t, f], rhs=RKm[rows_, t, h % 2, q], start=False,
                                              stop=True)
                    i_.then_inc(s_y2, 1)

            @block.vector
            def _(dve):
                for c in range(NCH):
                    t, pb, b = c // 2, CH * (c % 2), c % 2
                    rows_ = slice(pb, pb + CH)
                    if c == 0:
                        nc.vector.tensor_scalar(U[rows_, t, :], Z[rows_, t, :], -1.0, None, ALU.mult
                                                ).then_inc(s_u, 1)
                    else:
                        dve.wait_ge(s_pu, c)
                        kit.dve(nc.vector.scalar_tensor_tensor(
                            pairs(U[rows_, t, :])[:, :, 0, :], ps[rows_, 0, 0:NT * RWN].rearrange(
                                "p (m n) -> p m n", m=NT), -1.0, pairs(Z[rows_, t, :])[:, :, 0, :], ALU.mult,
                            ALU.subtract))
                        nc.vector.scalar_tensor_tensor(
                            pairs(U[rows_, t, :])[:, :, 1, :], ps[rows_, 1, 0:NT * RWN].rearrange(
                                "p (m n) -> p m n", m=NT), -1.0, pairs(Z[rows_, t, :])[:, :, 1, :], ALU.mult,
                            ALU.subtract).then_inc(s_u, 1)
                    dve.wait_ge(s_pm, c + 1)
                    pm = ps[:, 6 + b, 0:NT * RWN]
                    if c < NCH - 1:
                        if c == 0:
                            kit.dve(nc.vector.tensor_copy(flat(M[:, :, :]), pm))
                        else:
                            dve.wait_ge(s_y1, c)
                            kit.dve(nc.vector.tensor_tensor(flat(M[:, :, :]), flat(M[:, :, :]), pm, ALU.add))
                        nc.vector.tensor_tensor(M[:, :, :], M[:, :, :],
                                                endG[:, :, c:c + 1].broadcast_to([P, NT, RWN]), ALU.mult
                                                ).then_inc(s_M, 1)
                    if c:
                        dve.wait_ge(s_y1, c)
                        dve.wait_ge(s_y2c, c + 1)
                        y = YT[:, :, c * CH:(c + 1) * CH]
                        nc.vector.tensor_tensor(y, ps[:, 4 + b, 0:NT * CH].rearrange("p (m s) -> p m s", m=NT), y,
                                                ALU.add).then_inc(s_y, 1)

            @block.scalar
            def _(act):
                for c in range(NCH):
                    act.wait_ge(s_y2, c + 1)
                    nc.scalar.activation(YT[:, :, c * CH:(c + 1) * CH],
                                         ps[:, 2 + c % 2, 0:NT * CH].rearrange("p (m s) -> p m s", m=NT), ACT.Copy
                                         ).then_inc(s_y2c, 1)

        sq = sb("y_sq", [P, NT, S])
        s_mean, s_c, s_var, s_ve, s_sd = (sem(n) for n in ("y_mean", "y_squares", "y_var", "y_var_eps", "y_sd"))
        with nc.Block() as block:
            @block.tensor
            def _(pe):
                for b in range(2):
                    i_ = nc.tensor.matmul(ps[:, b, :], lhsT=kit.c("headsum"), rhs=two(YT[:, :, :])[:, b, :],
                                          start=True, stop=True)
                i_.then_inc(s_mean, 1)
                pe.wait_ge(s_c, 1)
                for b in range(2):
                    i_ = nc.tensor.matmul(ps[:, 2 + b, :], lhsT=kit.c("headsum"), rhs=two(sq[:, :, :])[:, b, :],
                                          start=True, stop=True)
                i_.then_inc(s_var, 1)

            @block.vector
            def _(dve):
                dve.wait_ge(s_mean, 1)
                kit.dve(nc.vector.scalar_tensor_tensor(two(YT[:, :, :]), ps[:, 0:2, :], -1.0 / RWN, two(YT[:, :, :]),
                                                       ALU.mult, ALU.add))
                nc.vector.tensor_tensor(flat(sq[:, :, :]), flat(YT[:, :, :]), flat(YT[:, :, :]), ALU.mult).then_inc(s_c, 1)
                dve.wait_ge(s_var, 1)
                nc.vector.tensor_scalar(two(sq[:, :, :]), ps[:, 2:4, :], 1.0 / RWN, GN_EPS, ALU.mult,
                                        ALU.add).then_inc(s_ve, 1)
                dve.wait_ge(s_sd, 1)
                kit.dve(nc.vector.reciprocal(flat(sq[:, :, :]), flat(sq[:, :, :])))
                kit.dve(nc.vector.tensor_tensor(flat(YT[:, :, :]), flat(YT[:, :, :]), flat(sq[:, :, :]), ALU.mult))
                for m in range(NT):
                    kit.dve(nc.vector.tensor_scalar(YT[:, m, :], YT[:, m, :], kit.cols("rwkv_ln_w_2", m),
                                                    kit.cols("rwkv_ln_b_2", m), ALU.mult, ALU.add))
                kit.dve(nc.vector.tensor_tensor(flat(YT[:, :, :]), flat(YT[:, :, :]), flat(bonus[:, :, :]), ALU.add))
                kit.dve(nc.vector.tensor_tensor(flat(outT), flat(YT[:, :, :]), flat(gate[:, :, :]), ALU.mult))

            @block.scalar
            def _(act):
                act.wait_ge(s_ve, 1)
                nc.scalar.activation(flat(sq[:, :, :]), flat(sq[:, :, :]), ACT.Sqrt).then_inc(s_sd, 1)


def stage_conv_glu(kit, w, act_out, head_next):
    nc, ps = kit.nc, kit.ps
    first = kit.units
    uses = list(kit.pairs)
    turns = F2 // UN
    FT = F2 // P
    s_taps, s_base, s_conv, s_silu, s_glu = (kit.sem("conv_" + n) for n in ("taps", "base", "sums", "silu", "glu"))
    srcs = lambda i, j: (w, F2 * j + UN * i)
    c0 = COLS["conv_w0"]
    taps_all = kit.col[:, c0:c0 + 4 * 2 * FT].rearrange("p (j f) -> p j f", j=4)
    outf = flat(act_out)
    per = 2 * 4 * 2
    with ExitStack() as st:
        y = kit.sb("conv_y", [P, 2, 4, S], st)
        taps = kit.sb("conv_taps", [P, 2, 4, 4], st)

        with nc.Block() as block:
            @block.sync
            def _(sp):
                run_turns(sp, 1, turns, lambda i: load_pair(kit, sp, first, i, srcs, True))
                head_next(sp, first + 8 * turns)

            @block.tensor
            def _(pe):
                run_turns(pe, 0, turns, lambda i: multiply_pair(kit, pe, "T", first, i, kit.hT, uses))

            @block.scalar
            def _(act):
                def body(i):
                    for j in range(2):
                        act.wait_ge(s_taps, 2 + 2 * i)
                        act.wait_ge(kit.weights_used, first + 4 * (j + 1) + 8 * i)
                        act.wait_ge(s_glu, 1 + i)
                        for q in range(4):
                            nc.scalar.activation(y[:, j, q, :], ps[:, 2 * j + q // 2, (q % 2) * S:(q % 2 + 1) * S],
                                                 ACT.Identity, scale=taps[:, j, 2, q:q + 1],
                                                 bias=taps[:, j, 3, q:q + 1]).then_inc(s_base, 1)
                    act.wait_ge(kit.pair_free[1], uses[1] + 2 + i)
                    nc.scalar.activation(flat(y[:, 1, :, :]), flat(y[:, 1, :, :]), ACT.Silu).then_inc(s_silu, 1)
                run_turns(act, 0, turns, body)

            @block.vector
            def _(dve):
                nc.vector.memset(kit.stat[:, 63:64], 0.0).then_inc(s_glu, 1)

                def body(i):
                    dve.wait_ge(s_glu, 1 + i)
                    for j in range(2):
                        nc.vector.tensor_copy(taps[:, j, :, :], taps_all[:, :, ds(FT * j + 4 * i, 4)]
                                              ).then_inc(s_taps, 1)
                    dve.wait_ge(s_taps, 2 + 2 * i)
                    for j in range(2):
                        for q in range(4):
                            n = 2 * (4 * j + q)
                            dve.wait_ge(s_base, 8 * i + 4 * j + 2 * (q // 2) + 2)
                            u = ps[:, 2 * j + q // 2, (q % 2) * S:(q % 2 + 1) * S]
                            nc.vector.scalar_tensor_tensor(y[:, j, q, 1:S], u[:, 0:S - 1], taps[:, j, 1, q:q + 1],
                                                           y[:, j, q, 1:S], ALU.mult, ALU.add).then_inc(s_conv, 1)
                            dve.wait_ge(s_conv, per * i + n + 1)
                            step = nc.vector.scalar_tensor_tensor(y[:, j, q, 2:S], u[:, 0:S - 2],
                                                                  taps[:, j, 0, q:q + 1], y[:, j, q, 2:S], ALU.mult,
                                                                  ALU.add).then_inc(s_conv, 1)
                        dve.wait_ge(s_conv, per * i + 8 * (j + 1))
                        nc.vector.memset(kit.stat[:, 62:63], 0.0).then_inc(kit.pair_free[j], 1)
                    dve.wait_ge(s_silu, 1 + i)
                    nc.vector.tensor_tensor(outf[:, ds(4 * S * i, 4 * S)], flat(y[:, 0, :, :]), flat(y[:, 1, :, :]),
                                            ALU.mult).then_inc(s_glu, 1)
                run_turns(dve, 0, turns, body)
    kit.units = first + 8 * turns
    kit.pairs = [u + turns for u in uses]

def program(nc, ins, at, out):
    with ExitStack() as ctx:
        kit = Kit(nc, ctx, ins, at)
        kit.turns = 0
        mem = {"bias_dram": nc.dram_tensor("bias_rows", (AH, 2 * S), F32, kind="Internal")}

        w_in = ins["w_in"][0]
        q0, k0, v0, gq0, gv0, gr0, lr0 = 0, AW, 2 * AW, 3 * AW, 3 * AW + 2 * GH * GK, 3 * AW + 2 * GH * GK + GH * GV, \
            3 * AW + 2 * GH * GK + 2 * GH * GV
        first_src = lambda i, j: (w_in, q0 + UN * j)
        stage_setup(kit, mem, lambda sp: load_pair(kit, sp, 0, 0, first_src, False))
        norm_steps(kit, kit.x, None, True, lambda k: kit.cols("attn_norm_w", k), None, None)
        mix = ctx.enter_context(ExitStack())
        gqk = kit.sb("gqk_T", [P, 2 * GH, S], mix)
        gv = kit.sb("gv_rows", [P, ST, GH * GV], mix)
        gr = kit.sb("gr_rows", [P, ST, GH * GV], mix)
        glr = kit.sb("glr_T", [GRANK, 2, S], mix)
        att = ctx.enter_context(ExitStack())
        qkT = kit.sb("qk_T", [P, 2 * AW // P, S], att)
        v = kit.sb("v_rows", [P, ST, AW], att)
        wlr = kit.sb("w_lr", [P, KT, 2 * GRANK], att)
        lr_ready = kit.loads(1)
        s_lr = kit.sem("lowrank_codes")

        def lr_sync(sp):
            sp.dma_start(wlr[:, :, :], w_in[:, lr0:lr0 + 2 * GRANK].rearrange("(k p) n -> p k n", p=P)
                         ).then_inc(kit.loaded, 16)

        def lr_pe(pe):
            pe.wait_ge(kit.loaded, lr_ready)
            for d in range(2):
                for k in range(KT):
                    ins_ = nc.tensor.matmul(kit.ps[0:GRANK, 6 + d, 0:S], lhsT=wlr[:, k, d * GRANK:(d + 1) * GRANK],
                                            rhs=kit.hT[:, k, :], start=(k == 0), stop=(k == KT - 1))
                ins_.then_inc(s_lr, 1)

        def lr_act(act):
            for d in range(2):
                act.wait_ge(s_lr, d + 1)
                kit.act(nc.scalar.activation(glr[:, d, :], kit.ps[0:GRANK, 6 + d, 0:S], ACT.Copy))

        qk_flat = flat(qkT[:, :, :])
        gqk_flat = flat(gqk[:, :, :])

        def at_T(t, base):
            return lambda i, j: t[:, ds(base + 4 * S * j + 8 * S * i, 4 * S)]

        def at_rows(t, base):
            return lambda i, j: t[:, :, ds(base + UN * j + 2 * UN * i, UN)]

        parts = [Part("T", 1, lambda i, j: (w_in, q0 + UN * j), at_T(qk_flat, 0), AD ** -0.5),
                 Part("T", 1, lambda i, j: (w_in, k0 + UN * j), at_T(qk_flat, 8 * S)),
                 Part("rows", 1, lambda i, j: (w_in, v0 + UN * j), at_rows(v, 0)),
                 Part("T", 1, lambda i, j: (w_in, gq0 + UN * j), at_T(gqk_flat, 0)),
                 Part("rows", 1, lambda i, j: (w_in, gv0 + UN * j), at_rows(gv, 0)),
                 Part("rows", 1, lambda i, j: (w_in, gr0 + UN * j), at_rows(gr, 0))]
        w_out = ins["w_out"][0]
        wo_src = lambda i, j: (w_out, UN * j + 2 * UN * i)
        stage_product(kit, parts, kit.hT, lambda sp, n: load_pair(kit, sp, n, 0, wo_src, True),
                      extra_pe=lr_pe, extra_act=lr_act, extra_sync=lr_sync)
        stage_attention(kit, qkT[:, 0:AW // P, :], qkT[:, AW // P:, :], v, mem["bias_dram"], kit.hT)
        att.close()

        stage_gla(kit, gqk, gv, gr, glr, kit.hT[:, AW // P:, :])
        mix.close()
        ffn = ctx.enter_context(ExitStack())
        ada = Ada(kit, ffn)
        w_gate, w_up, w_down = ins["w_gate"][0], ins["w_up"][0], ins["w_down"][0]
        with ExitStack() as st:
            mixed = kit.sb("mixed", [P, ST, D], st)
            glu_src = lambda i, j: ((w_gate, w_up)[j], 0)
            stage_project(kit, w_out, ada, True, mixed[:, :, :],
                          lambda sp, n: load_pair(kit, sp, n, 0, glu_src, True))
            stage_add(kit, mixed, None)
        norm_steps(kit, kit.x, None, True, lambda k: kit.cols("ffn_norm_w", k), None, None)
        with ExitStack() as st:
            actT = kit.sb("act_T", [P, F1 // P, S], st)
            silu = kit.sb("silu", [P, 4 * S], st)

            def down_head(sp, n):
                for k in range(SLOTS):
                    load_wide(kit, sp, n + k, 0, w_down, P * k)
            stage_glu(kit, ada, actT[:, :, :], silu[:, :], w_gate, w_up, down_head)
            w2 = ins["w_in_2"][0]
            r_src = lambda i, j: (w2, (0, 2 * RH * RK + 2 * RH * RV)[j])
            stage_down(kit, w_down, F1 // P, actT, kit.x, lambda sp, n: load_pair(kit, sp, n, 0, r_src, True))

        with ExitStack() as st:
            fin = kit.sb("final_w", [P, D], st)
            kit.loads(1)
            with nc.Block() as block:
                @block.sync
                def _(sp):
                    sp.dma_start(fin[:, :], ins["final_norm_w"].partition_broadcast(P)).then_inc(kit.loaded, 16)
                    sp.wait_ge(kit.loaded, kit.loads_done)
            norm_steps(kit, kit.x, None, False, None, None, fin)
        ffn.close()
        modcols = kit.modcols
        stage_modulation(kit, modcols)

        def norm_mod(n):
            norm_steps(kit, kit.x, None, True, lambda k: kit.modT[:, KT * n + k:KT * n + k + 1],
                       lambda k: modcols[:, (8, 56)[n] + k:(8, 56)[n] + k + 1], None)
        norm_mod(0)
        st_rw = ctx.enter_context(ExitStack())
        rw = kit.sb("rw_T", [P, 3 * RWW // P, S], st_rw)
        low = kit.sb("low_T", [P, 4, S], st_rw)
        st_moba = ctx.enter_context(ExitStack())
        mqk = kit.sb("mqk_T", [P, 2 * MH, S], st_moba)
        mv = kit.sb("mv_rows", [P, ST, MH * MD], st_moba)
        st_ret = ctx.enter_context(ExitStack())
        rqk = kit.sb("rqk_T", [P, 4, S], st_ret)
        rvg = kit.sb("rvg_rows", [P, ST, 2 * RH * RV], st_ret)
        with ExitStack() as st:
            LW = DRANK + ARANK + GGRANK
            wlow = kit.sb("w_low", [P, KT, LW], st)
            low_ready = kit.loads(1)
            s_low = kit.sem("codes2")
            l0 = RCOLS + 3 * RWW
            m0 = RCOLS + WCOLS
            spans = ((0, DRANK), (DRANK, DRANK + ARANK), (DRANK + ARANK, DRANK + ARANK + P), (DRANK + ARANK + P, LW))

            def low_sync(sp):
                sp.dma_start(wlow[:, :, :], w2[:, l0:l0 + LW].rearrange("(k p) n -> p k n", p=P)).then_inc(kit.loaded, 16)

            def low_pe(pe):
                pe.wait_ge(kit.loaded, low_ready)
                for q, (a, b) in enumerate(spans):
                    for k in range(KT):
                        i_ = nc.tensor.matmul(kit.ps[0:b - a, 4 + q, 0:S], lhsT=wlow[:, k, a:b], rhs=kit.hT[:, k, :],
                                              start=(k == 0), stop=(k == KT - 1))
                    i_.then_inc(s_low, 1)

            def low_act(act):
                for q, (a, b) in enumerate(spans):
                    act.wait_ge(s_low, q + 1)
                    kit.act(nc.scalar.activation(low[0:b - a, q, :], kit.ps[0:b - a, 4 + q, 0:S], ACT.Copy))

            rwf, rqkf, mqkf = flat(rw[:, :, :]), flat(rqk[:, :, :]), flat(mqk[:, :, :])
            c1 = RCOLS
            parts = [Part("T", 1, r_src, lambda i, j: (rqkf, rwf)[j][:, 0:4 * S]),
                     Part("T", 1, lambda i, j: (w2, c1 + RWW + RWW * j), at_T(rwf, 4 * S)),
                     Part("T", 1, lambda i, j: (w2, m0 + UN * j), at_T(mqkf, 0), MD ** -0.5),
                     Part("T", 1, lambda i, j: (w2, m0 + MH * MD + UN * j), at_T(mqkf, 8 * S)),
                     Part("rows", 1, lambda i, j: (w2, 2 * RH * RK + UN * j), at_rows(rvg, 0)),
                     Part("rows", 1, lambda i, j: (w2, m0 + 2 * MH * MD + UN * j), at_rows(mv, 0))]
            wo2 = ins["w_out_2"][0]
            wo2_src = lambda i, j: (wo2, UN * j)
            stage_product(kit, parts, kit.hT, lambda sp, n: load_pair(kit, sp, n, 0, wo2_src, True),
                          extra_pe=low_pe, extra_act=low_act, extra_sync=low_sync)
        stage_retention(kit, rqk, rvg, kit.hT[:, 0:4, :])
        st_ret.close()
        stage_moba(kit, mqk, mv, kit.hT[:, 8:16, :])
        st_moba.close()
        stage_rwkv(kit, rw, low, kit.hT[:, 4:8, :])
        st_rw.close()
        w_up2, w_down2 = ins["w_ffn_up_2"][0], ins["w_ffn_down_2"][0]
        up_src = lambda i, j: (w_up2, F2 * j + UN * i)
        with ExitStack() as st:
            mixed = kit.sb("mixed2", [P, ST, D], st)
            row = kit.sb("gate1_row", [P, D], st)
            stage_gate_row(kit, "gate1", modcols, lambda k: 40 + k, row)
            stage_project(kit, wo2, ada, False, mixed[:, :, :],
                          lambda sp, n: load_pair(kit, sp, n, 0, up_src, True))
            stage_add(kit, mixed, row[:, :])
        norm_mod(1)
        with ExitStack() as st:
            actT = kit.sb("act2_T", [P, F2 // P, S], st)

            def down2_head(sp, n):
                for k in range(SLOTS):
                    load_wide(kit, sp, n + k, 0, w_down2, P * k)
            stage_conv_glu(kit, w_up2, actT[:, :, :], down2_head)
            gate = kit.sb("gate2_row", [P, D], st)
            stage_gate_row(kit, "gate2", modcols, lambda k: 88 + k if k < 8 else k - 8, gate)
            stage_down(kit, w_down2, F2 // P, actT, kit.x, lambda sp, n: None, gate)
        with ExitStack() as st:
            fin = kit.sb("final_w2", [P, D], st)
            kit.loads(1)
            with nc.Block() as block:
                @block.sync
                def _(sp):
                    sp.dma_start(fin[:, :], ins["norm_final_2"].partition_broadcast(P)).then_inc(kit.loaded, 16)
                    sp.wait_ge(kit.loaded, kit.loads_done)
            norm_steps(kit, kit.x, None, False, None, None, fin)
        s_fin = kit.sem("stored")
        with nc.Block() as block:
            @block.sync
            def _(sp):
                sp.dma_start(out.rearrange("b (t p) d -> p (b t) d", p=P), kit.x[:, :, :]).then_inc(s_fin, 16)
                sp.wait_ge(s_fin, 16)


INPUTS = ["x", "attn_norm_w", "w_in", "rel_bias_table", "gla_gate_w_fwd", "gla_gate_b_fwd", "gla_gate_w_bwd",
          "gla_gate_b_bwd", "gla_norm_w", "w_out", "ffn_norm_w", "w_gate", "w_up", "w_down", "final_norm_w", "c_2",
          "w_in_2", "w_out_2", "rwkv_mu_2", "rwkv_w0_2", "rwkv_w_up_2", "rwkv_a0_2", "rwkv_a_up_2", "rwkv_g_up_2",
          "rwkv_k_k_2", "rwkv_k_a_2", "rwkv_r_k_2", "rwkv_ln_w_2", "rwkv_ln_b_2", "w_ffn_up_2", "ffn_conv_w_2",
          "ffn_conv_b_2", "w_ffn_down_2", "w_ada_2", "b_ada_2", "norm_mix_2", "norm_ffn_2", "norm_final_2"]


def kernel(**inputs):
    import concourse.bacc as bacc
    from concourse.bass_utils import run_bass_kernel_spmd as run

    nc = bacc.Bacc("TRN2", target_bir_lowering=False, num_devices=1)
    consts, at = constants()
    arrays, aps = {}, {}
    for name in INPUTS + ["consts"]:
        a = np.ascontiguousarray(consts if name == "consts" else inputs[name])
        arrays[f"in_{name}_dram"] = a
        aps[name] = nc.dram_tensor(f"in_{name}_dram", a.shape, mybir.dt.from_np(a.dtype), kind="ExternalInput").ap()
    out = nc.dram_tensor("out_0_dram", (1, S, D), F32, kind="ExternalOutput").ap()
    program(nc, aps, at, out)
    return run(nc, [arrays], core_ids=[0]).results[0]["out_0_dram"]
```

```python
from contextlib import ExitStack
import math

import numpy as np

import concourse.bass as bass
from concourse import mybir

ALU = mybir.AluOpType
ACT = mybir.ActivationFunctionType
AX = mybir.AxisListType.X
F32 = mybir.dt.float32
R32 = mybir.dt.float32r
ds = bass.ds

P = 128
S = 256
ST = S // P
D = 2048
KT = D // P
NORM_EPS = 1e-6
AH, AD = 16, 64
AW = AH * AD
BUCKETS, MAXDIST = 32, 1024
PATTERNS = ((128, 1), (512, 4), (2048, 16))
GH, GK, GV = 4, 128, 256
GCH = 64
GRANK = 16
GTAU = 16.0
F1 = 5632
RH, RK, RV = 4, 64, 128
RWH, RWN = 8, 64
RWW = RWH * RWN
DRANK, ARANK, GGRANK = 96, 96, 256
GN_EPS = 64e-5
MH, MD = 8, 128
F2 = 5632
RCOLS = 2 * RH * RK + 2 * RH * RV
WCOLS = 3 * RWW + DRANK + ARANK + GGRANK
CH = 64
NCH = S // CH

LOADS = 4
UK, UN = 4, 512
UNIT = UK * UN // 2
SPLITS = 4
AHEAD = 3
ADA_GROUPS = 6 * D // (2 * UN)

COLS = {}
_n = 0
for _name, _w in (("attn_norm_w", 16), ("ffn_norm_w", 16), ("norm_mix_2", 16), ("norm_ffn_2", 16), ("c_2", 16),
                  ("gla_norm_w", 8), ("mu_rkv", 12), ("rwkv_w0_2", 4), ("rwkv_a0_2", 4), ("rwkv_k_k_2", 4),
                  ("rwkv_k_a_2", 4), ("rwkv_r_k_2", 4), ("rwkv_ln_w_2", 4), ("rwkv_ln_b_2", 4),
                  ("gla_gate_b_fwd", 4), ("gla_gate_b_bwd", 4), ("mu_wd", 1), ("mu_wa", 1), ("mu_wg", 2),
                  ("conv_w0", 88), ("conv_w1", 88), ("conv_w2", 88), ("conv_b", 88)):
    COLS[_name] = _n
    _n += _w
NCOLS = _n


def t5_bucket(rel):
    nb = BUCKETS // 2
    n = np.abs(rel)
    exact = nb // 2
    large = exact + (np.log(np.maximum(n, 1) / exact) / math.log(MAXDIST / exact) * (nb - exact)).astype(np.int64)
    return np.where(rel > 0, nb, 0) + np.where(n < exact, n, np.minimum(large, nb - 1))


def constants():
    i = np.arange(P)
    r, c = i[:, None], i[None, :]
    same = (r // CH) == (c // CH)
    parts = [("ident", r == c), ("ones", np.ones((P, P))), ("headsum", same), ("flip", r + c == P - 1),
             ("incl", same & (r <= c)), ("strict", same & (r < c)), ("anti", same & (r >= c))]
    b = 1
    while b < CH:
        lvl = (r // (2 * b) == c // (2 * b)) & (r % (2 * b) < b) & (c % (2 * b) >= b)
        parts.append((f"lvlT{b}", lvl))
        if b == 1:
            parts.append(("lvl1", lvl.T))
        b *= 2
    tok = np.arange(S)
    off = tok[None, :] - tok[:, None]
    count = sum(((off % dil == 0) & (np.abs(off) <= win // 2)).astype(np.float64) for win, dil in PATTERNS)
    parts.append(("carry", np.broadcast_to(np.tile(tok % CH != 0, 4), (P, 4 * S))))
    lnc = np.where(count > 0, np.log(np.maximum(count, 1)), -1e30)
    parts.append(("lncount", lnc.reshape(ST, P, S).transpose(1, 0, 2).reshape(P, -1)))
    g = np.log1p(-np.exp2(-5.0 - np.arange(RH)))
    d = tok[None, :] - i[:, None]
    ret = np.where(d[:, None, :] >= 0, np.exp(g[None, :, None] * np.maximum(d, 0)[:, None, :]), 0.0) * RK ** -0.5
    parts.append(("retdecay", ret.reshape(P, -1)))
    dist = np.where(off <= 0, -off, 1e34)
    parts.append(("distance", dist.reshape(ST, P, S).transpose(1, 0, 2).reshape(P, -1)))
    hot = np.zeros((P, 2 * S))
    m = np.arange(2 * S - 1)
    hot[t5_bucket(m - (S - 1)), m] = 1
    parts.append(("onehot", hot))
    at, n = {}, 0
    for name, a in parts:
        at[name] = (n, n + a.shape[1])
        n += a.shape[1]
    return np.concatenate([np.asarray(a, np.float32) for _, a in parts], axis=1), at


class Kit:

    def __init__(self, nc, ctx, ins, at):
        self.nc, self.ins, self.at = nc, ins, at
        self.ctx = ctx
        self.units = 0
        self.pairs = [0, 0]
        self.loads_done = 0
        self.norms = 0
        self.dve_steps = 0
        self.act_steps = 0
        sb = self.sb
        self.x = sb("x_rows", [P, ST, D])
        at_h = nc.sbuf_base
        self.hT = sb("h_T", [P, KT, S])
        self.x_lo_t = nc.alloc_sbuf_tensor_at("h_lo_T", [P, KT, S], R32, offset=-(-at_h // 32) * 32)
        self.raw = sb("raw_weights", [P, LOADS, 2 * UNIT])
        self.w_hi_t = sb("weights_hi", [P, SPLITS, UNIT], dt=R32)
        self.w_lo_t = sb("weights_lo", [P, SPLITS, UNIT], dt=R32)
        self.x_splits = self.act_splits = self.ada_groups = 0
        self.resident = at["carry"][1]
        self.cst = sb("cst", [P, self.resident])
        self.col = sb("col", [P, NCOLS])
        self.stat = sb("stat", [P, 64])
        self.modT = sb("modT", [P, 2 * KT])
        self.modcols = sb("modcols", [P, 6 * D // P])
        self.ps = ctx.enter_context(nc.psum_tensor("ps", [P, 8, 512], F32))
        self.weights_in = [self.sem(f"weights_in{i}") for i in range(LOADS)]
        self.w_hi, self.w_lo, self.x_hi, self.x_lo, self.a_hi, self.a_lo = (
            self.sem(n) for n in ("weights_hi", "weights_lo", "x_hi", "x_lo", "act_hi", "act_lo"))
        self.ada_w = [self.sem("ada_w0"), self.sem("ada_w1")]
        self.ada_b, self.ada_acc, self.ada_sum, self.ada_out = (
            self.sem("ada_" + n) for n in ("b_loaded", "acc", "sum", "out"))
        self.weights_used = self.sem("weights_used")
        self.pair_free = [self.sem(f"pair_free{i}") for i in range(2)]
        self.dve_order = self.sem("dve_order")
        self.act_order = self.sem("act_order")
        self.loaded = self.sem("loaded")
        self.spreads = 0
        self.spread = [self.sem("gate_row_" + n) for n in ("diag", "spread", "copied")]
        self.n_sumsq = self.sem("norm_sumsq")
        self.n_mean = self.sem("norm_mean")
        self.n_rms = self.sem("norm_rms")
        self.n_rstd = self.sem("norm_rstd")
        self.n_scaled = self.sem("norm_scaled")
        self.n_turned = self.sem("norm_turned")
        self.n_out = [self.sem("norm_out_dve"), self.sem("norm_out_act")]

    def loads(self, n):
        self.loads_done = self.loads_done + 16 * n
        return self.loads_done

    def sb(self, name, shape, ctx=None, dt=F32):
        return (ctx or self.ctx).enter_context(self.nc.sbuf_tensor(name, shape, dt))

    def sem(self, name):
        return self.ctx.enter_context(self.nc.semaphore(name))

    def const_src(self, name):
        a, b = self.at[name]
        return self.ins["consts"][:, a:b]

    def c(self, name):
        a, b = self.at[name]
        return self.cst[:, a:b]

    def cols(self, name, k):
        return self.col[:, COLS[name] + k:COLS[name] + k + 1]

    def dve(self, ins):
        self.dve_steps += 1
        ins.then_inc(self.dve_order, 1)
        self.nc.vector.wait_ge(self.dve_order, self.dve_steps)

    def act(self, ins):
        self.act_steps += 1
        ins.then_inc(self.act_order, 1)
        self.nc.scalar.wait_ge(self.act_order, self.act_steps)


def flat(ap):
    return ap.rearrange("p a b -> p (a b)")


def load(kit, sp, l, i, src):
    if l >= LOADS:
        sp.wait_ge(kit.w_lo, 2 * (l - LOADS) + 2 + 16 * i)
    sp.dma_start(kit.raw[:, l % LOADS, :].rearrange("p (k n) -> p k n", k=src.shape[1]), src
                 ).then_inc(kit.weights_in[l % LOADS], 16)


def block_src(w, u, col):
    return w[u * UK * P:(u + 1) * UK * P, ds(col, UN)].rearrange("(k p) n -> p k n", p=P)


def load_block(kit, sp, l, i, w, col):
    for u in range(4):
        load(kit, sp, l + u, i, block_src(w, u, col))


def wide_src(w, row):
    return w[ds(row, P), :].rearrange("p (a n) -> p a n", a=1)


def split_hi(kit, act, n, i):
    act.wait_ge(kit.weights_in[(n // 2) % LOADS], 16 * (n // (2 * LOADS) + 1) + 32 * i)
    if n >= SPLITS:
        act.wait_ge(kit.weights_used, n - SPLITS + 1 + 16 * i)
    raw = kit.raw[:, (n // 2) % LOADS, (n % 2) * UNIT:(n % 2 + 1) * UNIT]
    kit.nc.scalar.activation(kit.w_hi_t[:, n % SPLITS, :], raw, ACT.Copy).then_inc(kit.w_hi, 1)


def split_lo(kit, dve, n, i):
    dve.wait_ge(kit.w_hi, n + 1 + 16 * i)
    raw = kit.raw[:, (n // 2) % LOADS, (n % 2) * UNIT:(n % 2 + 1) * UNIT]
    kit.nc.vector.tensor_tensor(kit.w_lo_t[:, n % SPLITS, :], raw, kit.w_hi_t[:, n % SPLITS, :].bitcast(F32),
                                ALU.subtract).then_inc(kit.w_lo, 1)


def split_x_hi(kit, act):
    for u in range(4):
        kit.nc.scalar.activation(kit.x_hi_t[:, 4 * u:4 * u + 4, :], kit.hT[:, 4 * u:4 * u + 4, :], ACT.Copy
                                 ).then_inc(kit.x_hi, 1)


def split_x_lo(kit, dve, base):
    for u in range(4):
        dve.wait_ge(kit.x_hi, base + u + 1)
        kit.nc.vector.tensor_tensor(kit.x_lo_t[:, 4 * u:4 * u + 4, :], kit.hT[:, 4 * u:4 * u + 4, :],
                                    kit.x_hi_t[:, 4 * u:4 * u + 4, :].bitcast(F32), ALU.subtract
                                    ).then_inc(kit.x_lo, 1)


def multiply_block(kit, pe, form, j, n0, i, use, xbase, mid=None):
    nc = kit.nc
    xh, xl = kit.x_hi_t, kit.x_lo_t
    pe.wait_ge(kit.pair_free[j], use + 1 + i)
    for u in range(8):
        n = n0 + u
        s = n % SPLITS
        if j == 0 and u % 2 == 0:
            pe.wait_ge(kit.x_lo, xbase + u // 2 + 1)
        pe.wait_ge(kit.w_lo, n + 1 + 16 * i)
        for kk in range(2):
            k = 2 * u + kk
            a = kk * UN
            for q in range(2 if form == "rows" else 4):
                if form == "rows":
                    out = kit.ps[:, 2 * j + q, :]
                    wh, wl = (w[:, s, a:a + UN] for w in (kit.w_hi_t, kit.w_lo_t))
                    h, l = (x[:, k, q * P:(q + 1) * P] for x in (xh, xl))
                    passes = ((h, wh), (h, wl), (l, wh))
                    start = k == 0
                else:
                    out = kit.ps[:, 2 * j + q // 2, (q % 2) * S:(q % 2 + 1) * S]
                    wh, wl = (w[:, s, a + q * P:a + (q + 1) * P] for w in (kit.w_hi_t, kit.w_lo_t))
                    h, l = xh[:, k, :], xl[:, k, :]
                    passes = ((wh, h), (wh, l), (wl, h))
                    start = k == 0 and q % 2 == 0
                for m, (lhsT, rhs) in enumerate(passes):
                    ins = nc.tensor.matmul(out, lhsT=lhsT, rhs=rhs, start=start and m == 0,
                                           stop=(k == KT - 1 and m == 2), skip_group_check=True)
        ins.then_inc(kit.weights_used, 1)
        if mid and u == 0:
            mid()


class Part:

    def __init__(self, form, turns, srcs, dst, scale=1.0):
        self.form, self.turns, self.srcs, self.dst, self.scale = form, turns, srcs, dst, scale


def run_turns(eng, start, turns, body):
    if turns - start > 1:
        with eng.Fori(start, turns) as i:
            body(i)
    elif turns - start == 1:
        body(start)


def stage_product(kit, parts, head_next, ada=None, groups=(), low=None):
    nc = kit.nc
    first = kit.units
    starts, n = [], first
    for part in parts:
        starts.append(n)
        n += 16 * part.turns
    end = n
    uses = list(kit.pairs)
    xbase = kit.x_splits
    kit.x_splits += 4
    lead = kit.ada_groups

    with nc.Block() as block:
        @block.sync
        def _(sp):
            if low:
                low[0](sp)
            for p, part in enumerate(parts):
                l = starts[p] // 2
                group = groups[p] if p < len(groups) else None

                def rest(i, then):
                    for half in range(2):
                        w, col = part.srcs(i, 1) if half == 0 else then if then else (None, None)
                        for u in range(4):
                            if group is not None:
                                ada.load(sp, lead + p, 0, 4 * half + u, 2 * UN * group)
                                if half == 0 and u == 2:
                                    ada.load_bias(sp, lead + p, 0, 2 * UN * group)
                            if w is not None:
                                load(kit, sp, l + 4 + 4 * half + u, i, block_src(w, u, col))
                run_turns(sp, 0, part.turns - 1, lambda i: rest(i, part.srcs(i + 1, 0)))
                rest(part.turns - 1, parts[p + 1].srcs(0, 0) if p + 1 < len(parts) else None)
            head_next(sp, end // 2)

        @block.tensor
        def _(pe):
            if low:
                low[1](pe)
            done = 0
            for p, part in enumerate(parts):
                def body(i):
                    for j in range(2):
                        mid = None
                        if j == 0 and ada and 0 < p <= len(groups):
                            mid = lambda: ada.sums(pe, lead + p, 0)
                        multiply_block(kit, pe, part.form, j, starts[p] + 8 * j, i, uses[j] + done, xbase, mid)
                run_turns(pe, 0, part.turns, body)
                done += part.turns
            if ada and len(groups) == len(parts):
                ada.sums(pe, lead + len(groups), 0)

        @block.scalar
        def _(act):
            split_x_hi(kit, act)
            for p, part in enumerate(parts):
                def body(i):
                    for j in range(2):
                        for u in range(8):
                            split_hi(kit, act, starts[p] + AHEAD + 8 * j + u, i)
                        act.wait_ge(kit.weights_used, starts[p] + 8 * (j + 1) + 16 * i)
                        src = kit.ps[:, 2 * j:2 * j + 2, :]
                        nc.scalar.activation(part.dst(i, j), flat(src) if part.form == "T" else src, ACT.Copy,
                                             scale=part.scale).then_inc(kit.pair_free[j], 1)
                run_turns(act, 0, part.turns, body)
            if low:
                low[2](act)

        @block.vector
        def _(dve):
            if low:
                low[3](dve)
            split_x_lo(kit, dve, xbase)
            for p, part in enumerate(parts):
                def body(i):
                    for s in range(16):
                        split_lo(kit, dve, starts[p] + AHEAD + s, i)
                        if p < len(groups):
                            if s == 0 and p > 0:
                                ada.copy(dve, lead + p, 0, groups[p - 1])
                            ada.product(dve, lead + p, 0, s)
                run_turns(dve, 0, part.turns, body)
            if groups:
                ada.copy(dve, lead + len(groups), 0, groups[-1])

    kit.units = end
    kit.pairs = [u + (end - first) // 16 for u in uses]
    kit.ada_groups += len(groups)


def stage_down(kit, w, w_tiles, actT, out, head_next, gate=None):
    nc = kit.nc
    first, k_lo = kit.units, kit.act_splits
    kit.act_splits += w_tiles
    lead = w_tiles % 8
    R = 8
    last = head_next is None

    def in_turns(eng, body):
        for k in range(lead):
            body(k, 0, 0)
        turns = w_tiles // 8
        with eng.Fori(0, turns - 1) as i:
            for k in range(lead, lead + 8):
                body(k, i, 0)
        for k in range(lead, lead + 8):
            body(k, turns - 1, w_tiles - 8 - lead)

    with nc.Block() as block:
        @block.sync
        def _(sp):
            def body(k, i, _):
                load(kit, sp, first // 2 + k, i, wide_src(w, P * k + 8 * P * i))
            for k in range(LOADS, lead):
                body(k, 0, 0)
            turns = w_tiles // 8
            with sp.Fori(0, turns) as i:
                for k in range(max(lead, LOADS), lead + 8):
                    body(k, i, 0)
            if not last:
                head_next(sp, first // 2 + w_tiles)

        @block.tensor
        def _(pe):
            def body(k, i, past):
                pe.wait_ge(kit.a_lo, k_lo + k + 1 + 8 * i)
                for half in range(2):
                    n = first + 2 * k + half
                    s = n % SPLITS
                    pe.wait_ge(kit.w_lo, n + 1 + 16 * i)
                    for t in range(ST):
                        h, l = (x[:, k % R, t * P:(t + 1) * P] for x in (kit.x_hi_t, kit.x_lo_t))
                        for q in range(2):
                            wh, wl = (x[:, s, q * UN:(q + 1) * UN] for x in (kit.w_hi_t, kit.w_lo_t))
                            for m, (lhsT, rhs) in enumerate(((h, wh), (h, wl), (l, wh))):
                                ins = nc.tensor.matmul(kit.ps[:, 4 * t + 2 * half + q, :], lhsT=lhsT, rhs=rhs,
                                                       start=(k == 0 and m == 0), stop=(k + past == w_tiles - 1
                                                                                        and m == 2),
                                                       skip_group_check=True)
                    ins.then_inc(kit.weights_used, 1)
            in_turns(pe, body)

        @block.scalar
        def _(act):
            def tile(k, i):
                if k >= R:
                    act.wait_ge(kit.weights_used, first + 2 * (k - R) + 2 + 16 * i)
                nc.scalar.activation(kit.x_hi_t[:, k % R, :], actT[:, ds(k + 8 * i, 1), :].rearrange(
                    "p a s -> p (a s)"), ACT.Copy).then_inc(kit.a_hi, 1)

            def body(k, i, past):
                for half in range(2):
                    if not (last and k + past == w_tiles - 1) and not (last and k + past == w_tiles - 2 and half):
                        split_hi(kit, act, first + 2 * k + half + AHEAD, i)
                if k + past + 4 < w_tiles:
                    tile(k + 4, i)
            for k in range(4):
                tile(k, 0)
            in_turns(act, body)

        @block.vector
        def _(dve):
            def tile(k, i):
                dve.wait_ge(kit.a_hi, k_lo + k + 1 + 8 * i)
                nc.vector.tensor_tensor(kit.x_lo_t[:, k % R, :], actT[:, ds(k + 8 * i, 1), :].rearrange(
                    "p a s -> p (a s)"), kit.x_hi_t[:, k % R, :].bitcast(F32), ALU.subtract).then_inc(kit.a_lo, 1)

            def body(k, i, past):
                for half in range(2):
                    if not (last and k + past == w_tiles - 1) and not (last and k + past == w_tiles - 2 and half):
                        split_lo(kit, dve, first + 2 * k + half + AHEAD, i)
                if k + past + 4 < w_tiles:
                    tile(k + 4, i)
            for k in range(4):
                tile(k, 0)
            in_turns(dve, body)
            dve.wait_ge(kit.weights_used, first + 2 * w_tiles)
            for t in range(ST):
                sums = flat(kit.ps[:, 4 * t:4 * t + 4, :])
                if gate is not None:
                    kit.dve(nc.vector.tensor_tensor(sums, sums, gate[:, :], ALU.mult))
                kit.dve(nc.vector.tensor_tensor(out[:, t, :], sums, out[:, t, :], ALU.add))
    kit.units = first + 2 * w_tiles


def norm_steps(kit, x, tiles, with_T, wcol, bcol, row_w):
    nc = kit.nc
    r = kit.norms
    kit.norms += 1
    turns = kit.turns
    width = KT

    with ExitStack() as st:
        xn = kit.sb(f"xn{r}", [P, ST, D], st) if with_T else None
        with nc.Block() as block:
            @block.scalar
            def _(act):
                for t in range(ST):
                    nc.scalar.activation(flat(kit.ps[:, 0:4, :]), x[:, t, :], ACT.Square,
                                         accum_out=kit.stat[:, t:t + 1]).then_inc(kit.n_sumsq, 1)
                    act.wait_ge(kit.n_sumsq, ST * r + t + 1)
                act.wait_ge(kit.n_mean, r + 1)
                nc.scalar.activation(kit.stat[:, 4:6], kit.stat[:, 2:4], ACT.Sqrt).then_inc(kit.n_rms, 1)
                if with_T:
                    for k in range(1, width, 2):
                        act.wait_ge(kit.n_turned, width * turns + k + 1)
                        nc.scalar.activation(kit.hT[:, k, :], kit.ps[:, 4 + k % 4, 0:S], ACT.Identity,
                                             scale=wcol(k), bias=bcol(k) if bcol else 0.0
                                             ).then_inc(kit.n_out[1], 1)

            @block.vector
            def _(dve):
                dve.wait_ge(kit.n_sumsq, ST * (r + 1))
                nc.vector.tensor_scalar(kit.stat[:, 2:4], kit.stat[:, 0:2], 1.0 / D, NORM_EPS, ALU.mult,
                                        ALU.add).then_inc(kit.n_mean, 1)
                dve.wait_ge(kit.n_rms, r + 1)
                nc.vector.reciprocal(kit.stat[:, 6:8], kit.stat[:, 4:6]).then_inc(kit.n_rstd, 1)
                dve.wait_ge(kit.n_rstd, r + 1)
                for t in range(ST):
                    nc.vector.tensor_scalar(xn[:, t, :] if with_T else x[:, t, :], x[:, t, :],
                                            kit.stat[:, 6 + t:7 + t], None, ALU.mult).then_inc(kit.n_scaled, 1)
                if with_T:
                    for k in range(0, width, 2):
                        dve.wait_ge(kit.n_turned, width * turns + k + 1)
                        if bcol:
                            ins = nc.vector.tensor_scalar(kit.hT[:, k, :], kit.ps[:, 4 + k % 4, 0:S], wcol(k),
                                                          bcol(k), ALU.mult, ALU.add)
                        else:
                            ins = nc.vector.tensor_scalar(kit.hT[:, k, :], kit.ps[:, 4 + k % 4, 0:S], wcol(k),
                                                          None, ALU.mult)
                        ins.then_inc(kit.n_out[0], 1)
                else:
                    dve.wait_ge(kit.n_scaled, ST * (r + 1))
                    for t in range(ST):
                        kit.dve(nc.vector.tensor_tensor(x[:, t, :], x[:, t, :], row_w[:, :], ALU.mult))

            if with_T:
                @block.tensor
                def _(pe):
                    pe.wait_ge(kit.n_scaled, ST * (r + 1))
                    for k in range(width):
                        if k >= 4:
                            pe.wait_ge(kit.n_out[k % 2], width // 2 * turns + (k - 4) // 2 + 1)
                        for t in range(ST):
                            ins = nc.tensor.transpose(kit.ps[:, 4 + k % 4, t * P:(t + 1) * P],
                                                      xn[:, t, k * P:(k + 1) * P], kit.c("ident"))
                        ins.then_inc(kit.n_turned, 1)
    if with_T:
        kit.turns += 1


def stage_setup(kit, mem, head):
    nc, ins = kit.nc, kit.ins
    rows = [("attn_norm_w", 0), ("ffn_norm_w", 0), ("norm_mix_2", 0), ("norm_ffn_2", 0), ("c_2", 0),
            ("gla_norm_w", 0), ("mu_rkv", 0), ("rwkv_w0_2", 0), ("rwkv_a0_2", 0), ("rwkv_k_k_2", 0),
            ("rwkv_k_a_2", 0), ("rwkv_r_k_2", 0), ("rwkv_ln_w_2", 0), ("rwkv_ln_b_2", 0)]
    names = list(COLS)
    width = {n: (COLS[names[i + 1]] if i + 1 < len(names) else NCOLS) - COLS[n] for i, n in enumerate(names)}
    mu = ins["rwkv_mu_2"]
    c3 = 3 * RWW

    def src(name):
        if name == "mu_rkv":
            return mu[0:1, 0:c3].rearrange("a (r f) -> (a r) f", f=P)
        if name == "mu_wg":
            return mu[0:1, c3 + DRANK + ARANK:WCOLS].rearrange("a (r f) -> (a r) f", f=P)
        if name == "rwkv_r_k_2":
            return ins[name].rearrange("a (r h) n -> (a r) (h n)", h=2)
        if name.startswith("conv_w"):
            j = int(name[-1])
            return ins["ffn_conv_w_2"][0, j:j + 1, :].rearrange("a (r f) -> (a r) f", f=P)
        if name == "conv_b":
            return ins["ffn_conv_b_2"].rearrange("a (r f) -> (a r) f", f=P)
        return ins[name].rearrange("a (r f) -> (a r) f", f=P)

    packs = [names[0:14], names[14:19], ["conv_w0"], ["conv_w1"], ["conv_w2"], ["conv_b"]]
    s_zero, s_rows, s_turn, s_col = (kit.sem(n) for n in ("pack_zeroed", "pack_loaded", "pack_turned", "pack_out"))
    s_bias, s_biasrow, s_biasout = (kit.sem(n) for n in ("bias_rows", "bias_rows_copied", "bias_rows_stored"))
    loads = sum(len(p) for p in packs)
    setup_loads = kit.loads(4)

    with ExitStack() as st:
        pack = kit.sb("pack", [P, len(packs), P], st)
        table = kit.sb("table", [BUCKETS, AH], st)
        hot = kit.sb("onehot", [BUCKETS, 2 * S], st)
        brow = kit.sb("brow", [AH, 2 * S], st)
        with nc.Block() as block:
            @block.sync
            def _(sp):
                sp.dma_start(kit.x[:, :, :], ins["x"].rearrange("b (t p) d -> p (b t) d", p=P)
                             ).then_inc(kit.loaded, 16)
                sp.dma_start(kit.cst[:, :], ins["consts"][:, 0:kit.resident]).then_inc(kit.loaded, 16)
                sp.dma_start(table[:, :], ins["rel_bias_table"]).then_inc(kit.loaded, 16)
                sp.dma_start(hot[:, :], kit.const_src("onehot")[0:BUCKETS, :]).then_inc(kit.loaded, 16)
                sp.wait_ge(s_zero, 1)
                for n, names_ in enumerate(packs):
                    at = 0
                    for name in names_:
                        w = width[name]
                        if name in ("mu_wd", "mu_wa"):
                            a = c3 + (DRANK if name == "mu_wa" else 0)
                            sp.dma_start(pack[at:at + 1, n, 0:DRANK], mu[0:1, a:a + DRANK]).then_inc(s_rows, 16)
                        else:
                            sp.dma_start(pack[at:at + w, n, :], src(name)).then_inc(s_rows, 16)
                        at += w
                head(sp)
                sp.wait_ge(s_biasrow, 1)
                sp.dma_start(mem["bias_dram"].ap(), brow[:, :]).then_inc(s_biasout, 16)
                sp.wait_ge(s_biasout, 16)

            @block.vector
            def _(dve):
                nc.vector.memset(pack[:, 1, :], 0.0).then_inc(s_zero, 1)
                for j in range(2):
                    nc.vector.memset(kit.ps[:, 2 * j, 0:8], 0.0).then_inc(kit.pair_free[j], 1)
                at = 0
                for n, names_ in enumerate(packs):
                    w = sum(width[x] for x in names_)
                    dve.wait_ge(s_turn, n + 1)
                    nc.vector.tensor_copy(kit.col[:, at:at + w], kit.ps[:, 4 + n % 2, 0:w]).then_inc(s_col, 1)
                    at += w
                dve.wait_ge(s_bias, 1)
                nc.vector.tensor_copy(brow[:, :], kit.ps[0:AH, 7, :]).then_inc(s_biasrow, 1)
                for n in range(AHEAD):
                    split_lo(kit, dve, n, 0)

            @block.scalar
            def _(act):
                act.wait_ge(s_col, 1)
                a = COLS["c_2"]
                kit.act(nc.scalar.activation(kit.col[:, a:a + KT], kit.col[:, a:a + KT], ACT.Silu))
                for n in range(AHEAD):
                    split_hi(kit, act, n, 0)

            @block.tensor
            def _(pe):
                pe.wait_ge(kit.loaded, setup_loads)
                nc.tensor.matmul(kit.ps[0:AH, 7, :], lhsT=table[:, :], rhs=hot[:, :],
                                 start=True, stop=True).then_inc(s_bias, 1)
                pe.wait_ge(s_rows, 16 * loads)
                for n, names_ in enumerate(packs):
                    w = sum(width[x] for x in names_)
                    if n >= 2:
                        pe.wait_ge(s_col, n - 1)
                    nc.tensor.transpose(kit.ps[:, 4 + n % 2, 0:w], pack[0:w, n, :], kit.c("ident")[0:w, 0:w]
                                        ).then_inc(s_turn, 1)


def stage_attention(kit, qT, kT, v, bias_dram, outT):
    nc = kit.nc
    (s_logits, s_biased, s_max, s_neg, s_exp, s_recip, s_p, s_turned, s_pT, s_out, s_done) = (
        kit.sem("attn_" + n) for n in ("logits", "biased", "max", "negmax", "exp", "recip", "probs",
                                       "turned", "probsT", "out", "stored"))
    tables_ready = kit.loads(AH + 1)
    with ExitStack() as st:
        hank = kit.sb("hankel", [P, AH, 3 * P], st)
        L = kit.sb("logits", [P, 2, ST, S], st)
        E = kit.sb("expd", [P, 2, ST, S], st)
        ET = kit.sb("probsT", [P, 2, ST, S], st)
        lncount = kit.sb("lncount", [P, ST * S], st)
        sc = kit.sb("attn_sc", [P, 2, 4, ST], st)
        mx, neg, tot, rec = (sc[:, :, n, :] for n in range(4))
        ps = kit.ps
        with nc.Block() as block:
            @block.sync
            def _(sp):
                src = bias_dram.ap()
                sp.dma_start(lncount[:, :], kit.const_src("lncount")).then_inc(kit.loaded, 16)
                for h in range(AH):
                    sp.dma_start(hank[:, h, :], bass.AP(tensor=src.tensor, offset=h * 2 * S,
                                                        ap=[[1, P], [1, 3 * P]])).then_inc(kit.loaded, 16)

            @block.tensor
            def _(pe):
                def logits(h):
                    hb, tile, b = AD * (h % 2), h // 2, h % 2
                    if h == 0:
                        pe.wait_ge(kit.loaded, tables_ready)
                    if h >= 2:
                        pe.wait_ge(s_biased, h - 1)
                    for t in range(ST):
                        nc.tensor.matmul(ps[:, b, t * S:(t + 1) * S], lhsT=qT[hb:hb + AD, tile, t * P:(t + 1) * P],
                                         rhs=kT[hb:hb + AD, tile, :], start=True, stop=False)
                        ins = nc.tensor.matmul(ps[:, b, t * S:(t + 1) * S], lhsT=kit.c("flip"),
                                               rhs=hank[:, h, P - t * P:P - t * P + S], start=False, stop=True)
                    ins.then_inc(s_logits, 1)

                logits(0)
                for h in range(AH):
                    if h + 1 < AH:
                        logits(h + 1)
                    b = h % 2
                    pe.wait_ge(s_p, ST * (h + 1))
                    if h >= 2:
                        pe.wait_ge(s_pT, h - 1)
                    for jt in range(ST):
                        for t in range(ST):
                            ins = nc.tensor.transpose(ps[:, 2 + b, jt * S + t * P:jt * S + (t + 1) * P],
                                                      E[:, b, t, jt * P:(jt + 1) * P], kit.c("ident"))
                    ins.then_inc(s_turned, 1)
                    pe.wait_ge(s_pT, h + 1)
                    if h % 2 == 0 and h >= 4:
                        pe.wait_ge(s_done, h // 2 - 1)
                    hb = AD * (h % 2)
                    for jt in range(ST):
                        ins = nc.tensor.matmul(ps[hb:hb + AD, 4 + (h // 2) % 2, 0:S],
                                               lhsT=v[:, jt, h * AD:(h + 1) * AD], rhs=ET[:, b, jt, :],
                                               start=(jt == 0), stop=(jt == ST - 1))
                    ins.then_inc(s_out, 1)

            @block.vector
            def _(dve):
                dve.wait_ge(kit.loaded, tables_ready)
                for h in range(AH + 2):
                    if h < AH:
                        b = h % 2
                        dve.wait_ge(s_logits, h + 1)
                        if h >= 2:
                            dve.wait_ge(s_exp, ST * (h - 1))
                        nc.vector.tensor_tensor(flat(L[:, b, :, :]), ps[:, b, :], lncount[:, :],
                                                ALU.add).then_inc(s_biased, 1)
                        dve.wait_ge(s_biased, h + 1)
                        nc.vector.tensor_reduce(mx[:, b, :], L[:, b, :, :], AX, ALU.max).then_inc(s_max, 1)
                        dve.wait_ge(s_max, h + 1)
                        nc.vector.tensor_scalar(neg[:, b, :], mx[:, b, :], -1.0, None, ALU.mult).then_inc(s_neg, 1)
                    if 1 <= h <= AH:
                        g = h - 1
                        b = g % 2
                        dve.wait_ge(s_exp, ST * (g + 1))
                        nc.vector.reciprocal(rec[:, b, :], tot[:, b, :]).then_inc(s_recip, 1)
                        dve.wait_ge(s_recip, g + 1)
                        for t in range(ST):
                            nc.vector.tensor_scalar(E[:, b, t, :], E[:, b, t, :], rec[:, b, t:t + 1], None,
                                                    ALU.mult).then_inc(s_p, 1)
                    if h >= 3 and h % 2 == 1:
                        pair = (h - 3) // 2
                        dve.wait_ge(s_out, 2 * pair + 2)
                        nc.vector.tensor_copy(outT[:, pair, :], ps[:, 4 + pair % 2, 0:S]).then_inc(s_done, 1)

            @block.scalar
            def _(act):
                for h in range(AH + 1):
                    if h < AH:
                        b = h % 2
                        act.wait_ge(s_neg, h + 1)
                        if h >= 2:
                            act.wait_ge(s_turned, h - 1)
                        for t in range(ST):
                            nc.scalar.activation(E[:, b, t, :], L[:, b, t, :], ACT.Exp, bias=neg[:, b, t:t + 1],
                                                 accum_out=tot[:, b, t:t + 1]).then_inc(s_exp, 1)
                    if h >= 1:
                        g = h - 1
                        act.wait_ge(s_turned, g + 1)
                        if g >= 2:
                            act.wait_ge(s_out, g - 1)
                        nc.scalar.activation(flat(ET[:, g % 2, :, :]), ps[:, 2 + g % 2, :], ACT.Copy
                                             ).then_inc(s_pT, 1)


def stage_gla(kit, gqk, gv, gr, glr, outT, ctx_name="gla"):
    nc, ps, ins = kit.nc, kit.ps, kit.ins
    W = GH * S
    G16 = 1.0 / GTAU
    sem = lambda n: kit.sem("gla_" + n)
    w_ready = kit.loads(2)
    with ExitStack() as st:
        gw = kit.sb("gate_w", [GRANK, 2, GH * GK], st)
        A = kit.sb("gla_a", [P, 2, W], st)
        B = kit.sb("gla_b", [P, 2, W], st)
        G = kit.sb("gla_g", [P, 2, W], st)
        E = kit.sb("gla_e", [P, 2, W], st)
        q_in = kit.sb("gla_qin", [P, 2, W], st)
        k_in = kit.sb("gla_kin", [P, 2, W], st)
        k_end = B
        last = kit.sb("gla_last", [P, 2, GH * NCH], st)
        dec = kit.sb("gla_dec", [P, 2, GH * NCH], st)
        AT = kit.sb("gla_AT", [P, 2, ST, P], st)
        tmp = kit.sb("gla_tmp", [P, 2, S], st)

        s_z, s_s, s_ln, s_G, s_D, s_eq, s_ek, s_ee = (
            sem(n) for n in ("gate", "biased", "softplus", "sums", "to_end", "exp_q", "exp_k", "exp_end"))
        with nc.Block() as block:
            @block.sync
            def _(sp):
                sp.dma_start(gw[:, 0, :], ins["gla_gate_w_fwd"][0]).then_inc(kit.loaded, 16)
                sp.dma_start(gw[:, 1, :], ins["gla_gate_w_bwd"][0]).then_inc(kit.loaded, 16)

            @block.tensor
            def _(pe):
                pe.wait_ge(kit.loaded, w_ready)
                for d in range(2):
                    for m in range(GH):
                        i_ = nc.tensor.matmul(ps[:, 2 * d + m // 2, (m % 2) * S:(m % 2 + 1) * S],
                                              lhsT=gw[:, d, m * P:(m + 1) * P], rhs=glr[:, d, :], start=True,
                                              stop=True)
                    i_.then_inc(s_z, 1)

            @block.vector
            def _(dve):
                for d, name in enumerate(("gla_gate_b_fwd", "gla_gate_b_bwd")):
                    dve.wait_ge(s_z, d + 1)
                    for m in range(GH):
                        nc.vector.tensor_scalar(A[:, d, m * S:(m + 1) * S],
                                                ps[:, 2 * d + m // 2, (m % 2) * S:(m % 2 + 1) * S],
                                                kit.cols(name, m), None, ALU.add).then_inc(s_s, 1)
                dve.wait_ge(s_s, 2 * GH)
                dve.wait_ge(s_ln, 1)
                kit.dve(nc.vector.scalar_tensor_tensor(flat(A[:, :, :]), flat(A[:, :, :]), 0.0, flat(B[:, :, :]),
                                                       ALU.min, ALU.subtract))
                for d in range(2):
                    kit.dve(nc.vector.tensor_tensor_scan(G[:, d, :], kit.c("carry"), A[:, d, :], 0.0, ALU.mult,
                                                         ALU.add))
                chunks = lambda t: t.rearrange("p (g c) -> p g c", c=GCH)
                for d in range(2):
                    kit.dve(nc.vector.tensor_copy(last[:, d, :], chunks(G[:, d, :])[:, :, GCH - 1]))
                kit.dve(nc.vector.tensor_tensor(B[:, 1, :], A[:, 1, :], G[:, 1, :], ALU.subtract))
                lastb = lambda d: last[:, d, :].unsqueeze(2).broadcast_to([P, GH * NCH, GCH])
                nc.vector.tensor_tensor(chunks(G[:, 1, :]), chunks(B[:, 1, :]), lastb(1), ALU.add).then_inc(s_G, 1)
                dve.wait_ge(s_G, 1)
                for d in range(2):
                    nc.vector.tensor_tensor(chunks(B[:, d, :]), lastb(d), chunks(G[:, d, :]),
                                            ALU.subtract).then_inc(s_D, 1)
                qk = flat(gqk[:, :, :])
                dve.wait_ge(s_eq, 1)
                for d in range(2):
                    kit.dve(nc.vector.scalar_tensor_tensor(q_in[:, d, :], qk[:, 0:W], GK ** -0.5, E[:, d, :],
                                                           ALU.mult, ALU.mult))
                dve.wait_ge(s_ek, 1)
                for d in range(2):
                    kit.dve(nc.vector.tensor_tensor(k_in[:, d, :], qk[:, W:2 * W], A[:, d, :], ALU.mult))
                dve.wait_ge(s_ee, 1)
                for d in range(2):
                    kit.dve(nc.vector.tensor_tensor(k_end[:, d, :], qk[:, W:2 * W], B[:, d, :], ALU.mult))

            @block.scalar
            def _(act):
                act.wait_ge(s_s, 2 * GH)
                kit.act(nc.scalar.activation(flat(B[:, :, :]), flat(A[:, :, :]), ACT.Abs))
                kit.act(nc.scalar.activation(flat(E[:, :, :]), flat(B[:, :, :]), ACT.Exp, scale=-1.0))
                nc.scalar.activation(flat(B[:, :, :]), flat(E[:, :, :]), ACT.Ln, bias=1.0).then_inc(s_ln, 1)
                act.wait_ge(s_G, 1)
                nc.scalar.activation(flat(E[:, :, :]), flat(G[:, :, :]), ACT.Exp, scale=G16).then_inc(s_eq, 1)
                nc.scalar.activation(flat(A[:, :, :]), flat(G[:, :, :]), ACT.Exp, scale=-G16).then_inc(s_ek, 1)
                act.wait_ge(s_D, 2)
                nc.scalar.activation(flat(B[:, :, :]), flat(B[:, :, :]), ACT.Exp, scale=G16).then_inc(s_ee, 1)
                kit.act(nc.scalar.activation(flat(dec[:, :, :]), flat(last[:, :, :]), ACT.Exp, scale=G16))

        krow = A[:, :, :].rearrange("p d (t f) -> p d t f", t=ST)
        states = flat(G[:, :, :])[:, 0:6 * GV].rearrange("p (d c v) -> p d c v", d=2, c=3)
        orow = flat(E[:, :, :]).rearrange("p (t f) -> p t f", t=ST)

        def update(d, n):
            bank, half = {(0, 0): (2, 0), (0, 2): (2, 1), (1, 1): (3, 0),
                          (0, 1): (4, 0), (1, 0): (4, 1), (1, 2): (7, 0)}[d, n]
            return ps[:, bank, half * GV:(half + 1) * GV]

        s_kt, s_kr, s_A, s_AT, s_U, s_st, s_O, s_oo = (
            sem(n) for n in ("kend_turned", "kend_rows", "products", "masked", "updates", "states", "out", "out_rows"))
        with nc.Block() as block:
            @block.tensor
            def _(pe):
                for g in range(4):
                    d, t = g // 2, g % 2
                    for h in range(GH):
                        i_ = nc.tensor.transpose(ps[:, g, h * P:(h + 1) * P],
                                                 k_end[:, d, h * S + t * P:h * S + (t + 1) * P], kit.c("ident"))
                    i_.then_inc(s_kt, 1)
                pe.wait_ge(s_kr, 4)

                def products(h):
                    if h >= 2:
                        pe.wait_ge(s_AT, h - 1)
                    for d in range(2):
                        for t in range(ST):
                            a = h * S + t * P
                            i_ = nc.tensor.matmul(ps[:, h % 2, d * S + t * P:d * S + (t + 1) * P],
                                                  lhsT=k_in[:, d, a:a + P], rhs=q_in[:, d, a:a + P], start=True,
                                                  stop=True)
                    i_.then_inc(s_A, 1)

                def updates(h):
                    if h >= 1:
                        pe.wait_ge(s_st, h)
                    for d in range(2):
                        for n in range(3):
                            c = n if d == 0 else NCH - 1 - n
                            t, pb = c // 2, CH * (c % 2)
                            i_ = nc.tensor.matmul(update(d, n),
                                                  lhsT=krow[pb:pb + CH, d, t, h * GK:(h + 1) * GK],
                                                  rhs=gv[pb:pb + CH, t, h * GV:(h + 1) * GV], start=True, stop=True)
                    i_.then_inc(s_U, 1)

                products(0)
                updates(0)
                for h in range(GH):
                    if h + 1 < GH:
                        products(h + 1)
                    pe.wait_ge(s_AT, h + 1)
                    pe.wait_ge(s_st, h + 1)
                    if h >= 2:
                        pe.wait_ge(s_oo, h - 1)
                    for t in range(ST):
                        o = ps[:, 5 + h % 2, t * GV:(t + 1) * GV]
                        i_ = nc.tensor.matmul(o, lhsT=AT[:, h % 2, t, :], rhs=gv[:, t, h * GV:(h + 1) * GV],
                                              start=True, stop=False, skip_group_check=True)
                        for c in range(2 * t, 2 * t + 2):
                            pb = CH * (c % 2)
                            for d, n in ((0, c - 1), (1, NCH - 2 - c)):
                                if n >= 0:
                                    i_ = nc.tensor.matmul(o[pb:pb + CH, :],
                                                          lhsT=q_in[:, d, h * S + c * CH:h * S + (c + 1) * CH],
                                                          rhs=states[:, d, n, :], start=False, stop=False,
                                                          skip_group_check=True)
                    i_.then_inc(s_O, 1)
                    if h + 1 < GH:
                        updates(h + 1)

            @block.vector
            def _(dve):
                for h in range(GH):
                    dve.wait_ge(s_A, h + 1)
                    if h >= 2:
                        dve.wait_ge(s_O, h - 1)
                    for d, mask in enumerate(("incl", "anti")):
                        kit.dve(nc.vector.tensor_tensor(
                            tmp[:, d, :].rearrange("p (t c) -> p t c", t=ST),
                            ps[:, h % 2, d * S:(d + 1) * S].rearrange("p (t c) -> p t c", t=ST),
                            kit.c(mask).unsqueeze(1).broadcast_to([P, ST, P]), ALU.mult))
                    nc.vector.tensor_tensor(flat(AT[:, h % 2, :, :]), tmp[:, 0, :], tmp[:, 1, :],
                                            ALU.add).then_inc(s_AT, 1)
                    dve.wait_ge(s_U, h + 1)
                    if h >= 1:
                        dve.wait_ge(s_O, h)
                    for n in range(3):
                        for d in range(2):
                            c = n if d == 0 else NCH - 1 - n
                            u = update(d, n)
                            if n == 0:
                                kit.dve(nc.vector.tensor_copy(states[:, d, 0, :], u))
                            else:
                                step = nc.vector.scalar_tensor_tensor(states[:, d, n, :], states[:, d, n - 1, :],
                                                                      dec[:, d, h * NCH + c:h * NCH + c + 1], u,
                                                                      ALU.mult, ALU.add)
                                if (n, d) == (2, 1):
                                    step.then_inc(s_st, 1)
                                else:
                                    kit.dve(step)

            @block.scalar
            def _(act):
                for g in range(4):
                    act.wait_ge(s_kt, g + 1)
                    nc.scalar.activation(krow[:, g // 2, g % 2, :], ps[:, g, :], ACT.Copy).then_inc(s_kr, 1)
                for h in range(GH):
                    act.wait_ge(s_O, h + 1)
                    nc.scalar.activation(orow[:, :, h * GV:(h + 1) * GV],
                                         ps[:, 5 + h % 2, :].rearrange("p (t v) -> p t v", t=ST), ACT.Copy
                                         ).then_inc(s_oo, 1)
        gated_norm(kit, "gla", orow, gr, GH, GV, outT, lambda k: kit.cols("gla_norm_w", k))


def gated_norm(kit, name, orow, gate, heads, width, outT, wcol):
    nc, ps = kit.nc, kit.ps
    tiles = heads * width // P
    n = heads * ST
    s_sq, s_mean, s_rms, s_silu, s_rows, s_turn, s_od, s_oa = (
        kit.sem(f"{name}_{x}") for x in ("sumsq", "mean", "rms", "silu", "normed", "turned", "out_dve", "out_act"))
    stat = kit.stat
    with nc.Block() as block:
        @block.scalar
        def _(act):
            for t in range(ST):
                for h in range(heads):
                    j = t * heads + h
                    kit.act(nc.scalar.activation(ps[:, 0, 0:width], orow[:, t, h * width:(h + 1) * width], ACT.Square,
                                                 accum_out=stat[:, 8 + j:9 + j]))
            nc.scalar.activation(stat[:, 32:33], stat[:, 8:9], ACT.Copy).then_inc(s_sq, 1)
            act.wait_ge(s_mean, 1)
            nc.scalar.activation(stat[:, 24:24 + n], stat[:, 16:16 + n], ACT.Sqrt).then_inc(s_rms, 1)
            nc.scalar.activation(gate[:, :, :], gate[:, :, :], ACT.Silu).then_inc(s_silu, 1)
            for k in range(1, tiles, 2):
                act.wait_ge(s_turn, k + 1)
                nc.scalar.activation(outT[:, k, :], ps[:, 4 + k % 4, 0:S], ACT.Identity,
                                     scale=wcol(k) if wcol else 1.0).then_inc(s_oa, 1)

        @block.vector
        def _(dve):
            dve.wait_ge(s_sq, 1)
            nc.vector.tensor_scalar(stat[:, 16:16 + n], stat[:, 8:8 + n], 1.0 / width, NORM_EPS, ALU.mult,
                                    ALU.add).then_inc(s_mean, 1)
            dve.wait_ge(s_rms, 1)
            kit.dve(nc.vector.reciprocal(stat[:, 8:8 + n], stat[:, 24:24 + n]))
            dve.wait_ge(s_silu, 1)
            for t in range(ST):
                for h in range(heads):
                    a, b = h * width, (h + 1) * width
                    j = 8 + t * heads + h
                    nc.vector.scalar_tensor_tensor(orow[:, t, a:b], orow[:, t, a:b], stat[:, j:j + 1],
                                                   gate[:, t, a:b], ALU.mult, ALU.mult).then_inc(s_rows, 1)
            for k in range(0, tiles, 2):
                dve.wait_ge(s_turn, k + 1)
                if wcol:
                    i_ = nc.vector.tensor_scalar(outT[:, k, :], ps[:, 4 + k % 4, 0:S], wcol(k), None, ALU.mult)
                else:
                    i_ = nc.vector.tensor_copy(outT[:, k, :], ps[:, 4 + k % 4, 0:S])
                i_.then_inc(s_od, 1)

        @block.tensor
        def _(pe):
            pe.wait_ge(s_rows, n)
            for k in range(tiles):
                if k >= 4:
                    pe.wait_ge(s_oa if k % 2 else s_od, (k - 4) // 2 + 1)
                for t in range(ST):
                    i_ = nc.tensor.transpose(ps[:, 4 + k % 4, t * P:(t + 1) * P], orow[:, t, k * P:(k + 1) * P],
                                             kit.c("ident"))
                i_.then_inc(s_turn, 1)


class Ada:

    def __init__(self, kit, ctx, name):
        self.kit = kit
        self.w = kit.sb(f"ada_w_{name}", [P, 2, 2, 2 * UN], ctx)
        self.acc = kit.sb(f"ada_acc_{name}", [P, 2 * UN], ctx)
        self.b = kit.sb(f"ada_b_{name}", [1, 2 * UN], ctx)

    def load(self, sp, lead, i, m, col):
        kit = self.kit
        a = 8 * lead + m
        if a >= 2:
            sp.wait_ge(kit.ada_acc, 2 * (a - 1) + 16 * i)
        w = kit.ins["w_ada_2"][0]
        sp.dma_start(self.w[:, m % 2, :, :], w[2 * m * P:2 * (m + 1) * P, ds(col, 2 * UN)]
                     .rearrange("(k p) n -> p k n", p=P)).then_inc(kit.ada_w[m % 2], 16)

    def load_bias(self, sp, lead, i, col):
        kit = self.kit
        if lead:
            sp.wait_ge(kit.ada_sum, lead + i)
        sp.dma_start(self.b[:, :], kit.ins["b_ada_2"][:, ds(col, 2 * UN)]).then_inc(kit.ada_b, 16)

    def product(self, dve, lead, i, s):
        nc, kit = self.kit.nc, self.kit
        m, k = s // 2, s % 2
        if s == 0 and lead:
            dve.wait_ge(kit.ada_sum, lead + i)
        if k == 0:
            dve.wait_ge(kit.ada_w[m % 2], 64 * lead + 64 * i + 16 * (m // 2 + 1))
        w, c = self.w[:, m % 2, k, :], kit.cols("c_2", s)
        if s:
            dve.wait_ge(kit.ada_acc, 16 * lead + s + 16 * i)
            step = nc.vector.scalar_tensor_tensor(self.acc[:, :], w, c, self.acc[:, :], ALU.mult, ALU.add)
        else:
            step = nc.vector.tensor_scalar(self.acc[:, :], w, c, None, ALU.mult)
        step.then_inc(kit.ada_acc, 1)

    def sums(self, pe, lead, i):
        nc, kit = self.kit.nc, self.kit
        pe.wait_ge(kit.ada_acc, 16 * lead + 16 * i)
        pe.wait_ge(kit.ada_b, 16 * lead + 16 * i)
        if lead > 1:
            pe.wait_ge(kit.ada_out, lead - 1 + i)
        ones = kit.c("ones")
        for q in range(8):
            nc.tensor.matmul(kit.ps[:, 6, q:q + 1], lhsT=self.acc[:, q * P:(q + 1) * P], rhs=ones[:, 0:1],
                             start=True, stop=False)
            step = nc.tensor.matmul(kit.ps[:, 6, q:q + 1], lhsT=self.b[:, q * P:(q + 1) * P], rhs=ones[0:1, 0:1],
                                    start=False, stop=True)
        step.then_inc(kit.ada_sum, 1)

    def copy(self, dve, lead, i, group):
        kit = self.kit
        dve.wait_ge(kit.ada_sum, lead + i)
        kit.nc.vector.tensor_copy(kit.modcols[:, ds(8 * group, 8)], kit.ps[:, 6, 0:8]).then_inc(kit.ada_out, 1)


def stage_glu(kit, ada, act_out, tmp, w_gate, w_up, head_next):
    nc = kit.nc
    first = kit.units
    uses = list(kit.pairs)
    turns = F1 // UN
    lead = kit.ada_groups
    with_ada = ADA_GROUPS - lead
    kit.ada_groups = ADA_GROUPS
    xbase = kit.x_splits
    kit.x_splits += 4
    s_glu = kit.sem("glu_out")
    outf = flat(act_out)

    def in_turns(eng, body):
        body(0, True, False, False)
        with eng.Fori(1, with_ada) as i:
            body(i, True, True, False)
        body(with_ada, False, True, False)
        with eng.Fori(with_ada + 1, turns - 1) as i:
            body(i, False, False, False)
        body(turns - 1, False, False, True)

    with nc.Block() as block:
        @block.sync
        def _(sp):
            def body(i, group, _, last):
                for m in range(8):
                    if group:
                        ada.load(sp, lead, i, m, 2 * UN * lead + 2 * UN * i)
                        if m == 2:
                            ada.load_bias(sp, lead, i, 2 * UN * lead + 2 * UN * i)
                    if m < 4:
                        load(kit, sp, first // 2 + 4 + m, i, block_src(w_up, m, UN * i))
                    elif not last:
                        load(kit, sp, first // 2 + 4 + m, i, block_src(w_gate, m - 4, UN * i + UN))
            in_turns(sp, body)
            head_next(sp, first // 2 + 8 * turns)

        @block.tensor
        def _(pe):
            def body(i, group, summed, last):
                mid = (lambda: ada.sums(pe, lead, i)) if summed else None
                multiply_block(kit, pe, "T", 0, first, i, uses[0], xbase, mid)
                multiply_block(kit, pe, "T", 1, first + 8, i, uses[1], xbase)
            in_turns(pe, body)

        @block.scalar
        def _(act):
            split_x_hi(kit, act)

            def body(i, *_):
                for u in range(8):
                    split_hi(kit, act, first + AHEAD + u, i)
                act.wait_ge(kit.weights_used, first + 8 + 16 * i)
                act.wait_ge(s_glu, 1 + i)
                nc.scalar.activation(tmp, flat(kit.ps[:, 0:2, :]), ACT.Silu).then_inc(kit.pair_free[0], 1)
                for u in range(8):
                    split_hi(kit, act, first + AHEAD + 8 + u, i)
            in_turns(act, body)

        @block.vector
        def _(dve):
            nc.vector.memset(kit.stat[:, 63:64], 0.0).then_inc(s_glu, 1)
            split_x_lo(kit, dve, xbase)

            def body(i, group, summed, last):
                for s in range(16):
                    split_lo(kit, dve, first + AHEAD + s, i)
                    if summed and s == 0:
                        ada.copy(dve, lead, i, lead - 1 + i)
                    if group:
                        ada.product(dve, lead, i, s)
                dve.wait_ge(kit.pair_free[0], uses[0] + 2 + i)
                dve.wait_ge(kit.weights_used, first + 16 + 16 * i)
                dve.wait_ge(kit.pair_free[1], uses[1] + 1 + i)
                nc.vector.tensor_tensor(outf[:, ds(4 * S * i, 4 * S)], tmp, flat(kit.ps[:, 2:4, :]),
                                        ALU.mult).then_inc(s_glu, 1)
                dve.wait_ge(s_glu, 2 + i)
                nc.vector.memset(kit.stat[:, 62:63], 0.0).then_inc(kit.pair_free[1], 1)
            in_turns(dve, body)
    kit.units = first + 16 * turns
    kit.pairs = [u + turns for u in uses]


def stage_add(kit, mixed, gate_row):
    nc = kit.nc
    with nc.Block() as block:
        @block.vector
        def _(dve):
            for t in range(ST):
                if gate_row is not None:
                    kit.dve(nc.vector.tensor_tensor(mixed[:, t, :], mixed[:, t, :], gate_row, ALU.mult))
                kit.dve(nc.vector.tensor_tensor(kit.x[:, t, :], kit.x[:, t, :], mixed[:, t, :], ALU.add))


def stage_modulation(kit, modcols):
    nc = kit.nc
    with nc.Block() as block:
        @block.vector
        def _(dve):
            for n, (scale, w) in enumerate(((KT, "norm_mix_2"), (4 * KT, "norm_ffn_2"))):
                a = COLS[w]
                kit.dve(nc.vector.scalar_tensor_tensor(kit.modT[:, KT * n:KT * (n + 1)], modcols[:, scale:scale + KT],
                                                       1.0, kit.col[:, a:a + KT], ALU.add, ALU.mult))


def stage_gate_row(kit, name, modcols, at, row):
    nc = kit.nc
    s_diag, s_row, s_out = kit.spread
    n0 = KT * kit.spreads
    kit.spreads += 1
    with ExitStack() as st:
        diag = kit.sb(f"{name}_diag", [P, KT, P], st)
        with nc.Block() as block:
            @block.vector
            def _(dve):
                for k in range(KT):
                    nc.vector.tensor_scalar(diag[:, k, :], kit.c("ident"), modcols[:, at(k):at(k) + 1], None,
                                            ALU.mult).then_inc(s_diag, 1)

            @block.tensor
            def _(pe):
                for k in range(KT):
                    pe.wait_ge(s_diag, n0 + k + 1)
                    nc.tensor.matmul(kit.ps[:, 4 + k // 4, (k % 4) * P:(k % 4 + 1) * P], lhsT=kit.c("ones"),
                                     rhs=diag[:, k, :], start=True, stop=True).then_inc(s_row, 1)

            @block.scalar
            def _(act):
                for q in range(4):
                    act.wait_ge(s_row, n0 + 4 * (q + 1))
                    nc.scalar.activation(row[:, q * UN:(q + 1) * UN], kit.ps[:, 4 + q, :], ACT.Copy
                                         ).then_inc(s_out, 1)


def stage_retention(kit, rqk, rvg, outT):
    nc, ps = kit.nc, kit.ps
    table_ready = kit.loads(1)
    s_S, s_PT, s_O, s_oo = (kit.sem("ret_" + n) for n in ("products", "decayed", "out", "rows"))
    with ExitStack() as st:
        decay = kit.sb("ret_decay", [P, RH, S], st)
        PT = kit.sb("ret_PT", [P, 2, 3 * P], st)
        orow = kit.sb("ret_rows", [P, ST, RH * RV], st)
        with nc.Block() as block:
            @block.sync
            def _(sp):
                sp.dma_start(flat(decay[:, :, :]), kit.const_src("retdecay")).then_inc(kit.loaded, 16)

            @block.tensor
            def _(pe):
                def products(h):
                    hb, tile, b = RK * (h % 2), h // 2, h % 2
                    if h >= 2:
                        pe.wait_ge(s_PT, h - 1)
                    for jt in range(ST):
                        a = jt * P
                        ins = nc.tensor.matmul(ps[:, b, jt * S:jt * S + S - a],
                                               lhsT=rqk[hb:hb + RK, 2 + tile, a:a + P],
                                               rhs=rqk[hb:hb + RK, tile, a:S], start=True, stop=True)
                    ins.then_inc(s_S, 1)

                products(0)
                for h in range(RH):
                    if h + 1 < RH:
                        products(h + 1)
                    pe.wait_ge(s_PT, h + 1)
                    if h >= 2:
                        pe.wait_ge(s_oo, h - 1)
                    v = lambda jt: rvg[:, jt, h * RV:(h + 1) * RV]
                    b = h % 2
                    nc.tensor.matmul(ps[:, 2 + b, 0:RV], lhsT=PT[:, b, 0:P], rhs=v(0), start=True, stop=True)
                    nc.tensor.matmul(ps[:, 2 + b, RV:2 * RV], lhsT=PT[:, b, P:2 * P], rhs=v(0), start=True,
                                     stop=False)
                    nc.tensor.matmul(ps[:, 2 + b, RV:2 * RV], lhsT=PT[:, b, 2 * P:3 * P], rhs=v(1), start=False,
                                     stop=True).then_inc(s_O, 1)

            @block.vector
            def _(dve):
                dve.wait_ge(kit.loaded, table_ready)
                for h in range(RH):
                    dve.wait_ge(s_S, h + 1)
                    if h >= 2:
                        dve.wait_ge(s_O, h - 1)
                    kit.dve(nc.vector.tensor_tensor(PT[:, h % 2, 0:S], ps[:, h % 2, 0:S], decay[:, h, :], ALU.mult))
                    nc.vector.tensor_tensor(PT[:, h % 2, S:S + P], ps[:, h % 2, S:S + P], decay[:, h, 0:P],
                                            ALU.mult).then_inc(s_PT, 1)

            @block.scalar
            def _(act):
                for h in range(RH):
                    act.wait_ge(s_O, h + 1)
                    nc.scalar.activation(orow[:, :, h * RV:(h + 1) * RV],
                                         ps[:, 2 + h % 2, 0:2 * RV].rearrange("p (t v) -> p t v", t=ST), ACT.Copy
                                         ).then_inc(s_oo, 1)
        gated_norm(kit, "ret", orow, rvg[:, :, RH * RV:], RH, RV, outT, None)


def stage_moba(kit, mqk, mv, outT):
    nc, ps = kit.nc, kit.ps
    (s_logits, s_biased, s_max, s_neg, s_exp, s_recip, s_p, s_turned, s_pT, s_out, s_done) = (
        kit.sem("moba_" + n) for n in ("logits", "biased", "max", "negmax", "exp", "recip", "probs",
                                       "turned", "probsT", "out", "stored"))
    table_ready = kit.loads(1)
    span = ((0, P), (P, P + S))
    with ExitStack() as st:
        dist = kit.sb("distance", [P, ST, S], st)
        L = kit.sb("moba_logits", [P, 2, 3 * P], st)
        E = kit.sb("moba_exp", [P, 2, 3 * P], st)
        ET = kit.sb("moba_probsT", [P, 2, 3 * P], st)
        sc = kit.sb("moba_sc", [P, 2, 4, ST], st)
        mx, neg, tot, rec = (sc[:, :, n, :] for n in range(4))
        with nc.Block() as block:
            @block.sync
            def _(sp):
                sp.dma_start(flat(dist[:, :, :]), kit.const_src("distance")).then_inc(kit.loaded, 16)

            @block.tensor
            def _(pe):
                def logits(h):
                    if h >= 2:
                        pe.wait_ge(s_biased, ST * (h - 1))
                    for t in range(ST):
                        a, b = span[t]
                        ins = nc.tensor.matmul(ps[:, h % 2, a:b], lhsT=mqk[:, h, t * P:(t + 1) * P],
                                               rhs=mqk[:, MH + h, 0:b - a], start=True, stop=True)
                    ins.then_inc(s_logits, 1)

                logits(0)
                for h in range(MH):
                    if h + 1 < MH:
                        logits(h + 1)
                    b = h % 2
                    pe.wait_ge(s_p, ST * (h + 1))
                    if h >= 2:
                        pe.wait_ge(s_pT, h - 1)
                    for n in range(3):
                        ins = nc.tensor.transpose(ps[:, 2 + b, n * P:(n + 1) * P], E[:, b, n * P:(n + 1) * P],
                                                  kit.c("ident"))
                    ins.then_inc(s_turned, 1)
                    pe.wait_ge(s_pT, h + 1)
                    if h >= 2:
                        pe.wait_ge(s_done, h - 1)
                    nc.tensor.matmul(ps[:, 4 + b, 0:S], lhsT=mv[:, 0, h * MD:(h + 1) * MD], rhs=ET[:, b, 0:S],
                                     start=True, stop=False)
                    nc.tensor.matmul(ps[:, 4 + b, P:S], lhsT=mv[:, 1, h * MD:(h + 1) * MD], rhs=ET[:, b, S:S + P],
                                     start=False, stop=True).then_inc(s_out, 1)

            @block.vector
            def _(dve):
                dve.wait_ge(kit.loaded, table_ready)
                for h in range(MH + 2):
                    if h < MH:
                        b = h % 2
                        slope = 2.0 ** (-8.0 * (h + 1) / MH)
                        dve.wait_ge(s_logits, h + 1)
                        if h >= 2:
                            dve.wait_ge(s_exp, ST * (h - 1))
                        for t in range(ST):
                            x, y = span[t]
                            nc.vector.scalar_tensor_tensor(L[:, b, x:y], dist[:, t, 0:y - x], -slope, ps[:, b, x:y],
                                                           ALU.mult, ALU.add).then_inc(s_biased, 1)
                        dve.wait_ge(s_biased, ST * (h + 1))
                        for t in range(ST):
                            x, y = span[t]
                            nc.vector.tensor_reduce(mx[:, b, t:t + 1], L[:, b, x:y], AX, ALU.max).then_inc(s_max, 1)
                        dve.wait_ge(s_max, ST * (h + 1))
                        nc.vector.tensor_scalar(neg[:, b, :], mx[:, b, :], -1.0, None, ALU.mult).then_inc(s_neg, 1)
                    if 1 <= h <= MH:
                        g = h - 1
                        b = g % 2
                        dve.wait_ge(s_exp, ST * (g + 1))
                        nc.vector.reciprocal(rec[:, b, :], tot[:, b, :]).then_inc(s_recip, 1)
                        dve.wait_ge(s_recip, g + 1)
                        for t in range(ST):
                            x, y = span[t]
                            nc.vector.tensor_scalar(E[:, b, x:y], E[:, b, x:y], rec[:, b, t:t + 1], None,
                                                    ALU.mult).then_inc(s_p, 1)
                    if h >= 2:
                        g = h - 2
                        dve.wait_ge(s_out, g + 1)
                        nc.vector.tensor_copy(outT[:, g, :], ps[:, 4 + g % 2, 0:S]).then_inc(s_done, 1)

            @block.scalar
            def _(act):
                for h in range(MH + 1):
                    if h < MH:
                        b = h % 2
                        act.wait_ge(s_neg, h + 1)
                        if h >= 2:
                            act.wait_ge(s_turned, h - 1)
                        for t in range(ST):
                            x, y = span[t]
                            nc.scalar.activation(E[:, b, x:y], L[:, b, x:y], ACT.Exp, bias=neg[:, b, t:t + 1],
                                                 accum_out=tot[:, b, t:t + 1]).then_inc(s_exp, 1)
                    if h >= 1:
                        g = h - 1
                        act.wait_ge(s_turned, g + 1)
                        if g >= 2:
                            act.wait_ge(s_out, g - 1)
                        nc.scalar.activation(ET[:, g % 2, :], ps[:, 2 + g % 2, 0:3 * P], ACT.Copy).then_inc(s_pT, 1)


def stage_rwkv(kit, rw, low, outT):
    nc, ps, ins = kit.nc, kit.ps, kit.ins
    NT = RWW // P
    W = NT * S
    sem = lambda n: kit.sem("rw_" + n)
    c3 = 3 * NT
    with ExitStack() as st:
        sb = lambda n, shape: kit.sb("rw_" + n, shape, st)
        kap, bet, kt, rt = (sb(n, [P, NT, S]) for n in ("kap", "bet", "kt", "rt"))
        bonus, gate = sb("bonus", [P, NT, S]), sb("gate", [P, NT, S])
        endG = sb("end_decay", [P, NT, NCH])
        gp = sb("gp", [P, NT, S])

        inner = ExitStack()
        new = kit.sb("rw_new", [P, c3, S], inner)
        lnew = kit.sb("rw_lnew", [P, 4, S], inner)
        wup = kit.sb("rw_wup", [DRANK, RWW], inner)
        aup = kit.sb("rw_aup", [ARANK, RWW], inner)
        gup = kit.sb("rw_gup", [P, 2, RWW], inner)
        t1, t2 = kit.sb("rw_t1", [P, NT, S], inner), kit.sb("rw_t2", [P, NT, S], inner)
        up_ready = kit.loads(3)
        s_shift, s_code, s_z, s_sw, s_sa = (
            sem(n) for n in ("shifted", "codes", "low_products", "decay_gate", "a_gate"))

        def bank_tile(m, base):
            return ps[:, base + m // 2, (m % 2) * S:(m % 2 + 1) * S]

        with nc.Block() as block:
            @block.sync
            def _(sp):
                sp.dma_start(wup[:, :], ins["rwkv_w_up_2"][0]).then_inc(kit.loaded, 16)
                sp.dma_start(aup[:, :], ins["rwkv_a_up_2"][0]).then_inc(kit.loaded, 16)
                sp.dma_start(gup[:, :, :], ins["rwkv_g_up_2"][0].rearrange("(k p) n -> p k n", p=P)
                             ).then_inc(kit.loaded, 16)

            @block.vector
            def _(dve):
                lows = ((DRANK, 0, 1), (ARANK, 1, 2), (P, 2, 4))
                for m, a, b in lows:
                    nc.vector.tensor_tensor(lnew[0:m, a:b, 1:S], low[0:m, a:b, 0:S - 1], low[0:m, a:b, 1:S],
                                            ALU.subtract)
                    kit.dve(nc.vector.tensor_scalar(lnew[0:m, a:b, 0:1], low[0:m, a:b, 0:1], -1.0, None, ALU.mult))
                for q, (m, name, k) in enumerate(((DRANK, "mu_wd", 0), (ARANK, "mu_wa", 0), (P, "mu_wg", 0),
                                                  (P, "mu_wg", 1))):
                    nc.vector.scalar_tensor_tensor(lnew[0:m, q, :], lnew[0:m, q, :], kit.cols(name, k)[0:m, :],
                                                   low[0:m, q, :], ALU.mult, ALU.add).then_inc(s_shift, 1)
                nc.vector.tensor_tensor(new[:, :, 1:S], rw[:, :, 0:S - 1], rw[:, :, 1:S], ALU.subtract)
                kit.dve(nc.vector.tensor_scalar(new[:, :, 0:1], rw[:, :, 0:1], -1.0, None, ALU.mult))
                for q in range(c3):
                    kit.dve(nc.vector.scalar_tensor_tensor(new[:, q, :], new[:, q, :], kit.cols("mu_rkv", q),
                                                           rw[:, q, :], ALU.mult, ALU.add))

            @block.scalar
            def _(act):
                act.wait_ge(s_shift, 4)
                nc.scalar.activation(lnew[0:DRANK, 0, :], lnew[0:DRANK, 0, :], ACT.Tanh).then_inc(s_code, 1)
                nc.scalar.activation(lnew[:, 2:4, :], lnew[:, 2:4, :], ACT.Sigmoid).then_inc(s_code, 1)
                act.wait_ge(s_z, 1)
                for m in range(NT):
                    nc.scalar.activation(t1[:, m, :], bank_tile(m, 0), ACT.Sigmoid, bias=kit.cols("rwkv_w0_2", m)
                                         ).then_inc(s_sw, 1)
                act.wait_ge(s_z, 2)
                for m in range(NT):
                    nc.scalar.activation(t2[:, m, :], bank_tile(m, 2), ACT.Sigmoid, bias=kit.cols("rwkv_a0_2", m)
                                         ).then_inc(s_sa, 1)
                act.wait_ge(s_z, 3)
                kit.act(nc.scalar.activation(flat(gate[:, :, :]), flat(ps[:, 4:6, :]), ACT.Copy))

            @block.tensor
            def _(pe):
                pe.wait_ge(kit.loaded, up_ready)
                pe.wait_ge(s_code, 2)
                for base, w, r, q in ((0, wup, DRANK, 0), (2, aup, ARANK, 1)):
                    for m in range(NT):
                        i_ = nc.tensor.matmul(bank_tile(m, base), lhsT=w[:, m * P:(m + 1) * P], rhs=lnew[0:r, q, :],
                                              start=True, stop=True)
                    i_.then_inc(s_z, 1)
                for m in range(NT):
                    for k in range(2):
                        i_ = nc.tensor.matmul(bank_tile(m, 4), lhsT=gup[:, k, m * P:(m + 1) * P],
                                              rhs=lnew[:, 2 + k, :], start=(k == 0), stop=(k == 1))
                i_.then_inc(s_z, 1)

        r, k, v = (new[:, n * NT:(n + 1) * NT, :] for n in range(3))
        G = bonus
        s_G, s_Gm, s_eG, s_enG, s_eGm, s_sq, s_ss, s_max, s_nrm, s_rkk, s_sum = (
            sem(n) for n in ("G", "G_before", "exp_G", "exp_minus_G", "exp_G_before", "kk_sq", "kk_sumsq", "kk_max",
                             "kk_norm", "rk_products", "rk_sums"))
        two = lambda ap: ap.rearrange("p (b a) s -> p b (a s)", b=2)
        with nc.Block() as block:
            @block.vector
            def _(dve):
                kit.dve(nc.vector.tensor_scalar(flat(t1[:, :, :]), flat(t1[:, :, :]), -math.exp(-0.5), None, ALU.mult))
                nc.vector.tensor_tensor_scan(flat(G[:, :, :]), kit.c("carry"), flat(t1[:, :, :]), 0.0, ALU.mult, ALU.add
                                             ).then_inc(s_G, 1)
                dve.wait_ge(s_G, 1)
                dve.wait_ge(s_enG, 1)
                nc.vector.tensor_tensor(flat(t1[:, :, :]), flat(G[:, :, :]), flat(t1[:, :, :]), ALU.subtract).then_inc(s_Gm, 1)
                for m in range(NT):
                    kit.dve(nc.vector.tensor_scalar(kap[:, m, :], k[:, m, :], kit.cols("rwkv_k_k_2", m), None,
                                                    ALU.mult))
                nc.vector.tensor_tensor(flat(bet[:, :, :]), flat(kap[:, :, :]), flat(kap[:, :, :]), ALU.mult).then_inc(s_sq, 1)
                dve.wait_ge(s_ss, 1)
                nc.vector.tensor_scalar(two(bet[:, :, :]), ps[:, 0:2, :], 1e-24, None, ALU.max).then_inc(s_max, 1)
                for m in range(NT):
                    kit.dve(nc.vector.tensor_scalar(gp[:, m, :], t2[:, m, :], -1.0, kit.cols("rwkv_k_a_2", m),
                                                    ALU.add, ALU.mult))
                kit.dve(nc.vector.scalar_tensor_tensor(flat(k), flat(gp[:, :, :]), 1.0, flat(k), ALU.add, ALU.mult))
                dve.wait_ge(s_nrm, 1)
                kit.dve(nc.vector.reciprocal(flat(bet[:, :, :]), flat(bet[:, :, :])))
                kit.dve(nc.vector.tensor_tensor(flat(kap[:, :, :]), flat(kap[:, :, :]), flat(bet[:, :, :]), ALU.mult))
                kit.dve(nc.vector.tensor_tensor(flat(gp[:, :, :]), flat(r), flat(k), ALU.mult))
                for m in range(NT):
                    nc.vector.tensor_scalar(gp[:, m, :], gp[:, m, :], kit.cols("rwkv_r_k_2", m), None,
                                            ALU.mult).then_inc(s_rkk, 1)
                dve.wait_ge(s_enG, 1)
                kit.dve(nc.vector.tensor_tensor(flat(bet[:, :, :]), flat(kap[:, :, :]), flat(t2[:, :, :]), ALU.mult))
                kit.dve(nc.vector.tensor_tensor(flat(bet[:, :, :]), flat(bet[:, :, :]), flat(kt[:, :, :]), ALU.mult))
                kit.dve(nc.vector.tensor_tensor(flat(kt[:, :, :]), flat(k), flat(kt[:, :, :]), ALU.mult))
                dve.wait_ge(s_eG, 1)
                kit.dve(nc.vector.tensor_copy(endG[:, :, :], rt[:, :, :].rearrange("p m (c s) -> p m c s", s=CH)
                                              [:, :, :, CH - 1]))
                kit.dve(nc.vector.tensor_tensor(flat(rt[:, :, :]), flat(r), flat(rt[:, :, :]), ALU.mult))
                dve.wait_ge(s_eGm, 1)
                kit.dve(nc.vector.tensor_tensor(flat(kap[:, :, :]), flat(kap[:, :, :]), flat(t1[:, :, :]), ALU.mult))
                dve.wait_ge(s_sum, 1)
                kit.dve(nc.vector.tensor_tensor(two(bonus[:, :, :]), ps[:, 2:4, :], two(v), ALU.mult))

            @block.scalar
            def _(act):
                act.wait_ge(s_G, 1)
                nc.scalar.activation(flat(rt[:, :, :]), flat(G[:, :, :]), ACT.Exp).then_inc(s_eG, 1)
                nc.scalar.activation(flat(kt[:, :, :]), flat(G[:, :, :]), ACT.Exp, scale=-1.0).then_inc(s_enG, 1)
                act.wait_ge(s_Gm, 1)
                nc.scalar.activation(flat(t1[:, :, :]), flat(t1[:, :, :]), ACT.Exp).then_inc(s_eGm, 1)
                act.wait_ge(s_max, 1)
                nc.scalar.activation(flat(bet[:, :, :]), flat(bet[:, :, :]), ACT.Sqrt).then_inc(s_nrm, 1)

            @block.tensor
            def _(pe):
                for need, count, src, base, done in ((s_sq, 1, bet, 0, s_ss), (s_rkk, NT, gp, 2, s_sum)):
                    pe.wait_ge(need, count)
                    for b in range(2):
                        i_ = nc.tensor.matmul(ps[:, base + b, :], lhsT=kit.c("headsum"),
                                              rhs=two(src[:, :, :])[:, b, :], start=True, stop=True)
                    i_.then_inc(done, 1)

        srcs = (kap, bet, kt, v)
        kap_r, bet_r, kt_r, v_r = (rw[:, n * NT:(n + 1) * NT, :] if n < 3 else gp for n in range(4))
        kap_r, bet_r, kt_r, v_r = (x.rearrange("p m s -> p (m s)").rearrange("p (t f) -> p t f", t=ST)
                                   for x in (kap_r, bet_r, kt_r, v_r[:, :, :]))
        dsts = (kap_r, bet_r, kt_r, v_r)
        s_tr, s_rows = sem("turned"), sem("rows")
        with nc.Block() as block:
            @block.tensor
            def _(pe):
                for n in range(8):
                    src, t = srcs[n // 2], n % 2
                    for m in range(NT):
                        i_ = nc.tensor.transpose(ps[:, n, m * P:(m + 1) * P], src[:, m, t * P:(t + 1) * P],
                                                 kit.c("ident"))
                    i_.then_inc(s_tr, 1)

            @block.scalar
            def _(act):
                for n in range(8):
                    act.wait_ge(s_tr, n + 1)
                    nc.scalar.activation(dsts[n // 2][:, n % 2, :], ps[:, n, :], ACT.Copy).then_inc(s_rows, 1)
        inner.close()

        RB, RKm = sb("RB_T", [P, ST, 2, 4 * P]), sb("RK_T", [P, ST, 2, 4 * P])
        KxT = sb("Kx_T", [P, NT, S])
        Z = sb("Z", [P, ST, RWW])
        solve = ExitStack()
        AT, X, XT, BT, P1, Off = (kit.sb("rw_" + n, [P, 2, 4 * P], solve) for n in ("A_T", "X", "X_T", "B_T", "P1",
                                                                                    "off"))
        bv = Off[:, 0, :]
        blocks = [2 ** n for n in range(1, int(math.log2(CH)))]
        s_pr, s_ev, s_off, s_p1, s_p1c, s_m, s_x, s_bv, s_bvc, s_zk, s_zkc = (
            sem(n) for n in ("products", "masked", "between", "offX", "offX_copied", "XoffX", "X_updated", "BV",
                             "BV_copied", "Z_Kx", "Z_Kx_copied"))
        heads4 = lambda ap: ap.rearrange("p (h c) -> p h c", h=4)
        mask4 = lambda name: kit.c(name).unsqueeze(1).broadcast_to([P, 4, P])
        for t in range(ST):
            a = t * P
            NL = len(blocks)
            with nc.Block() as block:
                @block.tensor
                def _(pe):
                    n = 0
                    for lhs, rhs in ((bet, kap), (kap, bet), (kt, kap), (bet, rt), (kt, rt)):
                        for par in range(2):
                            hb = RWN * par
                            if n >= 8:
                                pe.wait_ge(s_ev, 10 * t + n - 7)
                            for m in range(NT):
                                i_ = nc.tensor.matmul(ps[:, n % 8, m * P:(m + 1) * P],
                                                      lhsT=lhs[hb:hb + RWN, m, a:a + P],
                                                      rhs=rhs[hb:hb + RWN, m, a:a + P], start=True, stop=True)
                            i_.then_inc(s_pr, 1)
                            n += 1
                    pe.wait_ge(s_ev, 10 * (t + 1))
                    for l in range(NL):
                        for g in range(2):
                            lv = 2 * (t * NL + l) + g
                            pe.wait_ge(s_off, lv + 1)
                            pe.wait_ge(s_x, lv - 1) if lv >= 2 else None
                            for m in range(4):
                                q = slice(m * P, (m + 1) * P)
                                i_ = nc.tensor.matmul(ps[:, g, q], lhsT=Off[:, g, q], rhs=X[:, g, q], start=True,
                                                      stop=True)
                            i_.then_inc(s_p1, 1)
                        for g in range(2):
                            lv = 2 * (t * NL + l) + g
                            pe.wait_ge(s_p1c, lv + 1)
                            for m in range(4):
                                q = slice(m * P, (m + 1) * P)
                                nc.tensor.matmul(ps[:, 2 + 2 * g, q], lhsT=XT[:, g, q], rhs=P1[:, g, q], start=True,
                                                 stop=True)
                            for m in range(4):
                                q = slice(m * P, (m + 1) * P)
                                i_ = nc.tensor.matmul(ps[:, 3 + 2 * g, q], lhsT=P1[:, g, q], rhs=XT[:, g, q],
                                                      start=True, stop=True)
                            i_.then_inc(s_m, 1)
                    pe.wait_ge(s_x, 2 * NL * (t + 1))
                    for h in range(RWH):
                        q = slice((h // 2) * P, (h // 2 + 1) * P)
                        f = slice(h * RWN, (h + 1) * RWN)
                        i_ = nc.tensor.matmul(ps[:, 6, f], lhsT=BT[:, h % 2, q], rhs=v_r[:, t, f], start=True,
                                              stop=True)
                    i_.then_inc(s_bv, 1)
                    for h in range(RWH):
                        q = slice((h // 2) * P, (h // 2 + 1) * P)
                        f = slice(h * RWN, (h + 1) * RWN)
                        hb = RWN * (h % 2)
                        i_ = nc.tensor.matmul(ps[hb:hb + RWN, 7, q], lhsT=kap_r[:, t, f], rhs=XT[:, h % 2, q],
                                              start=True, stop=True)
                    i_.then_inc(s_zk, 1)
                    pe.wait_ge(s_bvc, t + 1)
                    for h in range(RWH):
                        q = slice((h // 2) * P, (h // 2 + 1) * P)
                        f = slice(h * RWN, (h + 1) * RWN)
                        i_ = nc.tensor.matmul(ps[:, 0, f], lhsT=XT[:, h % 2, q], rhs=bv[:, f], start=True, stop=True)
                    i_.then_inc(s_zk, 1)

                @block.vector
                def _(dve):
                    n = 0
                    for kind in range(5):
                        for par in range(2):
                            dve.wait_ge(s_pr, 10 * t + n + 1)
                            src = ps[:, n % 8, :]
                            if kind == 0:
                                kit.dve(nc.vector.tensor_copy(AT[:, par, :], src))
                                kit.dve(nc.vector.tensor_tensor(heads4(XT[:, par, :]), heads4(AT[:, par, :]),
                                                                mask4("lvlT1"), ALU.mult))
                                i_ = nc.vector.tensor_tensor(heads4(XT[:, par, :]), mask4("ident"),
                                                             heads4(XT[:, par, :]), ALU.subtract)
                            elif kind == 1:
                                kit.dve(nc.vector.tensor_tensor(heads4(X[:, par, :]), heads4(src), mask4("lvl1"),
                                                                ALU.mult))
                                i_ = nc.vector.tensor_tensor(heads4(X[:, par, :]), mask4("ident"),
                                                             heads4(X[:, par, :]), ALU.subtract)
                            else:
                                dst, mask = {2: (BT[:, par, :], "strict"), 3: (RB[:, t, par, :], "incl"),
                                             4: (RKm[:, t, par, :], "incl")}[kind]
                                i_ = nc.vector.tensor_tensor(heads4(dst), heads4(src), mask4(mask), ALU.mult)
                            i_.then_inc(s_ev, 1)
                            n += 1
                    dve.wait_ge(s_ev, 10 * (t + 1))
                    for l, b in enumerate(blocks):
                        for g in range(2):
                            lv = 2 * (t * NL + l) + g
                            if lv >= 2:
                                dve.wait_ge(s_p1, lv - 1)
                            nc.vector.tensor_tensor(heads4(Off[:, g, :]), heads4(AT[:, g, :]), mask4(f"lvlT{b}"),
                                                    ALU.mult).then_inc(s_off, 1)
                        for g in range(2):
                            lv = 2 * (t * NL + l) + g
                            dve.wait_ge(s_m, lv + 1)
                            if l < NL - 1:
                                nc.vector.tensor_tensor(X[:, g, :], X[:, g, :], ps[:, 2 + 2 * g, :], ALU.subtract)
                            nc.vector.tensor_tensor(XT[:, g, :], XT[:, g, :], ps[:, 3 + 2 * g, :],
                                                    ALU.subtract).then_inc(s_x, 1)

                @block.scalar
                def _(act):
                    for l in range(NL):
                        for g in range(2):
                            lv = 2 * (t * NL + l) + g
                            act.wait_ge(s_p1, lv + 1)
                            nc.scalar.activation(P1[:, g, :], ps[:, g, :], ACT.Copy).then_inc(s_p1c, 1)
                    act.wait_ge(s_bv, t + 1)
                    nc.scalar.activation(bv, ps[:, 6, :], ACT.Copy).then_inc(s_bvc, 1)
                    act.wait_ge(s_zk, 2 * t + 1)
                    nc.scalar.activation(KxT[:, :, a:a + P], heads4(ps[:, 7, :]), ACT.Copy).then_inc(s_zkc, 1)
                    act.wait_ge(s_zk, 2 * t + 2)
                    nc.scalar.activation(Z[:, t, :], ps[:, 0, :], ACT.Copy).then_inc(s_zkc, 1)
        solve.close()

        U, M, YT = sb("U", [P, ST, RWW]), sb("M", [P, NT, RWN]), sb("Y_T", [P, NT, S])
        s_pu, s_u, s_y2, s_y1, s_pm, s_M, s_y2c, s_y = (
            sem(n) for n in ("U_products", "U", "Y_chunk", "Y_state", "M_products", "M", "Y_copied", "Y"))
        pairs = lambda ap: ap.rearrange("p (m two n) -> p m two n", two=2, n=RWN)
        with nc.Block() as block:
            @block.tensor
            def _(pe):
                for c in range(NCH):
                    t, pb, b = c // 2, CH * (c % 2), c % 2
                    rows_ = slice(pb, pb + CH)
                    cs = slice(c * CH, (c + 1) * CH)
                    if c:
                        pe.wait_ge(s_M, c)
                        for h in range(RWH):
                            hb, m = RWN * (h % 2), h // 2
                            i_ = nc.tensor.matmul(ps[rows_, h % 2, m * RWN:(m + 1) * RWN],
                                                  lhsT=KxT[hb:hb + RWN, m, cs], rhs=M[hb:hb + RWN, m, :],
                                                  start=True, stop=True)
                        i_.then_inc(s_pu, 1)
                        if c >= 3:
                            pe.wait_ge(s_y, c - 2)
                        for h in range(RWH):
                            hb, m = RWN * (h % 2), h // 2
                            i_ = nc.tensor.matmul(ps[hb:hb + RWN, 4 + b, m * CH:(m + 1) * CH],
                                                  lhsT=M[hb:hb + RWN, m, :], rhs=rt[hb:hb + RWN, m, cs],
                                                  start=True, stop=True)
                        i_.then_inc(s_y1, 1)
                    pe.wait_ge(s_u, c + 1)
                    for h in range(RWH):
                        hb, m = RWN * (h % 2), h // 2
                        f = slice(h * RWN, (h + 1) * RWN)
                        o = ps[hb:hb + RWN, 6 + b, m * RWN:(m + 1) * RWN]
                        nc.tensor.matmul(o, lhsT=bet_r[rows_, t, f], rhs=U[rows_, t, f], start=True, stop=False)
                        i_ = nc.tensor.matmul(o, lhsT=kt_r[rows_, t, f], rhs=v_r[rows_, t, f], start=False,
                                              stop=True)
                    i_.then_inc(s_pm, 1)
                    if c >= 2:
                        pe.wait_ge(s_y2c, c - 1)
                    for h in range(RWH):
                        hb, m = RWN * (h % 2), h // 2
                        f = slice(h * RWN, (h + 1) * RWN)
                        q = slice(m * P + pb, m * P + pb + CH)
                        o = ps[hb:hb + RWN, 2 + b, m * CH:(m + 1) * CH]
                        nc.tensor.matmul(o, lhsT=U[rows_, t, f], rhs=RB[rows_, t, h % 2, q], start=True, stop=False)
                        i_ = nc.tensor.matmul(o, lhsT=v_r[rows_, t, f], rhs=RKm[rows_, t, h % 2, q], start=False,
                                              stop=True)
                    i_.then_inc(s_y2, 1)

            @block.vector
            def _(dve):
                for c in range(NCH):
                    t, pb, b = c // 2, CH * (c % 2), c % 2
                    rows_ = slice(pb, pb + CH)
                    if c == 0:
                        nc.vector.tensor_scalar(U[rows_, t, :], Z[rows_, t, :], -1.0, None, ALU.mult
                                                ).then_inc(s_u, 1)
                    else:
                        dve.wait_ge(s_pu, c)
                        kit.dve(nc.vector.scalar_tensor_tensor(
                            pairs(U[rows_, t, :])[:, :, 0, :], ps[rows_, 0, 0:NT * RWN].rearrange(
                                "p (m n) -> p m n", m=NT), -1.0, pairs(Z[rows_, t, :])[:, :, 0, :], ALU.mult,
                            ALU.subtract))
                        nc.vector.scalar_tensor_tensor(
                            pairs(U[rows_, t, :])[:, :, 1, :], ps[rows_, 1, 0:NT * RWN].rearrange(
                                "p (m n) -> p m n", m=NT), -1.0, pairs(Z[rows_, t, :])[:, :, 1, :], ALU.mult,
                            ALU.subtract).then_inc(s_u, 1)
                    dve.wait_ge(s_pm, c + 1)
                    pm = ps[:, 6 + b, 0:NT * RWN]
                    if c < NCH - 1:
                        if c == 0:
                            kit.dve(nc.vector.tensor_copy(flat(M[:, :, :]), pm))
                        else:
                            dve.wait_ge(s_y1, c)
                            kit.dve(nc.vector.tensor_tensor(flat(M[:, :, :]), flat(M[:, :, :]), pm, ALU.add))
                        nc.vector.tensor_tensor(M[:, :, :], M[:, :, :],
                                                endG[:, :, c:c + 1].broadcast_to([P, NT, RWN]), ALU.mult
                                                ).then_inc(s_M, 1)
                    if c:
                        dve.wait_ge(s_y1, c)
                        dve.wait_ge(s_y2c, c + 1)
                        y = YT[:, :, c * CH:(c + 1) * CH]
                        nc.vector.tensor_tensor(y, ps[:, 4 + b, 0:NT * CH].rearrange("p (m s) -> p m s", m=NT), y,
                                                ALU.add).then_inc(s_y, 1)

            @block.scalar
            def _(act):
                for c in range(NCH):
                    act.wait_ge(s_y2, c + 1)
                    nc.scalar.activation(YT[:, :, c * CH:(c + 1) * CH],
                                         ps[:, 2 + c % 2, 0:NT * CH].rearrange("p (m s) -> p m s", m=NT), ACT.Copy
                                         ).then_inc(s_y2c, 1)

        sq = sb("y_sq", [P, NT, S])
        s_mean, s_c, s_var, s_ve, s_sd = (sem(n) for n in ("y_mean", "y_squares", "y_var", "y_var_eps", "y_sd"))
        with nc.Block() as block:
            @block.tensor
            def _(pe):
                for b in range(2):
                    i_ = nc.tensor.matmul(ps[:, b, :], lhsT=kit.c("headsum"), rhs=two(YT[:, :, :])[:, b, :],
                                          start=True, stop=True)
                i_.then_inc(s_mean, 1)
                pe.wait_ge(s_c, 1)
                for b in range(2):
                    i_ = nc.tensor.matmul(ps[:, 2 + b, :], lhsT=kit.c("headsum"), rhs=two(sq[:, :, :])[:, b, :],
                                          start=True, stop=True)
                i_.then_inc(s_var, 1)

            @block.vector
            def _(dve):
                dve.wait_ge(s_mean, 1)
                kit.dve(nc.vector.scalar_tensor_tensor(two(YT[:, :, :]), ps[:, 0:2, :], -1.0 / RWN, two(YT[:, :, :]),
                                                       ALU.mult, ALU.add))
                nc.vector.tensor_tensor(flat(sq[:, :, :]), flat(YT[:, :, :]), flat(YT[:, :, :]), ALU.mult).then_inc(s_c, 1)
                dve.wait_ge(s_var, 1)
                nc.vector.tensor_scalar(two(sq[:, :, :]), ps[:, 2:4, :], 1.0 / RWN, GN_EPS, ALU.mult,
                                        ALU.add).then_inc(s_ve, 1)
                dve.wait_ge(s_sd, 1)
                kit.dve(nc.vector.reciprocal(flat(sq[:, :, :]), flat(sq[:, :, :])))
                kit.dve(nc.vector.tensor_tensor(flat(YT[:, :, :]), flat(YT[:, :, :]), flat(sq[:, :, :]), ALU.mult))
                for m in range(NT):
                    kit.dve(nc.vector.tensor_scalar(YT[:, m, :], YT[:, m, :], kit.cols("rwkv_ln_w_2", m),
                                                    kit.cols("rwkv_ln_b_2", m), ALU.mult, ALU.add))
                kit.dve(nc.vector.tensor_tensor(flat(YT[:, :, :]), flat(YT[:, :, :]), flat(bonus[:, :, :]), ALU.add))
                kit.dve(nc.vector.tensor_tensor(flat(outT), flat(YT[:, :, :]), flat(gate[:, :, :]), ALU.mult))

            @block.scalar
            def _(act):
                act.wait_ge(s_ve, 1)
                nc.scalar.activation(flat(sq[:, :, :]), flat(sq[:, :, :]), ACT.Sqrt).then_inc(s_sd, 1)


def stage_conv_glu(kit, w, act_out, head_next):
    nc, ps = kit.nc, kit.ps
    first = kit.units
    uses = list(kit.pairs)
    xbase = kit.x_splits
    kit.x_splits += 4
    turns = F2 // UN
    FT = F2 // P
    s_taps, s_base, s_conv, s_silu, s_glu = (kit.sem("conv_" + n) for n in ("taps", "base", "sums", "silu", "glu"))
    c0 = COLS["conv_w0"]
    taps_all = kit.col[:, c0:c0 + 4 * 2 * FT].rearrange("p (j f) -> p j f", j=4)
    outf = flat(act_out)
    per = 2 * 4 * 2
    col0 = (F2, 0)
    with ExitStack() as st:
        y = kit.sb("conv_y", [P, 2, 4, S], st)
        taps = kit.sb("conv_taps", [P, 2, 4, 4], st)
        tile = lambda j, q: ps[:, 2 * j + q // 2, (q % 2) * S:(q % 2 + 1) * S]

        with nc.Block() as block:
            @block.sync
            def _(sp):
                def body(i):
                    load_block(kit, sp, first // 2 + 4, i, w, col0[1] + UN * i)
                    load_block(kit, sp, first // 2 + 8, i, w, col0[0] + UN + UN * i)
                run_turns(sp, 0, turns - 1, body)
                load_block(kit, sp, first // 2 + 4, turns - 1, w, col0[1] + UN * (turns - 1))
                head_next(sp, first // 2 + 8 * turns)

            @block.tensor
            def _(pe):
                def body(i):
                    for j in range(2):
                        multiply_block(kit, pe, "T", j, first + 8 * j, i, uses[j], xbase)
                run_turns(pe, 0, turns, body)

            @block.scalar
            def _(act):
                split_x_hi(kit, act)

                def body(i):
                    for j in range(2):
                        for u in range(8):
                            split_hi(kit, act, first + AHEAD + 8 * j + u, i)
                            if (j, u) == (1, 3):
                                act.wait_ge(kit.pair_free[0], uses[0] + 2 + i)
                                nc.scalar.activation(flat(y[:, 0, :, :]), flat(y[:, 0, :, :]), ACT.Silu
                                                     ).then_inc(s_silu, 1)
                        act.wait_ge(s_taps, 2 + 2 * i)
                        act.wait_ge(kit.weights_used, first + 8 * (j + 1) + 16 * i)
                        act.wait_ge(s_glu, 1 + i)
                        for q in range(4):
                            nc.scalar.activation(y[:, j, q, :], tile(j, q), ACT.Identity, scale=taps[:, j, 2, q:q + 1],
                                                 bias=taps[:, j, 3, q:q + 1]).then_inc(s_base, 1)
                run_turns(act, 0, turns, body)

            @block.vector
            def _(dve):
                nc.vector.memset(kit.stat[:, 63:64], 0.0).then_inc(s_glu, 1)
                split_x_lo(kit, dve, xbase)

                def body(i):
                    dve.wait_ge(s_glu, 1 + i)
                    for j in range(2):
                        nc.vector.tensor_copy(taps[:, j, :, :], taps_all[:, :, ds((FT, 0)[j] + 4 * i, 4)]
                                              ).then_inc(s_taps, 1)
                    dve.wait_ge(s_taps, 2 + 2 * i)
                    for j in range(2):
                        for u in range(8):
                            split_lo(kit, dve, first + AHEAD + 8 * j + u, i)
                        for tap in (1, 0):
                            for q in range(4):
                                dve.wait_ge(s_base, 8 * i + 4 * j + 2 * (q // 2) + 2)
                                if tap == 0:
                                    dve.wait_ge(s_conv, per * i + 8 * j + q + 1)
                                b = 2 - tap
                                nc.vector.scalar_tensor_tensor(y[:, j, q, b:S], tile(j, q)[:, 0:S - b],
                                                               taps[:, j, tap, q:q + 1], y[:, j, q, b:S], ALU.mult,
                                                               ALU.add).then_inc(s_conv, 1)
                        dve.wait_ge(s_conv, per * i + 8 * (j + 1))
                        nc.vector.memset(kit.stat[:, 62:63], 0.0).then_inc(kit.pair_free[j], 1)
                    dve.wait_ge(s_silu, 1 + i)
                    nc.vector.tensor_tensor(outf[:, ds(4 * S * i, 4 * S)], flat(y[:, 0, :, :]), flat(y[:, 1, :, :]),
                                            ALU.mult).then_inc(s_glu, 1)
                run_turns(dve, 0, turns, body)
    kit.units = first + 16 * turns
    kit.pairs = [u + turns for u in uses]


def program(nc, ins, at, out):
    with ExitStack() as ctx:
        kit = Kit(nc, ctx, ins, at)
        kit.turns = 0
        mem = {"bias_dram": nc.dram_tensor("bias_rows", (AH, 2 * S), F32, kind="Internal")}

        w_in = ins["w_in"][0]
        q0, k0, v0, gq0, gv0, gr0, lr0 = 0, AW, 2 * AW, 3 * AW, 3 * AW + 2 * GH * GK, 3 * AW + 2 * GH * GK + GH * GV, \
            3 * AW + 2 * GH * GK + 2 * GH * GV
        stage_setup(kit, mem, lambda sp: load_block(kit, sp, 0, 0, w_in, q0))
        norm_steps(kit, kit.x, None, True, lambda k: kit.cols("attn_norm_w", k), None, None)
        mix = ctx.enter_context(ExitStack())
        gqk = kit.sb("gqk_T", [P, 2 * GH, S], mix)
        gv = kit.sb("gv_rows", [P, ST, GH * GV], mix)
        gr = kit.sb("gr_rows", [P, ST, GH * GV], mix)
        glr = kit.sb("glr_T", [GRANK, 2, S], mix)
        att = ctx.enter_context(ExitStack())
        qkT = kit.sb("qk_T", [P, 2 * AW // P, S], att)
        v = kit.sb("v_rows", [P, ST, AW], att)
        wlr = kit.sb("w_lr", [P, KT, 2 * GRANK], att)
        lr_ready = kit.loads(1)
        s_lr = kit.sem("lowrank_codes")

        def lr_sync(sp):
            sp.dma_start(wlr[:, :, :], w_in[:, lr0:lr0 + 2 * GRANK].rearrange("(k p) n -> p k n", p=P)
                         ).then_inc(kit.loaded, 16)

        def lr_pe(pe):
            pe.wait_ge(kit.loaded, lr_ready)
            for d in range(2):
                for k in range(KT):
                    ins_ = nc.tensor.matmul(kit.ps[0:GRANK, 5 + 2 * d, 0:S], lhsT=wlr[:, k, d * GRANK:(d + 1) * GRANK],
                                            rhs=kit.hT[:, k, :], start=(k == 0), stop=(k == KT - 1))
                ins_.then_inc(s_lr, 1)

        def lr_act(act):
            for d in range(2):
                act.wait_ge(s_lr, d + 1)
                kit.act(nc.scalar.activation(glr[:, d, :], kit.ps[0:GRANK, 5 + 2 * d, 0:S], ACT.Copy))

        qk_flat = flat(qkT[:, :, :])
        gqk_flat = flat(gqk[:, :, :])

        def at_T(t, base):
            return lambda i, j: t[:, ds(base + 4 * S * j + 8 * S * i, 4 * S)]

        def at_rows(t, base):
            return lambda i, j: t[:, :, ds(base + UN * j + 2 * UN * i, UN)]

        parts = [Part("T", 1, lambda i, j: (w_in, q0 + UN * j), at_T(qk_flat, 0), AD ** -0.5),
                 Part("T", 1, lambda i, j: (w_in, k0 + UN * j), at_T(qk_flat, 8 * S)),
                 Part("rows", 1, lambda i, j: (w_in, v0 + UN * j), at_rows(v, 0)),
                 Part("T", 1, lambda i, j: (w_in, gq0 + UN * j), at_T(gqk_flat, 0)),
                 Part("rows", 1, lambda i, j: (w_in, gv0 + UN * j), at_rows(gv, 0)),
                 Part("rows", 1, lambda i, j: (w_in, gr0 + UN * j), at_rows(gr, 0))]
        w_out = ins["w_out"][0]
        with ExitStack() as st:
            kit.x_hi_t = kit.sb("h_hi_1", [P, KT, S], st, R32)
            stage_product(kit, parts, lambda sp, l: load_block(kit, sp, l, 0, w_out, 0), Ada(kit, st, "a"),
                          range(len(parts)), (lr_sync, lr_pe, lr_act, lambda dve: dve.wait_ge(s_lr, 2)))
        stage_attention(kit, qkT[:, 0:AW // P, :], qkT[:, AW // P:, :], v, mem["bias_dram"], kit.hT)
        att.close()

        stage_gla(kit, gqk, gv, gr, glr, kit.hT[:, AW // P:, :])
        mix.close()
        w_gate, w_up, w_down = ins["w_gate"][0], ins["w_up"][0], ins["w_down"][0]
        with ExitStack() as st:
            mixed = kit.sb("mixed", [P, ST, D], st)
            kit.x_hi_t = kit.sb("h_hi_2", [P, KT, S], st, R32)
            to_mixed = [Part("rows", 2, lambda i, j: (w_out, UN * j + 2 * UN * i), at_rows(mixed, 0))]
            stage_product(kit, to_mixed, lambda sp, l: load_block(kit, sp, l, 0, w_gate, 0))
            stage_add(kit, mixed, None)
        norm_steps(kit, kit.x, None, True, lambda k: kit.cols("ffn_norm_w", k), None, None)
        with ExitStack() as st:
            kit.x_hi_t = kit.sb("h_hi_3", [P, KT, S], st, R32)
            actT = kit.sb("act_T", [P, F1 // P, S], st)
            silu = kit.sb("silu", [P, 4 * S], st)

            def down_head(sp, l):
                for k in range(LOADS):
                    load(kit, sp, l + k, 0, wide_src(w_down, P * k))
            stage_glu(kit, Ada(kit, st, "b"), actT[:, :, :], silu[:, :], w_gate, w_up, down_head)
            w2 = ins["w_in_2"][0]
            r_src = lambda i, j: (w2, (0, 2 * RH * RK + 2 * RH * RV)[j])
            stage_down(kit, w_down, F1 // P, actT, kit.x, lambda sp, l: load_block(kit, sp, l, 0, w2, 0))

        with ExitStack() as st:
            fin = kit.sb("final_w", [P, D], st)
            kit.loads(1)
            with nc.Block() as block:
                @block.sync
                def _(sp):
                    sp.dma_start(fin[:, :], ins["final_norm_w"].partition_broadcast(P)).then_inc(kit.loaded, 16)
                    sp.wait_ge(kit.loaded, kit.loads_done)
            norm_steps(kit, kit.x, None, False, None, None, fin)
        modcols = kit.modcols
        stage_modulation(kit, modcols)

        def norm_mod(n):
            norm_steps(kit, kit.x, None, True, lambda k: kit.modT[:, KT * n + k:KT * n + k + 1],
                       lambda k: modcols[:, (0, 48)[n] + k:(0, 48)[n] + k + 1], None)
        norm_mod(0)
        st_rw = ctx.enter_context(ExitStack())
        rw = kit.sb("rw_T", [P, 3 * RWW // P, S], st_rw)
        low = kit.sb("low_T", [P, 4, S], st_rw)
        st_moba = ctx.enter_context(ExitStack())
        mqk = kit.sb("mqk_T", [P, 2 * MH, S], st_moba)
        mv = kit.sb("mv_rows", [P, ST, MH * MD], st_moba)
        st_ret = ctx.enter_context(ExitStack())
        rqk = kit.sb("rqk_T", [P, 4, S], st_ret)
        rvg = kit.sb("rvg_rows", [P, ST, 2 * RH * RV], st_ret)
        with ExitStack() as st:
            LW = DRANK + ARANK + GGRANK
            wlow = kit.sb("w_low", [P, KT, LW], st)
            low_ready = kit.loads(1)
            s_low = kit.sem("codes2")
            l0 = RCOLS + 3 * RWW
            m0 = RCOLS + WCOLS
            spans = ((0, DRANK), (DRANK, DRANK + ARANK), (DRANK + ARANK, DRANK + ARANK + P), (DRANK + ARANK + P, LW))

            def low_sync(sp):
                sp.dma_start(wlow[:, :, :], w2[:, l0:l0 + LW].rearrange("(k p) n -> p k n", p=P)).then_inc(kit.loaded, 16)

            def low_pe(pe):
                pe.wait_ge(kit.loaded, low_ready)
                for q, (a, b) in enumerate(spans):
                    for k in range(KT):
                        i_ = nc.tensor.matmul(kit.ps[0:b - a, 4 + q, 0:S], lhsT=wlow[:, k, a:b], rhs=kit.hT[:, k, :],
                                              start=(k == 0), stop=(k == KT - 1))
                    i_.then_inc(s_low, 1)

            def low_act(act):
                for q, (a, b) in enumerate(spans):
                    act.wait_ge(s_low, q + 1)
                    kit.act(nc.scalar.activation(low[0:b - a, q, :], kit.ps[0:b - a, 4 + q, 0:S], ACT.Copy))

            rwf, rqkf, mqkf = flat(rw[:, :, :]), flat(rqk[:, :, :]), flat(mqk[:, :, :])
            c1 = RCOLS
            parts = [Part("T", 1, r_src, lambda i, j: (rqkf, rwf)[j][:, 0:4 * S]),
                     Part("T", 1, lambda i, j: (w2, c1 + RWW + RWW * j), at_T(rwf, 4 * S)),
                     Part("T", 1, lambda i, j: (w2, m0 + UN * j), at_T(mqkf, 0), MD ** -0.5),
                     Part("T", 1, lambda i, j: (w2, m0 + MH * MD + UN * j), at_T(mqkf, 8 * S)),
                     Part("rows", 1, lambda i, j: (w2, 2 * RH * RK + UN * j), at_rows(rvg, 0)),
                     Part("rows", 1, lambda i, j: (w2, m0 + 2 * MH * MD + UN * j), at_rows(mv, 0))]
            wo2 = ins["w_out_2"][0]
            kit.x_hi_t = kit.sb("h_hi_4", [P, KT, S], st, R32)
            stage_product(kit, parts, lambda sp, l: load_block(kit, sp, l, 0, wo2, 0),
                          low=(low_sync, low_pe, low_act, lambda dve: dve.wait_ge(s_low, 4)))
        stage_retention(kit, rqk, rvg, kit.hT[:, 0:4, :])
        st_ret.close()
        stage_moba(kit, mqk, mv, kit.hT[:, 8:16, :])
        st_moba.close()
        stage_rwkv(kit, rw, low, kit.hT[:, 4:8, :])
        st_rw.close()
        w_up2, w_down2 = ins["w_ffn_up_2"][0], ins["w_ffn_down_2"][0]
        with ExitStack() as st:
            mixed = kit.sb("mixed2", [P, ST, D], st)
            row = kit.sb("gate1_row", [P, D], st)
            stage_gate_row(kit, "gate1", modcols, lambda k: 2 * KT + k, row)
            kit.x_hi_t = kit.sb("h_hi_5", [P, KT, S], st, R32)
            to_mixed = [Part("rows", 2, lambda i, j: (wo2, UN * j + 2 * UN * i), at_rows(mixed, 0))]
            stage_product(kit, to_mixed, lambda sp, l: load_block(kit, sp, l, 0, w_up2, F2))
            stage_add(kit, mixed, row[:, :])
        norm_mod(1)
        with ExitStack() as st:
            kit.x_hi_t = kit.sb("h_hi_6", [P, KT, S], st, R32)
            actT = kit.sb("act2_T", [P, F2 // P, S], st)

            def down2_head(sp, l):
                for k in range(LOADS):
                    load(kit, sp, l + k, 0, wide_src(w_down2, P * k))
            stage_conv_glu(kit, w_up2, actT[:, :, :], down2_head)
            gate = kit.sb("gate2_row", [P, D], st)
            stage_gate_row(kit, "gate2", modcols, lambda k: 5 * KT + k, gate)
            stage_down(kit, w_down2, F2 // P, actT, kit.x, None, gate)
        with ExitStack() as st:
            fin = kit.sb("final_w2", [P, D], st)
            kit.loads(1)
            with nc.Block() as block:
                @block.sync
                def _(sp):
                    sp.dma_start(fin[:, :], ins["norm_final_2"].partition_broadcast(P)).then_inc(kit.loaded, 16)
                    sp.wait_ge(kit.loaded, kit.loads_done)
            norm_steps(kit, kit.x, None, False, None, None, fin)
        s_fin = kit.sem("stored")
        with nc.Block() as block:
            @block.sync
            def _(sp):
                sp.dma_start(out.rearrange("b (t p) d -> p (b t) d", p=P), kit.x[:, :, :]).then_inc(s_fin, 16)
                sp.wait_ge(s_fin, 16)


INPUTS = ["x", "attn_norm_w", "w_in", "rel_bias_table", "gla_gate_w_fwd", "gla_gate_b_fwd", "gla_gate_w_bwd",
          "gla_gate_b_bwd", "gla_norm_w", "w_out", "ffn_norm_w", "w_gate", "w_up", "w_down", "final_norm_w", "c_2",
          "w_in_2", "w_out_2", "rwkv_mu_2", "rwkv_w0_2", "rwkv_w_up_2", "rwkv_a0_2", "rwkv_a_up_2", "rwkv_g_up_2",
          "rwkv_k_k_2", "rwkv_k_a_2", "rwkv_r_k_2", "rwkv_ln_w_2", "rwkv_ln_b_2", "w_ffn_up_2", "ffn_conv_w_2",
          "ffn_conv_b_2", "w_ffn_down_2", "w_ada_2", "b_ada_2", "norm_mix_2", "norm_ffn_2", "norm_final_2"]


def kernel(**inputs):
    import concourse.bacc as bacc
    from concourse.bass_utils import run_bass_kernel_spmd as run

    nc = bacc.Bacc("TRN2", target_bir_lowering=False, num_devices=1)
    consts, at = constants()
    arrays, aps = {}, {}
    for name in INPUTS + ["consts"]:
        a = np.ascontiguousarray(consts if name == "consts" else inputs[name])
        arrays[f"in_{name}_dram"] = a
        aps[name] = nc.dram_tensor(f"in_{name}_dram", a.shape, mybir.dt.from_np(a.dtype), kind="ExternalInput").ap()
    out = nc.dram_tensor("out_0_dram", (1, S, D), F32, kind="ExternalOutput").ap()
    program(nc, aps, at, out)
    return run(nc, [arrays], core_ids=[0]).results[0]["out_0_dram"]
```

```python
from contextlib import ExitStack
import math

import numpy as np

import concourse.bass as bass
from concourse import mybir

ALU = mybir.AluOpType
ACT = mybir.ActivationFunctionType
AX = mybir.AxisListType.X
F32 = mybir.dt.float32
R32 = mybir.dt.float32r
ds = bass.ds

P = 128
S = 256
ST = S // P
D = 2048
KT = D // P
NORM_EPS = 1e-6
AH, AD = 16, 64
AW = AH * AD
BUCKETS, MAXDIST = 32, 1024
PATTERNS = ((128, 1), (512, 4), (2048, 16))
GH, GK, GV = 4, 128, 256
GCH = 64
GRANK = 16
GTAU = 16.0
F1 = 5632
RH, RK, RV = 4, 64, 128
RWH, RWN = 8, 64
RWW = RWH * RWN
DRANK, ARANK, GGRANK = 96, 96, 256
GN_EPS = 64e-5
MH, MD = 8, 128
F2 = 5632
RCOLS = 2 * RH * RK + 2 * RH * RV
WCOLS = 3 * RWW + DRANK + ARANK + GGRANK
CH = 64
NCH = S // CH

LOADS = 4
UK, UN = 4, 512
UNIT = UK * UN // 2
SPLITS = 4
AHEAD = 3

COLS = {}
_n = 0
for _name, _w in (("attn_norm_w", 16), ("ffn_norm_w", 16), ("norm_mix_2", 16), ("norm_ffn_2", 16), ("c_2", 16),
                  ("gla_norm_w", 8), ("mu_rkv", 12), ("rwkv_w0_2", 4), ("rwkv_a0_2", 4), ("rwkv_k_k_2", 4),
                  ("rwkv_k_a_2", 4), ("rwkv_r_k_2", 4), ("rwkv_ln_w_2", 4), ("rwkv_ln_b_2", 4),
                  ("gla_gate_b_fwd", 4), ("gla_gate_b_bwd", 4), ("mu_wd", 1), ("mu_wa", 1), ("mu_wg", 2),
                  ("conv_w0", 88), ("conv_w1", 88), ("conv_w2", 88), ("conv_b", 88), ("b_ada_2", 96)):
    COLS[_name] = _n
    _n += _w
NCOLS = _n


def t5_bucket(rel):
    nb = BUCKETS // 2
    n = np.abs(rel)
    exact = nb // 2
    large = exact + (np.log(np.maximum(n, 1) / exact) / math.log(MAXDIST / exact) * (nb - exact)).astype(np.int64)
    return np.where(rel > 0, nb, 0) + np.where(n < exact, n, np.minimum(large, nb - 1))


def constants():
    i = np.arange(P)
    r, c = i[:, None], i[None, :]
    same = (r // CH) == (c // CH)
    parts = [("ident", r == c), ("ones", np.ones((P, P))), ("headsum", same), ("flip", r + c == P - 1),
             ("incl", same & (r <= c)), ("strict", same & (r < c)), ("anti", same & (r >= c))]
    b = 1
    while b < CH:
        lvl = (r // (2 * b) == c // (2 * b)) & (r % (2 * b) < b) & (c % (2 * b) >= b)
        parts.append((f"lvlT{b}", lvl))
        if b == 1:
            parts.append(("lvl1", lvl.T))
        b *= 2
    tok = np.arange(S)
    off = tok[None, :] - tok[:, None]
    count = sum(((off % dil == 0) & (np.abs(off) <= win // 2)).astype(np.float64) for win, dil in PATTERNS)
    parts.append(("carry", np.broadcast_to(np.tile(tok % CH != 0, 4), (P, 4 * S))))
    lnc = np.where(count > 0, np.log(np.maximum(count, 1)), -1e30)
    parts.append(("lncount", lnc.reshape(ST, P, S).transpose(1, 0, 2).reshape(P, -1)))
    g = np.log1p(-np.exp2(-5.0 - np.arange(RH)))
    d = tok[None, :] - i[:, None]
    ret = np.where(d[:, None, :] >= 0, np.exp(g[None, :, None] * np.maximum(d, 0)[:, None, :]), 0.0) * RK ** -0.5
    parts.append(("retdecay", ret.reshape(P, -1)))
    dist = np.where(off <= 0, -off, 1e34)
    parts.append(("distance", dist.reshape(ST, P, S).transpose(1, 0, 2).reshape(P, -1)))
    hot = np.zeros((P, 2 * S))
    m = np.arange(2 * S - 1)
    hot[t5_bucket(m - (S - 1)), m] = 1
    parts.append(("onehot", hot))
    at, n = {}, 0
    for name, a in parts:
        at[name] = (n, n + a.shape[1])
        n += a.shape[1]
    return np.concatenate([np.asarray(a, np.float32) for _, a in parts], axis=1), at


class Kit:

    def __init__(self, nc, ctx, ins, at):
        self.nc, self.ins, self.at = nc, ins, at
        self.ctx = ctx
        self.units = 0
        self.pairs = [0, 0]
        self.loads_done = 0
        self.norms = self.turns = 0
        self.dve_steps = 0
        self.act_steps = 0
        sb = self.sb
        self.x = sb("x_rows", [P, ST, D])
        at_h = nc.sbuf_base
        self.hT = sb("h_T", [P, KT, S])
        self.x_lo_t = nc.alloc_sbuf_tensor_at("h_lo_T", [P, KT, S], R32, offset=-(-at_h // 32) * 32)
        self.raw = sb("raw_weights", [P, LOADS, 2 * UNIT])
        self.w_hi_t = sb("weights_hi", [P, SPLITS, UNIT], dt=R32)
        self.w_lo_t = sb("weights_lo", [P, SPLITS, UNIT], dt=R32)
        self.x_splits = self.act_splits = self.ada_groups = 0
        self.resident = at["carry"][1]
        self.cst = sb("cst", [P, self.resident])
        self.col = sb("col", [P, NCOLS])
        self.stat = sb("stat", [P, 64])
        self.modT = sb("modT", [P, 2 * KT])
        self.modcols = sb("modcols", [P, 6 * D // P])
        self.ps = ctx.enter_context(nc.psum_tensor("ps", [P, 8, 512], F32))
        self.weights_in = [self.sem(f"weights_in{i}") for i in range(LOADS)]
        self.w_hi, self.w_lo, self.x_hi, self.x_lo, self.a_hi, self.a_lo = (
            self.sem(n) for n in ("weights_hi", "weights_lo", "x_hi", "x_lo", "act_hi", "act_lo"))
        self.ada_w = [self.sem("ada_w0"), self.sem("ada_w1")]
        self.ada_acc, self.ada_sum, self.ada_out = (self.sem("ada_" + n) for n in ("acc", "sum", "out"))
        self.weights_used = self.sem("weights_used")
        self.pair_free = [self.sem(f"pair_free{i}") for i in range(2)]
        self.dve_order = self.sem("dve_order")
        self.act_order = self.sem("act_order")
        self.loaded = self.sem("loaded")
        self.gated_norm = [self.sem("gated_norm_" + n) for n in ("mean", "rms", "normed", "turned", "out_dve",
                                                                 "out_act")]
        self.gated_norms = (0, 0, 0)
        self.row_spread, self.row_copied, self.row_copies = self.sem("row_spread"), self.sem("row_copied"), 0
        self.x_added, self.added = self.sem("x_added"), 0
        self.down_sums, self.down_out = self.sem("down_sums"), 0
        self.final_x, self.finals = self.sem("final_x"), 0
        self.square_parts = 1
        self.n_mean = self.sem("norm_mean")
        self.n_rms = self.sem("norm_rms")
        self.n_scaled = self.sem("norm_scaled")
        self.n_turned = self.sem("norm_turned")
        self.n_out = [self.sem("norm_out_dve"), self.sem("norm_out_act")]

    def loads(self, n):
        self.loads_done = self.loads_done + 16 * n
        return self.loads_done

    def sb(self, name, shape, ctx=None, dt=F32):
        return (ctx or self.ctx).enter_context(self.nc.sbuf_tensor(name, shape, dt))

    def sem(self, name):
        return self.ctx.enter_context(self.nc.semaphore(name))

    def const_src(self, name):
        a, b = self.at[name]
        return self.ins["consts"][:, a:b]

    def c(self, name):
        a, b = self.at[name]
        return self.cst[:, a:b]

    def cols(self, name, k):
        return self.col[:, COLS[name] + k:COLS[name] + k + 1]

    def dve(self, ins):
        self.dve_steps += 1
        ins.then_inc(self.dve_order, 1)
        self.nc.vector.wait_ge(self.dve_order, self.dve_steps)

    def act(self, ins):
        self.act_steps += 1
        ins.then_inc(self.act_order, 1)
        self.nc.scalar.wait_ge(self.act_order, self.act_steps)


def flat(ap):
    return ap.rearrange("p a b -> p (a b)")


def load(kit, sp, l, i, src):
    if l >= LOADS:
        sp.wait_ge(kit.w_lo, 2 * (l - LOADS) + 2 + 16 * i)
    sp.dma_start(kit.raw[:, l % LOADS, :].rearrange("p (k n) -> p k n", k=src.shape[1]), src
                 ).then_inc(kit.weights_in[l % LOADS], 16)


def block_src(w, u, col):
    return w[u * UK * P:(u + 1) * UK * P, ds(col, UN)].rearrange("(k p) n -> p k n", p=P)


def load_block(kit, sp, l, i, w, col):
    for u in range(4):
        load(kit, sp, l + u, i, block_src(w, u, col))


def wide_src(w, row):
    return w[ds(row, P), :].rearrange("p (a n) -> p a n", a=1)


def split_hi(kit, act, n, i):
    act.wait_ge(kit.weights_in[(n // 2) % LOADS], 16 * (n // (2 * LOADS) + 1) + 32 * i)
    if n >= SPLITS:
        act.wait_ge(kit.weights_used, n - SPLITS + 1 + 16 * i)
    raw = kit.raw[:, (n // 2) % LOADS, (n % 2) * UNIT:(n % 2 + 1) * UNIT]
    kit.nc.scalar.activation(kit.w_hi_t[:, n % SPLITS, :], raw, ACT.Copy).then_inc(kit.w_hi, 1)


def split_lo(kit, dve, n, i):
    dve.wait_ge(kit.w_hi, n + 1 + 16 * i)
    raw = kit.raw[:, (n // 2) % LOADS, (n % 2) * UNIT:(n % 2 + 1) * UNIT]
    kit.nc.vector.tensor_tensor(kit.w_lo_t[:, n % SPLITS, :], raw, kit.w_hi_t[:, n % SPLITS, :].bitcast(F32),
                                ALU.subtract).then_inc(kit.w_lo, 1)


def split_x_hi(kit, act, norm):
    for u in range(4):
        if norm:
            norm.out_act(act, u)
        kit.nc.scalar.activation(kit.x_hi_t[:, 4 * u:4 * u + 4, :], kit.hT[:, 4 * u:4 * u + 4, :], ACT.Copy
                                 ).then_inc(kit.x_hi, 1)


def split_x_lo(kit, dve, base, norm, wait=None):
    for u in range(4):
        if norm:
            norm.out_dve(dve, u)
    if wait:
        dve.wait_ge(*wait)
    for u in range(4):
        dve.wait_ge(kit.x_hi, base + u + 1)
        kit.nc.vector.tensor_tensor(kit.x_lo_t[:, 4 * u:4 * u + 4, :], kit.hT[:, 4 * u:4 * u + 4, :],
                                    kit.x_hi_t[:, 4 * u:4 * u + 4, :].bitcast(F32), ALU.subtract
                                    ).then_inc(kit.x_lo, 1)


def multiply_block(kit, pe, form, j, n0, i, use, xbase, mid=None, spans=None):
    nc = kit.nc
    spans = spans or [(q * P, (q + 1) * P) for q in range(4)]
    xh, xl = kit.x_hi_t, kit.x_lo_t
    pe.wait_ge(kit.pair_free[j], use + 1 + i)
    for u in range(8):
        n = n0 + u
        s = n % SPLITS
        if xbase is not None and u % 2 == 0:
            pe.wait_ge(kit.x_lo, xbase + u // 2 + 1)
        pe.wait_ge(kit.w_lo, n + 1 + 16 * i)
        for kk in range(2):
            k = 2 * u + kk
            a = kk * UN
            for q in range(2 if form == "rows" else 4):
                if form == "rows":
                    out = kit.ps[:, 2 * j + q, :]
                    wh, wl = (w[:, s, a:a + UN] for w in (kit.w_hi_t, kit.w_lo_t))
                    h, l = (x[:, k, q * P:(q + 1) * P] for x in (xh, xl))
                    passes = ((h, wh), (h, wl), (l, wh))
                    start = k == 0
                else:
                    c0, c1 = spans[q]
                    out = kit.ps[0:c1 - c0, 2 * j + q // 2, (q % 2) * S:(q % 2 + 1) * S]
                    wh, wl = (w[:, s, a + c0:a + c1] for w in (kit.w_hi_t, kit.w_lo_t))
                    h, l = xh[:, k, :], xl[:, k, :]
                    passes = ((wh, h), (wh, l), (wl, h))
                    start = k == 0 and q % 2 == 0
                for m, (lhsT, rhs) in enumerate(passes):
                    ins = nc.tensor.matmul(out, lhsT=lhsT, rhs=rhs, start=start and m == 0,
                                           stop=(k == KT - 1 and m == 2), skip_group_check=True)
        ins.then_inc(kit.weights_used, 1)
        if mid and u == 0:
            mid()


class Columns:

    def __init__(self, form, w, col, out=None, scale=1.0, spans=None, add_at=0):
        self.form, self.w, self.col, self.out, self.scale, self.spans = form, w, col, out, scale, spans
        self.add_at = add_at


def run_turns(eng, start, turns, body):
    if turns - start > 1:
        with eng.Fori(start, turns) as i:
            body(i)
    elif turns - start == 1:
        body(start)


def stage_product(kit, blocks, head_next, norm=None, ada=None, low=None, rows=(), gate=None):
    nc = kit.nc
    first = kit.units
    start = [first + 8 * n for n in range(len(blocks))]
    end = first + 8 * len(blocks)
    uses = list(kit.pairs)
    xbase = kit.x_splits
    kit.x_splits += 4
    lead, groups = kit.ada_groups, len(blocks) // 4 if ada else 0
    added = kit.added
    adds = [n for n, b in enumerate(blocks) if b.out is None]
    kit.added += len(adds)
    if adds:
        kit.square_parts = len(adds)

    def group_of(n):
        return (n // 4 if n // 4 < groups else None), n % 4 == 0 and 0 < n // 4 <= groups

    with nc.Block() as block:
        @block.sync
        def _(sp):
            if low:
                low[0](sp)
            for n in range(len(blocks)):
                for u in range(4):
                    if group_of(n)[0] is not None and u % 2 == 0:
                        ada.load(sp, lead + n // 4, 0, 2 * (n % 4) + u // 2)
                    if n + 1 < len(blocks):
                        then = blocks[n + 1]
                        load(kit, sp, start[n] // 2 + 4 + u, 0, block_src(then.w, u, then.col))
            head_next(sp, end // 2)

        @block.tensor
        def _(pe):
            if norm:
                norm.turn(pe)
            if low:
                low[1](pe)
            for n, b in enumerate(blocks):
                mid = None
                if group_of(n)[1]:
                    mid = lambda: ada.sums(pe, lead + n // 4, 0)
                elif n < len(rows):
                    mid = lambda: rows[n].spread(pe)
                multiply_block(kit, pe, b.form, n % 2, start[n], 0, uses[n % 2] + n // 2, xbase if n == 0 else None,
                               mid, b.spans)
            if groups and len(blocks) % 4 == 0:
                ada.sums(pe, lead + groups, 0)

        @block.scalar
        def _(act):
            if norm:
                norm.root(act)
            split_x_hi(kit, act, norm)
            if low:
                low[2](act)

            def squares(n):
                act.wait_ge(kit.x_added, added + adds.index(n) + 1)
                for t in range(ST):
                    ins = nc.scalar.activation(kit.ps[:, 2 * (n % 2) + t, :],
                                               kit.x[:, t, blocks[n].add_at:blocks[n].add_at + UN], ACT.Square,
                                               accum_out=kit.stat[:, 8 * t + adds.index(n):8 * t + adds.index(n) + 1])
                ins.then_inc(kit.pair_free[n % 2], 1)

            for n, b in enumerate(blocks):
                j = n % 2
                for u in range(8):
                    split_hi(kit, act, start[n] + AHEAD + u, 0)
                    if u == 3 and n - 1 in adds:
                        squares(n - 1)
                    if u == 3 and n < len(rows):
                        rows[n].copy(act)
                if b.out is not None:
                    act.wait_ge(kit.weights_used, start[n] + 8)
                    src = kit.ps[:, 2 * j:2 * j + 2, :]
                    if b.spans:
                        for q, (c0, c1) in enumerate(b.spans):
                            ins = nc.scalar.activation(b.out[q], kit.ps[0:c1 - c0, 2 * j + q // 2,
                                                                        (q % 2) * S:(q % 2 + 1) * S], ACT.Copy)
                    else:
                        ins = nc.scalar.activation(b.out, flat(src) if b.form == "T" else src, ACT.Copy, scale=b.scale)
                    ins.then_inc(kit.pair_free[j], 1)
            if len(blocks) - 1 in adds:
                bring_root(kit)
                squares(len(blocks) - 1)

        @block.vector
        def _(dve):
            if norm:
                norm.scales(dve)
            split_x_lo(kit, dve, xbase, norm, (kit.act_order, kit.act_steps) if low else None)
            for n, b in enumerate(blocks):
                group, summed = group_of(n)
                for u in range(8):
                    split_lo(kit, dve, start[n] + AHEAD + u, 0)
                    if summed and u == 0:
                        ada.copy(dve, lead + n // 4, 0)
                    if group is not None and u % 2 == 0:
                        ada.product(dve, lead + group, 0, 4 * (n % 4) + u // 2)
                if b.out is None:
                    dve.wait_ge(kit.weights_used, start[n] + 8)
                    sums = kit.ps[:, 2 * (n % 2):2 * (n % 2) + 2, :]
                    x = kit.x[:, :, b.add_at:b.add_at + UN]
                    if gate is not None:
                        dve.wait_ge(kit.row_copied, rows[0].before + 4)
                        g = gate[:, b.add_at:b.add_at + UN].unsqueeze(1).broadcast_to([P, ST, UN])
                        kit.dve(nc.vector.tensor_tensor(sums, sums, g, ALU.mult))
                    nc.vector.tensor_tensor(x, sums, x, ALU.add).then_inc(kit.x_added, 1)
            if groups and len(blocks) % 4 == 0:
                ada.copy(dve, lead + groups, 0)

    kit.units = end
    kit.pairs = [uses[0] + (len(blocks) + 1) // 2, uses[1] + len(blocks) // 2]
    kit.ada_groups += groups


def stage_down(kit, w, w_tiles, actT, head_next, final_w, final_src, gate=None):
    nc = kit.nc
    first, k_lo = kit.units, kit.act_splits
    kit.act_splits += w_tiles
    lead = w_tiles % 8
    R = 8
    last = head_next is None
    added, out = kit.added, kit.down_out
    kit.added += 4
    kit.down_out += 2
    kit.square_parts = 2
    kit.loads(1)
    ends = ((0, 0), (0, 1), (1, 0), (1, 1))
    sums_of = lambda half, t: flat(kit.ps[:, 4 * t + 2 * half:4 * t + 2 * half + 2, :])

    def in_turns(eng, body):
        for k in range(lead):
            body(k, 0, 0)
        turns = w_tiles // 8
        with eng.Fori(0, turns - 1) as i:
            for k in range(lead, lead + 8):
                body(k, i, 0)
        for k in range(lead, lead + 8):
            body(k, turns - 1, w_tiles - 8 - lead)

    with nc.Block() as block:
        @block.sync
        def _(sp):
            sp.dma_start(final_w[:, :], final_src).then_inc(kit.loaded, 16)

            def body(k, i, _):
                load(kit, sp, first // 2 + k, i, wide_src(w, P * k + 8 * P * i))
            for k in range(LOADS, lead):
                body(k, 0, 0)
            turns = w_tiles // 8
            with sp.Fori(0, turns) as i:
                for k in range(max(lead, LOADS), lead + 8):
                    body(k, i, 0)
            if not last:
                head_next(sp, first // 2 + w_tiles)

        @block.tensor
        def _(pe):
            def body(k, i, past):
                pe.wait_ge(kit.a_lo, k_lo + k + 1 + 8 * i)
                for half in range(2):
                    n = first + 2 * k + half
                    s = n % SPLITS
                    pe.wait_ge(kit.w_lo, n + 1 + 16 * i)
                    for t in range(ST):
                        h, l = (x[:, k % R, t * P:(t + 1) * P] for x in (kit.x_hi_t, kit.x_lo_t))
                        for q in range(2):
                            wh, wl = (x[:, s, q * UN:(q + 1) * UN] for x in (kit.w_hi_t, kit.w_lo_t))
                            for m, (lhsT, rhs) in enumerate(((h, wh), (h, wl), (l, wh))):
                                ins = nc.tensor.matmul(kit.ps[:, 4 * t + 2 * half + q, :], lhsT=lhsT, rhs=rhs,
                                                       start=(k == 0 and m == 0), stop=(k + past == w_tiles - 1
                                                                                        and m == 2),
                                                       skip_group_check=True)
                        if t == 0 and k + past == w_tiles - 1:
                            ins.then_inc(kit.down_sums, 1)
                    ins.then_inc(kit.weights_used, 1)
            in_turns(pe, body)

        @block.scalar
        def _(act):
            def tile(k, i):
                if k >= R:
                    act.wait_ge(kit.weights_used, first + 2 * (k - R) + 2 + 16 * i)
                nc.scalar.activation(kit.x_hi_t[:, k % R, :], actT[:, ds(k + 8 * i, 1), :].rearrange(
                    "p a s -> p (a s)"), ACT.Copy).then_inc(kit.a_hi, 1)

            def body(k, i, past):
                for half in range(2):
                    if not (last and k + past == w_tiles - 1) and not (last and k + past == w_tiles - 2 and half):
                        split_hi(kit, act, first + 2 * k + half + AHEAD, i)
                if k + past + 4 < w_tiles:
                    tile(k + 4, i)
            for k in range(4):
                tile(k, 0)
            in_turns(act, body)
            bring_root(kit)
            for n, (half, t) in enumerate(ends):
                act.wait_ge(kit.x_added, added + n + 1)
                nc.scalar.activation(sums_of(half, t), kit.x[:, t, half * D // 2:(half + 1) * D // 2], ACT.Square,
                                     accum_out=kit.stat[:, 8 * t + half:8 * t + half + 1])

        @block.vector
        def _(dve):
            def tile(k, i):
                dve.wait_ge(kit.a_hi, k_lo + k + 1 + 8 * i)
                nc.vector.tensor_tensor(kit.x_lo_t[:, k % R, :], actT[:, ds(k + 8 * i, 1), :].rearrange(
                    "p a s -> p (a s)"), kit.x_hi_t[:, k % R, :].bitcast(F32), ALU.subtract).then_inc(kit.a_lo, 1)

            def body(k, i, past):
                for half in range(2):
                    if not (last and k + past == w_tiles - 1) and not (last and k + past == w_tiles - 2 and half):
                        split_lo(kit, dve, first + 2 * k + half + AHEAD, i)
                if k + past + 4 < w_tiles:
                    tile(k + 4, i)
            for k in range(4):
                tile(k, 0)
            in_turns(dve, body)
            for half, t in ends:
                if t == 0:
                    dve.wait_ge(kit.down_sums, out + half + 1)
                else:
                    dve.wait_ge(kit.weights_used, first + 2 * w_tiles - 1 + half)
                sums, x = sums_of(half, t), kit.x[:, t, half * D // 2:(half + 1) * D // 2]
                if gate is not None:
                    kit.dve(nc.vector.tensor_tensor(sums, sums, gate[:, half * D // 2:(half + 1) * D // 2], ALU.mult))
                nc.vector.tensor_tensor(x, sums, x, ALU.add).then_inc(kit.x_added, 1)
    kit.units = first + 2 * w_tiles


def rms_scales(kit, dve, r):
    nc, stat = kit.nc, kit.stat
    parts = stat[:, 0:16].rearrange("p (t b) -> p t b", t=ST)[:, :, 0:kit.square_parts]
    kit.dve(nc.vector.tensor_reduce(stat[:, 16:18], parts, AX, ALU.add))
    nc.vector.tensor_scalar(stat[:, 18:20], stat[:, 16:18], 1.0 / D, NORM_EPS, ALU.mult, ALU.add
                            ).then_inc(kit.n_mean, 1)
    dve.wait_ge(kit.n_rms, r + 1)
    kit.dve(nc.vector.reciprocal(stat[:, 20:22], stat[:, 18:20]))


def bring_root(kit, col=33):
    kit.nc.scalar.activation(kit.stat[:, col:col + 1], kit.c("ones")[:, 0:1], ACT.Sqrt)


def rms_root(kit, act, r):
    bring_root(kit, 32)
    act.wait_ge(kit.n_mean, r + 1)
    kit.nc.scalar.activation(kit.stat[:, 18:20], kit.stat[:, 18:20], ACT.Sqrt).then_inc(kit.n_rms, 1)


class Norm:

    def __init__(self, kit, ctx, wcol, bcol=None, modulated=None):
        self.kit, self.wcol, self.bcol, self.modulated = kit, wcol, bcol, modulated
        self.r, self.turns = kit.norms, kit.turns
        self.diag = kit.sb(f"norm_diag{kit.turns}", [P, ST, P], ctx)
        kit.norms += 1
        kit.turns += 1

    def scales(self, dve):
        kit = self.kit
        if self.modulated is not None:
            modulation(kit, self.modulated)
        rms_scales(kit, dve, self.r)
        for t in range(ST):
            kit.nc.vector.tensor_scalar(self.diag[:, t, :], kit.c("ident"), kit.stat[:, 20 + t:21 + t], None, ALU.mult
                                        ).then_inc(kit.n_scaled, 1)

    def root(self, act):
        rms_root(self.kit, act, self.r)

    def turn(self, pe):
        kit = self.kit
        pe.wait_ge(kit.n_scaled, ST * (self.turns + 1))
        for k in range(KT):
            if k >= 4:
                pe.wait_ge(kit.n_out[k % 2], KT // 2 * self.turns + (k - 4) // 2 + 1)
            for t in range(ST):
                ins = kit.nc.tensor.matmul(kit.ps[:, 4 + k % 4, t * P:(t + 1) * P], lhsT=kit.x[:, t, k * P:(k + 1) * P],
                                           rhs=self.diag[:, t, :], start=True, stop=True)
            ins.then_inc(kit.n_turned, 1)

    def out_dve(self, dve, u):
        kit = self.kit
        for k in (4 * u, 4 * u + 2):
            dve.wait_ge(kit.n_turned, KT * self.turns + k + 1)
            src = kit.ps[:, 4 + k % 4, 0:S]
            if self.bcol:
                ins = kit.nc.vector.tensor_scalar(kit.hT[:, k, :], src, self.wcol(k), self.bcol(k), ALU.mult, ALU.add)
            else:
                ins = kit.nc.vector.tensor_scalar(kit.hT[:, k, :], src, self.wcol(k), None, ALU.mult)
            ins.then_inc(kit.n_out[0], 1)

    def out_act(self, act, u):
        kit = self.kit
        for k in (4 * u + 1, 4 * u + 3):
            act.wait_ge(kit.n_turned, KT * self.turns + k + 1)
            kit.nc.scalar.activation(kit.hT[:, k, :], kit.ps[:, 4 + k % 4, 0:S], ACT.Identity, scale=self.wcol(k),
                                     bias=self.bcol(k) if self.bcol else 0.0).then_inc(kit.n_out[1], 1)
        for half in range(2):
            act.wait_ge(kit.n_out[half], KT // 2 * self.turns + 2 * u + 2)


def stage_final_norm(kit, weight, out=None):
    nc = kit.nc
    r, done = kit.norms, kit.finals
    kit.norms += 1
    kit.finals += 4
    quarters = [(t, slice(half * D // 2, (half + 1) * D // 2)) for t in range(ST) for half in range(2)]
    with nc.Block() as block:
        @block.vector
        def _(dve):
            rms_scales(kit, dve, r)
            dve.wait_ge(kit.loaded, kit.loads_done)
            for t, cols in quarters:
                nc.vector.scalar_tensor_tensor(kit.x[:, t, cols], kit.x[:, t, cols], kit.stat[:, 20 + t:21 + t],
                                               weight[:, cols], ALU.mult, ALU.mult).then_inc(kit.final_x, 1)

        @block.scalar
        def _(act):
            rms_root(kit, act, r)
            if out is None:
                for n, (t, cols) in enumerate(quarters):
                    act.wait_ge(kit.final_x, done + n + 1)
                    nc.scalar.activation(flat(kit.ps[:, 2 * n:2 * n + 2, :]), kit.x[:, t, cols], ACT.Square,
                                         accum_out=kit.stat[:, 8 * t + n % 2:8 * t + n % 2 + 1])

        if out is not None:
            @block.sync
            def _(sp):
                stored = kit.sem("stored")
                for n, (t, cols) in enumerate(quarters):
                    sp.wait_ge(kit.final_x, done + n + 1)
                    sp.dma_start(out[0, t * P:(t + 1) * P, cols], kit.x[:, t, cols]).then_inc(stored, 16)
                sp.wait_ge(stored, 16 * len(quarters))
    kit.square_parts = 2


def stage_setup(kit, mem, head):
    nc, ins = kit.nc, kit.ins
    names = list(COLS)
    width = {n: (COLS[names[i + 1]] if i + 1 < len(names) else NCOLS) - COLS[n] for i, n in enumerate(names)}
    mu = ins["rwkv_mu_2"]
    c3 = 3 * RWW

    def src(name):
        if name == "mu_rkv":
            return mu[0:1, 0:c3].rearrange("a (r f) -> (a r) f", f=P)
        if name == "mu_wg":
            return mu[0:1, c3 + DRANK + ARANK:WCOLS].rearrange("a (r f) -> (a r) f", f=P)
        if name == "rwkv_r_k_2":
            return ins[name].rearrange("a (r h) n -> (a r) (h n)", h=2)
        if name.startswith("conv_w"):
            j = int(name[-1])
            return ins["ffn_conv_w_2"][0, j:j + 1, :].rearrange("a (r f) -> (a r) f", f=P)
        if name == "conv_b":
            return ins["ffn_conv_b_2"].rearrange("a (r f) -> (a r) f", f=P)
        return ins[name].rearrange("a (r f) -> (a r) f", f=P)

    packs = [names[0:14], names[14:19], ["conv_w0"], ["conv_w1"], ["conv_w2"], ["conv_b"], ["b_ada_2"]]
    s_zero, s_rows, s_turn, s_col = (kit.sem(n) for n in ("pack_zeroed", "pack_loaded", "pack_turned", "pack_out"))
    s_bias, s_biasrow, s_biasout = (kit.sem(n) for n in ("bias_rows", "bias_rows_copied", "bias_rows_stored"))
    loads = sum(len(p) for p in packs)
    s_x = kit.sem("x_loaded")
    setup_loads = kit.loads(3)

    with ExitStack() as st:
        pack = kit.sb("pack", [P, len(packs), P], st)
        table = kit.sb("table", [BUCKETS, AH], st)
        hot = kit.sb("onehot", [BUCKETS, 2 * S], st)
        brow = kit.sb("brow", [AH, 2 * S], st)
        with nc.Block() as block:
            @block.sync
            def _(sp):
                sp.dma_start(kit.x[:, :, :], ins["x"].rearrange("b (t p) d -> p (b t) d", p=P)).then_inc(s_x, 16)
                sp.dma_start(kit.cst[:, :], ins["consts"][:, 0:kit.resident]).then_inc(kit.loaded, 16)
                sp.dma_start(table[:, :], ins["rel_bias_table"]).then_inc(kit.loaded, 16)
                sp.dma_start(hot[:, :], kit.const_src("onehot")[0:BUCKETS, :]).then_inc(kit.loaded, 16)
                for l in range(2):
                    head(sp, l)
                sp.wait_ge(s_zero, 1)
                for n, names_ in enumerate(packs):
                    at = 0
                    for name in names_:
                        w = width[name]
                        if name in ("mu_wd", "mu_wa"):
                            a = c3 + (DRANK if name == "mu_wa" else 0)
                            sp.dma_start(pack[at:at + 1, n, 0:DRANK], mu[0:1, a:a + DRANK]).then_inc(s_rows, 16)
                        else:
                            sp.dma_start(pack[at:at + w, n, :], src(name)).then_inc(s_rows, 16)
                        at += w
                for l in range(2, LOADS):
                    head(sp, l)
                sp.wait_ge(s_biasrow, 1)
                sp.dma_start(mem["bias_dram"].ap(), brow[:, :]).then_inc(s_biasout, 16)
                sp.wait_ge(s_biasout, 16)

            @block.vector
            def _(dve):
                nc.vector.memset(pack[:, 1, :], 0.0).then_inc(s_zero, 1)
                for j in range(2):
                    nc.vector.memset(kit.ps[:, 2 * j, 0:8], 0.0).then_inc(kit.pair_free[j], 1)
                at = 0
                for n, names_ in enumerate(packs):
                    w = sum(width[x] for x in names_)
                    dve.wait_ge(s_turn, n + 1)
                    nc.vector.tensor_copy(kit.col[:, at:at + w], kit.ps[:, 4 + n % 2, 0:w]).then_inc(s_col, 1)
                    at += w
                dve.wait_ge(s_bias, 1)
                nc.vector.tensor_copy(brow[:, :], kit.ps[0:AH, 7, :]).then_inc(s_biasrow, 1)
                for n in range(AHEAD):
                    split_lo(kit, dve, n, 0)

            @block.scalar
            def _(act):
                act.wait_ge(s_x, 16)
                for t in range(ST):
                    nc.scalar.activation(flat(kit.hT[:, 8 * t:8 * t + 8, :]), kit.x[:, t, :], ACT.Square,
                                         accum_out=kit.stat[:, 8 * t:8 * t + 1])
                act.wait_ge(s_col, 1)
                a = COLS["c_2"]
                kit.act(nc.scalar.activation(kit.col[:, a:a + KT], kit.col[:, a:a + KT], ACT.Silu))
                for n in range(AHEAD):
                    split_hi(kit, act, n, 0)

            @block.tensor
            def _(pe):
                pe.wait_ge(kit.loaded, setup_loads)
                nc.tensor.matmul(kit.ps[0:AH, 7, :], lhsT=table[:, :], rhs=hot[:, :],
                                 start=True, stop=True).then_inc(s_bias, 1)
                pe.wait_ge(s_rows, 16 * loads)
                for n, names_ in enumerate(packs):
                    w = sum(width[x] for x in names_)
                    if n >= 2:
                        pe.wait_ge(s_col, n - 1)
                    nc.tensor.transpose(kit.ps[:, 4 + n % 2, 0:w], pack[0:w, n, :], kit.c("ident")[0:w, 0:w]
                                        ).then_inc(s_turn, 1)


def in_steps(heads, steps):
    for tick in range(heads + max(delay for delay, _ in steps)):
        for delay, run in steps:
            if 0 <= tick - delay < heads:
                run(tick - delay)


class GlaGates:

    def __init__(self, kit, gw, glr, gr, A):
        self.kit, self.gw, self.glr, self.gr, self.A = kit, gw, glr, gr, A
        self.products, self.biased = kit.sem("gla_gate_products"), kit.sem("gla_gates_biased")

    def bank(self, d, m):
        return self.kit.ps[:, 2 * d + m // 2, (m % 2) * S:(m % 2 + 1) * S]

    def tensor(self, pe):
        for d in range(2):
            for m in range(GH):
                step = self.kit.nc.tensor.matmul(self.bank(d, m), lhsT=self.gw[:, d, m * P:(m + 1) * P],
                                                 rhs=self.glr[:, d, :], start=True, stop=True)
            step.then_inc(self.products, 1)
        pe.wait_ge(self.biased, 2 * GH)

    def vector(self, dve):
        for d, name in enumerate(("gla_gate_b_fwd", "gla_gate_b_bwd")):
            dve.wait_ge(self.products, d + 1)
            for m in range(GH):
                self.kit.nc.vector.tensor_scalar(self.A[:, d, m * S:(m + 1) * S], self.bank(d, m),
                                                 self.kit.cols(name, m), None, ALU.add).then_inc(self.biased, 1)

    def scalar(self, act):
        self.kit.nc.scalar.activation(self.gr[:, :, :], self.gr[:, :, :], ACT.Silu)


def stage_attention(kit, qT, kT, v, bias_dram, outT, gates):
    nc = kit.nc
    (s_first, s_logits, s_biased, s_max, s_neg, s_exp, s_recip, s_p, s_turned, s_pT, s_out, s_done) = (
        kit.sem("attn_" + n) for n in ("first_tables", "logits", "biased", "max", "negmax", "exp", "recip", "probs",
                                       "turned", "probsT", "out", "stored"))
    FIRST = 2
    tables_ready = kit.loads(AH - FIRST)
    with ExitStack() as st:
        hank = kit.sb("hankel", [P, AH, 3 * P], st)
        L = kit.sb("logits", [P, 2, ST, S], st)
        E = kit.sb("expd", [P, 3, ST, S], st)
        ET = kit.sb("probsT", [P, 2, ST, S], st)
        lncount = kit.sb("lncount", [P, ST * S], st)
        sc = kit.sb("attn_sc", [P, 3, 4, ST], st)
        mx, neg, tot, rec = (sc[:, :, n, :] for n in range(4))
        ps = kit.ps
        with nc.Block() as block:
            @block.sync
            def _(sp):
                src = bias_dram.ap()
                for h in range(AH):
                    sp.dma_start(hank[:, h, :], bass.AP(tensor=src.tensor, offset=h * 2 * S, ap=[[1, P], [1, 3 * P]])
                                 ).then_inc(s_first if h < FIRST else kit.loaded, 16)
                    if h == 0:
                        sp.dma_start(lncount[:, :], kit.const_src("lncount")).then_inc(s_first, 16)

            @block.tensor
            def _(pe):
                gates.tensor(pe)
                pe.wait_ge(s_first, 16 * (FIRST + 1))

                def logits(h):
                    hb, tile, b = AD * (h % 2), h // 2, h % 2
                    if h == FIRST:
                        pe.wait_ge(kit.loaded, tables_ready)
                    if h >= 2:
                        pe.wait_ge(s_biased, h - 1)
                    for t in range(ST):
                        nc.tensor.matmul(ps[:, b, t * S:(t + 1) * S], lhsT=qT[hb:hb + AD, tile, t * P:(t + 1) * P],
                                         rhs=kT[hb:hb + AD, tile, :], start=True, stop=False)
                        ins = nc.tensor.matmul(ps[:, b, t * S:(t + 1) * S], lhsT=kit.c("flip"),
                                               rhs=hank[:, h, P - t * P:P - t * P + S], start=False, stop=True)
                    ins.then_inc(s_logits, 1)

                def turn(h):
                    pe.wait_ge(s_p, ST * (h + 1))
                    if h >= 2:
                        pe.wait_ge(s_pT, h - 1)
                    for jt in range(ST):
                        for t in range(ST):
                            ins = nc.tensor.transpose(ps[:, 2 + h % 2, jt * S + t * P:jt * S + (t + 1) * P],
                                                      E[:, h % 3, t, jt * P:(jt + 1) * P], kit.c("ident"))
                    ins.then_inc(s_turned, 1)

                def sums(h):
                    pe.wait_ge(s_pT, h + 1)
                    if h % 2 == 0 and h >= 4:
                        pe.wait_ge(s_done, h // 2 - 1)
                    hb = AD * (h % 2)
                    for jt in range(ST):
                        ins = nc.tensor.matmul(ps[hb:hb + AD, 4 + (h // 2) % 2, 0:S],
                                               lhsT=v[:, jt, h * AD:(h + 1) * AD], rhs=ET[:, h % 2, jt, :],
                                               start=(jt == 0), stop=(jt == ST - 1))
                    ins.then_inc(s_out, 1)
                in_steps(AH, ((0, logits), (4, turn), (6, sums)))

            @block.vector
            def _(dve):
                gates.vector(dve)

                def biased(h):
                    dve.wait_ge(s_logits, h + 1)
                    if h >= 2:
                        dve.wait_ge(s_exp, ST * (h - 1))
                    nc.vector.tensor_tensor(flat(L[:, h % 2, :, :]), ps[:, h % 2, :], lncount[:, :],
                                            ALU.add).then_inc(s_biased, 1)

                def maximum(h):
                    dve.wait_ge(s_biased, h + 1)
                    if h >= 3:
                        dve.wait_ge(s_p, ST * (h - 2))
                    nc.vector.tensor_reduce(mx[:, h % 3, :], L[:, h % 2, :, :], AX, ALU.max).then_inc(s_max, 1)

                def negated(h):
                    dve.wait_ge(s_max, h + 1)
                    nc.vector.tensor_scalar(neg[:, h % 3, :], mx[:, h % 3, :], -1.0, None, ALU.mult
                                            ).then_inc(s_neg, 1)

                def recip(h):
                    dve.wait_ge(s_exp, ST * (h + 1))
                    nc.vector.reciprocal(rec[:, h % 3, :], tot[:, h % 3, :]).then_inc(s_recip, 1)

                def probs(h):
                    dve.wait_ge(s_recip, h + 1)
                    for t in range(ST):
                        nc.vector.tensor_scalar(E[:, h % 3, t, :], E[:, h % 3, t, :], rec[:, h % 3, t:t + 1], None,
                                                ALU.mult).then_inc(s_p, 1)

                def copy(h):
                    if h % 2:
                        dve.wait_ge(s_out, h + 1)
                        nc.vector.tensor_copy(outT[:, h // 2, :], ps[:, 4 + (h // 2) % 2, 0:S]).then_inc(s_done, 1)
                in_steps(AH, ((1, biased), (3, recip), (1, maximum), (3, probs), (1, negated), (7, copy)))

            @block.scalar
            def _(act):
                gates.scalar(act)

                def exp(h):
                    act.wait_ge(s_neg, h + 1)
                    if h >= 3:
                        act.wait_ge(s_turned, h - 2)
                    for t in range(ST):
                        nc.scalar.activation(E[:, h % 3, t, :], L[:, h % 2, t, :], ACT.Exp, bias=neg[:, h % 3, t:t + 1],
                                             accum_out=tot[:, h % 3, t:t + 1]).then_inc(s_exp, 1)

                def copy(h):
                    act.wait_ge(s_turned, h + 1)
                    if h >= 2:
                        act.wait_ge(s_out, h - 1)
                    nc.scalar.activation(flat(ET[:, h % 2, :, :]), ps[:, 2 + h % 2, :], ACT.Copy).then_inc(s_pT, 1)
                in_steps(AH, ((2, exp), (5, copy)))


def stage_gla(kit, A, gqk, gv, gr, outT):
    nc, ps = kit.nc, kit.ps
    W = GH * S
    G16 = 1.0 / GTAU
    sem = lambda n: kit.sem("gla_" + n)
    with ExitStack() as st:
        B = kit.sb("gla_b", [P, 2, W], st)
        G = kit.sb("gla_g", [P, 2, W], st)
        E = kit.sb("gla_e", [P, 2, W], st)
        q_in = kit.sb("gla_qin", [P, 2, W], st)
        k_in = kit.sb("gla_kin", [P, 2, W], st)
        k_end = B
        last = kit.sb("gla_last", [P, 2, GH * NCH], st)
        dec = kit.sb("gla_dec", [P, 2, GH * NCH], st)
        AT = kit.sb("gla_AT", [P, 2, ST, P], st)
        tmp = kit.sb("gla_tmp", [P, 2, S], st)
        states = kit.sb("gla_states", [P, 2, 2, 3, GV], st)
        krow = A.rearrange("p d (t f) -> p d t f", t=ST)
        orow = flat(E[:, :, :]).rearrange("p (t f) -> p t f", t=ST)
        chunks = lambda t: t.rearrange("p (g c) -> p g c", c=GCH)
        lastb = lambda d: last[:, d, :].unsqueeze(2).broadcast_to([P, GH * NCH, GCH])

        def update(d, n):
            bank, half = {(0, 0): (2, 0), (0, 2): (2, 1), (1, 1): (3, 0),
                          (0, 1): (4, 0), (1, 0): (4, 1), (1, 2): (7, 0)}[d, n]
            return ps[:, bank, half * GV:(half + 1) * GV]

        s_abs, s_e, s_ln, s_G, s_D, s_eq, s_ek, s_ee, s_in, s_end = (
            sem(n) for n in ("abs", "exp_abs", "softplus", "sums", "to_end", "exp_q", "exp_k",
                             "exp_end", "scaled", "k_end"))
        s_kt, s_kr, s_A, s_AT, s_U, s_st, s_O, s_oo = (
            sem(n) for n in ("kend_turned", "kend_rows", "products", "masked", "updates", "states", "out", "out_rows"))
        with nc.Block() as block:
            @block.tensor
            def _(pe):
                for g in range(4):
                    d, t = g // 2, g % 2
                    pe.wait_ge(s_end, d + 1)
                    for h in range(GH):
                        i_ = nc.tensor.transpose(ps[:, g, h * P:(h + 1) * P],
                                                 k_end[:, d, h * S + t * P:h * S + (t + 1) * P], kit.c("ident"))
                    i_.then_inc(s_kt, 1)
                pe.wait_ge(s_kr, 4)

                def products(h):
                    if h >= 2:
                        pe.wait_ge(s_AT, h - 1)
                    for d in range(2):
                        for t in range(ST):
                            a = h * S + t * P
                            i_ = nc.tensor.matmul(ps[:, h % 2, d * S + t * P:d * S + (t + 1) * P],
                                                  lhsT=k_in[:, d, a:a + P], rhs=q_in[:, d, a:a + P], start=True,
                                                  stop=True)
                    i_.then_inc(s_A, 1)

                def updates(h):
                    if h >= 1:
                        pe.wait_ge(s_st, h)
                    for d in range(2):
                        for n in range(3):
                            c = n if d == 0 else NCH - 1 - n
                            t, pb = c // 2, CH * (c % 2)
                            i_ = nc.tensor.matmul(update(d, n),
                                                  lhsT=krow[pb:pb + CH, d, t, h * GK:(h + 1) * GK],
                                                  rhs=gv[pb:pb + CH, t, h * GV:(h + 1) * GV], start=True, stop=True)
                    i_.then_inc(s_U, 1)

                def outputs(h):
                    pe.wait_ge(s_AT, h + 1)
                    pe.wait_ge(s_st, h + 1)
                    if h >= 2:
                        pe.wait_ge(s_oo, h - 1)
                    for t in range(ST):
                        o = ps[:, 5 + h % 2, t * GV:(t + 1) * GV]
                        i_ = nc.tensor.matmul(o, lhsT=AT[:, h % 2, t, :], rhs=gv[:, t, h * GV:(h + 1) * GV],
                                              start=True, stop=False, skip_group_check=True)
                        for c in range(2 * t, 2 * t + 2):
                            pb = CH * (c % 2)
                            for d, n in ((0, c - 1), (1, NCH - 2 - c)):
                                if n >= 0:
                                    i_ = nc.tensor.matmul(o[pb:pb + CH, :],
                                                          lhsT=q_in[:, d, h * S + c * CH:h * S + (c + 1) * CH],
                                                          rhs=states[:, h % 2, d, n, :], start=False, stop=False,
                                                          skip_group_check=True)
                    i_.then_inc(s_O, 1)
                in_steps(GH, ((0, products), (0, updates), (1, outputs)))

            @block.vector
            def _(dve):
                for d in range(2):
                    dve.wait_ge(s_ln, d + 1)
                    kit.dve(nc.vector.scalar_tensor_tensor(A[:, d, :], A[:, d, :], 0.0, B[:, d, :], ALU.min,
                                                           ALU.subtract))
                    step = nc.vector.tensor_tensor_scan(G[:, d, :], kit.c("carry"), A[:, d, :], 0.0, ALU.mult, ALU.add)
                    if d == 0:
                        step.then_inc(s_G, 1)
                        dve.wait_ge(s_G, 1)
                    else:
                        kit.dve(step)
                    kit.dve(nc.vector.tensor_copy(last[:, d, :], chunks(G[:, d, :])[:, :, GCH - 1]))
                    if d == 1:
                        kit.dve(nc.vector.tensor_tensor(B[:, 1, :], A[:, 1, :], G[:, 1, :], ALU.subtract))
                        nc.vector.tensor_tensor(chunks(G[:, 1, :]), chunks(B[:, 1, :]), lastb(1), ALU.add
                                                ).then_inc(s_G, 1)
                        dve.wait_ge(s_G, 2)
                    nc.vector.tensor_tensor(chunks(B[:, d, :]), lastb(d), chunks(G[:, d, :]), ALU.subtract
                                            ).then_inc(s_D, 1)
                qk = flat(gqk[:, :, :])
                for d in range(2):
                    dve.wait_ge(s_ee, d + 1)
                    nc.vector.tensor_tensor(k_end[:, d, :], qk[:, W:2 * W], B[:, d, :], ALU.mult).then_inc(s_end, 1)
                    dve.wait_ge(s_ek, d + 1)
                    kit.dve(nc.vector.tensor_tensor(k_in[:, d, :], qk[:, W:2 * W], A[:, d, :], ALU.mult))
                    dve.wait_ge(s_eq, d + 1)
                    nc.vector.scalar_tensor_tensor(q_in[:, d, :], qk[:, 0:W], GK ** -0.5, E[:, d, :], ALU.mult,
                                                   ALU.mult).then_inc(s_in, 1)
                dve.wait_ge(s_in, 2)

                def masked(h):
                    dve.wait_ge(s_A, h + 1)
                    if h >= 2:
                        dve.wait_ge(s_O, h - 1)
                    for d, mask in enumerate(("incl", "anti")):
                        kit.dve(nc.vector.tensor_tensor(
                            tmp[:, d, :].rearrange("p (t c) -> p t c", t=ST),
                            ps[:, h % 2, d * S:(d + 1) * S].rearrange("p (t c) -> p t c", t=ST),
                            kit.c(mask).unsqueeze(1).broadcast_to([P, ST, P]), ALU.mult))
                    nc.vector.tensor_tensor(flat(AT[:, h % 2, :, :]), tmp[:, 0, :], tmp[:, 1, :],
                                            ALU.add).then_inc(s_AT, 1)

                def add_updates(h):
                    dve.wait_ge(s_U, h + 1)
                    for n in range(3):
                        for d in range(2):
                            c = n if d == 0 else NCH - 1 - n
                            u = update(d, n)
                            if n == 0:
                                kit.dve(nc.vector.tensor_copy(states[:, h % 2, d, 0, :], u))
                            else:
                                step = nc.vector.scalar_tensor_tensor(states[:, h % 2, d, n, :],
                                                                      states[:, h % 2, d, n - 1, :],
                                                                      dec[:, d, h * NCH + c:h * NCH + c + 1], u,
                                                                      ALU.mult, ALU.add)
                                if (n, d) == (2, 1):
                                    step.then_inc(s_st, 1)
                                else:
                                    kit.dve(step)
                in_steps(GH, ((0, masked), (0, add_updates)))

            @block.scalar
            def _(act):
                for d in range(2):
                    nc.scalar.activation(B[:, d, :], A[:, d, :], ACT.Abs).then_inc(s_abs, 1)
                for d in range(2):
                    act.wait_ge(s_abs, d + 1)
                    nc.scalar.activation(E[:, d, :], B[:, d, :], ACT.Exp, scale=-1.0).then_inc(s_e, 1)
                for d in range(2):
                    act.wait_ge(s_e, d + 1)
                    nc.scalar.activation(B[:, d, :], E[:, d, :], ACT.Ln, bias=1.0).then_inc(s_ln, 1)
                for d in range(2):
                    act.wait_ge(s_G, d + 1)
                    nc.scalar.activation(A[:, d, :], G[:, d, :], ACT.Exp, scale=-G16).then_inc(s_ek, 1)
                    nc.scalar.activation(E[:, d, :], G[:, d, :], ACT.Exp, scale=G16).then_inc(s_eq, 1)
                    act.wait_ge(s_D, d + 1)
                    nc.scalar.activation(B[:, d, :], B[:, d, :], ACT.Exp, scale=G16).then_inc(s_ee, 1)
                kit.act(nc.scalar.activation(flat(dec[:, :, :]), flat(last[:, :, :]), ACT.Exp, scale=G16))
                act.wait_ge(s_in, 2)
                for g in range(4):
                    act.wait_ge(s_kt, g + 1)
                    nc.scalar.activation(krow[:, g // 2, g % 2, :], ps[:, g, :], ACT.Copy).then_inc(s_kr, 1)
                bring_root(kit)
                for h in range(GH):
                    act.wait_ge(s_O, h + 1)
                    head_rows(kit, orow, ps[:, 5 + h % 2, :], h, GH, GV).then_inc(s_oo, 1)
        gated_norm(kit, orow, gr, GH, GV, outT, lambda k: kit.cols("gla_norm_w", k))


def head_rows(kit, orow, src, h, heads, width):
    nc = kit.nc
    kit.act(nc.scalar.activation(orow[:, :, h * width:(h + 1) * width], src.rearrange("p (t v) -> p t v", t=ST),
                                 ACT.Copy))
    for t in range(ST):
        j = 8 + t * heads + h
        half = src[:, t * width:(t + 1) * width]
        ins = nc.scalar.activation(half, half, ACT.Square, accum_out=kit.stat[:, j:j + 1])
    return ins


def gated_norm(kit, orow, gate, heads, width, outT, wcol):
    nc, ps = kit.nc, kit.ps
    tiles = heads * width // P
    n = heads * ST
    s_mean, s_rms, s_rows, s_turn, s_od, s_oa = kit.gated_norm
    r, rows0, turned = kit.gated_norms
    kit.gated_norms = (r + 1, rows0 + n, turned + tiles)
    stat = kit.stat
    with nc.Block() as block:
        @block.scalar
        def _(act):
            bring_root(kit, 32)
            act.wait_ge(s_mean, r + 1)
            nc.scalar.activation(stat[:, 24:24 + n], stat[:, 16:16 + n], ACT.Sqrt).then_inc(s_rms, 1)
            for k in range(1, tiles, 2):
                act.wait_ge(s_turn, turned + k + 1)
                nc.scalar.activation(outT[:, k, :], ps[:, 4 + k % 4, 0:S], ACT.Identity,
                                     scale=wcol(k) if wcol else 1.0).then_inc(s_oa, 1)

        @block.vector
        def _(dve):
            nc.vector.tensor_scalar(stat[:, 16:16 + n], stat[:, 8:8 + n], 1.0 / width, NORM_EPS, ALU.mult,
                                    ALU.add).then_inc(s_mean, 1)
            dve.wait_ge(s_rms, r + 1)
            kit.dve(nc.vector.reciprocal(stat[:, 8:8 + n], stat[:, 24:24 + n]))
            for t in range(ST):
                for h in range(heads):
                    a, b = h * width, (h + 1) * width
                    j = 8 + t * heads + h
                    nc.vector.scalar_tensor_tensor(orow[:, t, a:b], orow[:, t, a:b], stat[:, j:j + 1],
                                                   gate[:, t, a:b], ALU.mult, ALU.mult).then_inc(s_rows, 1)
            for k in range(0, tiles, 2):
                dve.wait_ge(s_turn, turned + k + 1)
                if wcol:
                    i_ = nc.vector.tensor_scalar(outT[:, k, :], ps[:, 4 + k % 4, 0:S], wcol(k), None, ALU.mult)
                else:
                    i_ = nc.vector.tensor_copy(outT[:, k, :], ps[:, 4 + k % 4, 0:S])
                i_.then_inc(s_od, 1)

        @block.tensor
        def _(pe):
            pe.wait_ge(s_rows, rows0 + n)
            for k in range(tiles):
                if k >= 4:
                    pe.wait_ge(s_oa if k % 2 else s_od, turned // 2 + (k - 4) // 2 + 1)
                for t in range(ST):
                    i_ = nc.tensor.transpose(ps[:, 4 + k % 4, t * P:(t + 1) * P], orow[:, t, k * P:(k + 1) * P],
                                             kit.c("ident"))
                i_.then_inc(s_turn, 1)


class Ada:

    def __init__(self, kit, w, acc, free=None):
        self.kit, self.w, self.acc, self.free = kit, w, acc, free

    def load(self, sp, lead, j, m):
        kit = self.kit
        if self.free:
            sp.wait_ge(*self.free)
            self.free = None
        a = 8 * lead + m
        if a >= 2:
            sp.wait_ge(kit.ada_acc, 2 * (a - 1) + 16 * j)
        w = kit.ins["w_ada_2"][0]
        sp.dma_start(self.w[:, m % 2, :, :], w[2 * m * P:2 * (m + 1) * P, ds(2 * UN * lead + 2 * UN * j, 2 * UN)]
                     .rearrange("(k p) n -> p k n", p=P)).then_inc(kit.ada_w[m % 2], 16)

    def product(self, dve, lead, j, s):
        nc, kit = self.kit.nc, self.kit
        m, k = s // 2, s % 2
        if s == 0 and lead:
            dve.wait_ge(kit.ada_sum, lead + j)
        if k == 0:
            dve.wait_ge(kit.ada_w[m % 2], 64 * lead + 64 * j + 16 * (m // 2 + 1))
        w, c = self.w[:, m % 2, k, :], kit.cols("c_2", s)
        if s:
            dve.wait_ge(kit.ada_acc, 16 * lead + s + 16 * j)
            step = nc.vector.scalar_tensor_tensor(self.acc, w, c, self.acc, ALU.mult, ALU.add)
        else:
            step = nc.vector.tensor_scalar(self.acc, w, c, None, ALU.mult)
        step.then_inc(kit.ada_acc, 1)

    def sums(self, pe, lead, j):
        nc, kit = self.kit.nc, self.kit
        pe.wait_ge(kit.ada_acc, 16 * lead + 16 * j)
        if lead > 1:
            pe.wait_ge(kit.ada_out, lead - 1 + j)
        for q in range(8):
            step = nc.tensor.matmul(kit.ps[:, 6, q:q + 1], lhsT=self.acc[:, q * P:(q + 1) * P],
                                    rhs=kit.c("ones")[:, 0:1], start=True, stop=True)
        step.then_inc(kit.ada_sum, 1)

    def copy(self, dve, lead, j):
        kit = self.kit
        dve.wait_ge(kit.ada_sum, lead + j)
        a = 8 * (lead - 1)
        kit.nc.vector.tensor_tensor(kit.modcols[:, ds(a + 8 * j, 8)], kit.ps[:, 6, 0:8],
                                    kit.col[:, ds(COLS["b_ada_2"] + a + 8 * j, 8)], ALU.add).then_inc(kit.ada_out, 1)


def stage_glu(kit, norm, ada, act_out, tmp, w_gate, w_up, head_next):
    nc = kit.nc
    first = kit.units
    uses = list(kit.pairs)
    turns = F1 // UN
    lead = kit.ada_groups
    pairs = turns // 2
    kit.ada_groups += pairs
    xbase = kit.x_splits
    kit.x_splits += 4
    s_glu = kit.sem("glu_out")
    outf = flat(act_out)

    def in_turns(eng, body):
        body(0, 0, 0, False)
        body(1, 0, 1, False)
        with eng.Fori(1, pairs) as j:
            body(2 * j, j, 0, True)
            body(2 * j + 1, j, 1, False)
        body(turns - 1, pairs, None, True)

    with nc.Block() as block:
        @block.sync
        def _(sp):
            def body(i, j, half, _):
                for m in range(8):
                    if half is not None and m % 2 == 0:
                        ada.load(sp, lead, j, 4 * half + m // 2)
                    if m < 4:
                        load(kit, sp, first // 2 + 4 + m, i, block_src(w_up, m, UN * i))
                    elif half is not None:
                        load(kit, sp, first // 2 + 4 + m, i, block_src(w_gate, m - 4, UN * i + UN))
            in_turns(sp, body)
            head_next(sp, first // 2 + 8 * turns)

        @block.tensor
        def _(pe):
            def body(i, j, _, summed):
                mid = (lambda: ada.sums(pe, lead, j)) if summed else None
                multiply_block(kit, pe, "T", 0, first, i, uses[0], xbase, mid)
                multiply_block(kit, pe, "T", 1, first + 8, i, uses[1], None)
            norm.turn(pe)
            in_turns(pe, body)

        @block.scalar
        def _(act):
            norm.root(act)
            split_x_hi(kit, act, norm)

            def body(i, *_):
                for u in range(8):
                    split_hi(kit, act, first + AHEAD + u, i)
                act.wait_ge(kit.weights_used, first + 8 + 16 * i)
                act.wait_ge(s_glu, 1 + i)
                nc.scalar.activation(tmp, flat(kit.ps[:, 0:2, :]), ACT.Silu).then_inc(kit.pair_free[0], 1)
                for u in range(8):
                    split_hi(kit, act, first + AHEAD + 8 + u, i)
            in_turns(act, body)

        @block.vector
        def _(dve):
            nc.vector.memset(kit.stat[:, 63:64], 0.0).then_inc(s_glu, 1)
            norm.scales(dve)
            split_x_lo(kit, dve, xbase, norm)

            def body(i, j, half, summed):
                for s in range(16):
                    split_lo(kit, dve, first + AHEAD + s, i)
                    if summed and s == 0:
                        ada.copy(dve, lead, j)
                    if half is not None and s % 2 == 0:
                        ada.product(dve, lead, j, 8 * half + s // 2)
                dve.wait_ge(kit.pair_free[0], uses[0] + 2 + i)
                dve.wait_ge(kit.weights_used, first + 16 + 16 * i)
                dve.wait_ge(kit.pair_free[1], uses[1] + 1 + i)
                nc.vector.tensor_tensor(outf[:, ds(4 * S * i, 4 * S)], tmp, flat(kit.ps[:, 2:4, :]),
                                        ALU.mult).then_inc(s_glu, 1)
                dve.wait_ge(s_glu, 2 + i)
                nc.vector.memset(kit.stat[:, 62:63], 0.0).then_inc(kit.pair_free[1], 1)
            in_turns(dve, body)
    kit.units = first + 16 * turns
    kit.pairs = [u + turns for u in uses]


def modulation(kit, n):
    scale, a = ((KT, COLS["norm_mix_2"]), (4 * KT, COLS["norm_ffn_2"]))[n]
    kit.dve(kit.nc.vector.scalar_tensor_tensor(kit.modT[:, KT * n:KT * (n + 1)], kit.modcols[:, scale:scale + KT], 1.0,
                                               kit.col[:, a:a + KT], ALU.add, ALU.mult))


class Row:

    def __init__(self, kit, at, row):
        self.kit, self.at, self.row, self.before = kit, at, row, kit.row_copies
        kit.row_copies += 4

    def spread(self, pe):
        kit = self.kit
        if self.before:
            pe.wait_ge(kit.row_copied, self.before)
        for k in range(KT):
            ins = kit.nc.tensor.matmul(kit.ps[:, 4 + k // 4, (k % 4) * P:(k % 4 + 1) * P],
                                       lhsT=kit.modcols[:, self.at + k:self.at + k + 1].broadcast_to([P, P]),
                                       rhs=kit.c("ident"), start=True, stop=True)
            if k % 4 == 3:
                ins.then_inc(kit.row_spread, 1)

    def copy(self, act):
        kit = self.kit
        for q in range(4):
            act.wait_ge(kit.row_spread, self.before + q + 1)
            kit.nc.scalar.activation(self.row[:, q * UN:(q + 1) * UN], kit.ps[:, 4 + q, :], ACT.Copy
                                     ).then_inc(kit.row_copied, 1)


def stage_retention(kit, rqk, rvg, outT):
    nc, ps = kit.nc, kit.ps
    table_ready = kit.loads(1)
    s_S, s_PT, s_O, s_oo = (kit.sem("ret_" + n) for n in ("products", "decayed", "out", "rows"))
    with ExitStack() as st:
        decay = kit.sb("ret_decay", [P, RH, S], st)
        PT = kit.sb("ret_PT", [P, 2, 3 * P], st)
        orow = kit.sb("ret_rows", [P, ST, RH * RV], st)
        with nc.Block() as block:
            @block.sync
            def _(sp):
                sp.dma_start(flat(decay[:, :, :]), kit.const_src("retdecay")).then_inc(kit.loaded, 16)

            @block.tensor
            def _(pe):
                def products(h):
                    hb, tile, b = RK * (h % 2), h // 2, h % 2
                    if h >= 2:
                        pe.wait_ge(s_PT, h - 1)
                    for jt in range(ST):
                        a = jt * P
                        ins = nc.tensor.matmul(ps[:, b, jt * S:jt * S + S - a],
                                               lhsT=rqk[hb:hb + RK, 2 + tile, a:a + P],
                                               rhs=rqk[hb:hb + RK, tile, a:S], start=True, stop=True)
                    ins.then_inc(s_S, 1)

                products(0)
                for h in range(RH):
                    if h + 1 < RH:
                        products(h + 1)
                    pe.wait_ge(s_PT, h + 1)
                    if h >= 2:
                        pe.wait_ge(s_oo, h - 1)
                    v = lambda jt: rvg[:, jt, h * RV:(h + 1) * RV]
                    b = h % 2
                    nc.tensor.matmul(ps[:, 2 + b, 0:RV], lhsT=PT[:, b, 0:P], rhs=v(0), start=True, stop=True)
                    nc.tensor.matmul(ps[:, 2 + b, RV:2 * RV], lhsT=PT[:, b, P:2 * P], rhs=v(0), start=True,
                                     stop=False)
                    nc.tensor.matmul(ps[:, 2 + b, RV:2 * RV], lhsT=PT[:, b, 2 * P:3 * P], rhs=v(1), start=False,
                                     stop=True).then_inc(s_O, 1)

            @block.vector
            def _(dve):
                dve.wait_ge(kit.loaded, table_ready)
                for h in range(RH):
                    dve.wait_ge(s_S, h + 1)
                    if h >= 2:
                        dve.wait_ge(s_O, h - 1)
                    kit.dve(nc.vector.tensor_tensor(PT[:, h % 2, 0:S], ps[:, h % 2, 0:S], decay[:, h, :], ALU.mult))
                    nc.vector.tensor_tensor(PT[:, h % 2, S:S + P], ps[:, h % 2, S:S + P], decay[:, h, 0:P],
                                            ALU.mult).then_inc(s_PT, 1)

            @block.scalar
            def _(act):
                nc.scalar.activation(rvg[:, :, RH * RV:], rvg[:, :, RH * RV:], ACT.Silu)
                bring_root(kit)
                for h in range(RH):
                    act.wait_ge(s_O, h + 1)
                    head_rows(kit, orow, ps[:, 2 + h % 2, 0:2 * RV], h, RH, RV).then_inc(s_oo, 1)
        gated_norm(kit, orow, rvg[:, :, RH * RV:], RH, RV, outT, None)


def stage_moba(kit, mqk, mv, outT):
    nc, ps = kit.nc, kit.ps
    (s_logits, s_biased, s_max, s_neg, s_exp, s_recip, s_p, s_turned, s_pT, s_out, s_done) = (
        kit.sem("moba_" + n) for n in ("logits", "biased", "max", "negmax", "exp", "recip", "probs",
                                       "turned", "probsT", "out", "stored"))
    table_ready = kit.loads(1)
    span = ((0, P), (P, P + S))
    with ExitStack() as st:
        dist = kit.sb("distance", [P, ST, S], st)
        L = kit.sb("moba_logits", [P, 2, 3 * P], st)
        E = kit.sb("moba_exp", [P, 3, 3 * P], st)
        ET = kit.sb("moba_probsT", [P, 2, 3 * P], st)
        sc = kit.sb("moba_sc", [P, 3, 4, ST], st)
        mx, neg, tot, rec = (sc[:, :, n, :] for n in range(4))
        with nc.Block() as block:
            @block.sync
            def _(sp):
                sp.dma_start(flat(dist[:, :, :]), kit.const_src("distance")).then_inc(kit.loaded, 16)

            @block.tensor
            def _(pe):
                def logits(h):
                    if h >= 2:
                        pe.wait_ge(s_biased, ST * (h - 1))
                    for t in range(ST):
                        a, b = span[t]
                        ins = nc.tensor.matmul(ps[:, h % 2, a:b], lhsT=mqk[:, h, t * P:(t + 1) * P],
                                               rhs=mqk[:, MH + h, 0:b - a], start=True, stop=True)
                    ins.then_inc(s_logits, 1)

                def turn(h):
                    pe.wait_ge(s_p, ST * (h + 1))
                    if h >= 2:
                        pe.wait_ge(s_pT, h - 1)
                    for n in range(3):
                        ins = nc.tensor.transpose(ps[:, 2 + h % 2, n * P:(n + 1) * P],
                                                  E[:, h % 3, n * P:(n + 1) * P], kit.c("ident"))
                    ins.then_inc(s_turned, 1)

                def sums(h):
                    b = h % 2
                    pe.wait_ge(s_pT, h + 1)
                    if h >= 2:
                        pe.wait_ge(s_done, h - 1)
                    nc.tensor.matmul(ps[:, 4 + b, 0:S], lhsT=mv[:, 0, h * MD:(h + 1) * MD], rhs=ET[:, b, 0:S],
                                     start=True, stop=False)
                    nc.tensor.matmul(ps[:, 4 + b, P:S], lhsT=mv[:, 1, h * MD:(h + 1) * MD], rhs=ET[:, b, S:S + P],
                                     start=False, stop=True).then_inc(s_out, 1)
                in_steps(MH, ((0, logits), (4, turn), (6, sums)))

            @block.vector
            def _(dve):
                dve.wait_ge(kit.loaded, table_ready)

                def biased(h):
                    slope = 2.0 ** (-8.0 * (h + 1) / MH)
                    dve.wait_ge(s_logits, h + 1)
                    if h >= 2:
                        dve.wait_ge(s_exp, ST * (h - 1))
                    for t in range(ST):
                        x, y = span[t]
                        nc.vector.scalar_tensor_tensor(L[:, h % 2, x:y], dist[:, t, 0:y - x], -slope,
                                                       ps[:, h % 2, x:y], ALU.mult, ALU.add).then_inc(s_biased, 1)

                def maximum(h):
                    dve.wait_ge(s_biased, ST * (h + 1))
                    if h >= 3:
                        dve.wait_ge(s_p, ST * (h - 2))
                    for t in range(ST):
                        x, y = span[t]
                        nc.vector.tensor_reduce(mx[:, h % 3, t:t + 1], L[:, h % 2, x:y], AX, ALU.max
                                                ).then_inc(s_max, 1)

                def negated(h):
                    dve.wait_ge(s_max, ST * (h + 1))
                    nc.vector.tensor_scalar(neg[:, h % 3, :], mx[:, h % 3, :], -1.0, None, ALU.mult
                                            ).then_inc(s_neg, 1)

                def recip(h):
                    dve.wait_ge(s_exp, ST * (h + 1))
                    nc.vector.reciprocal(rec[:, h % 3, :], tot[:, h % 3, :]).then_inc(s_recip, 1)

                def probs(h):
                    dve.wait_ge(s_recip, h + 1)
                    for t in range(ST):
                        x, y = span[t]
                        nc.vector.tensor_scalar(E[:, h % 3, x:y], E[:, h % 3, x:y], rec[:, h % 3, t:t + 1], None,
                                                ALU.mult).then_inc(s_p, 1)

                def copy(h):
                    dve.wait_ge(s_out, h + 1)
                    nc.vector.tensor_copy(outT[:, h, :], ps[:, 4 + h % 2, 0:S]).then_inc(s_done, 1)
                in_steps(MH, ((1, biased), (3, recip), (1, maximum), (3, probs), (1, negated), (7, copy)))

            @block.scalar
            def _(act):
                def exp(h):
                    act.wait_ge(s_neg, h + 1)
                    if h >= 3:
                        act.wait_ge(s_turned, h - 2)
                    for t in range(ST):
                        x, y = span[t]
                        nc.scalar.activation(E[:, h % 3, x:y], L[:, h % 2, x:y], ACT.Exp,
                                             bias=neg[:, h % 3, t:t + 1], accum_out=tot[:, h % 3, t:t + 1]
                                             ).then_inc(s_exp, 1)

                def copy(h):
                    act.wait_ge(s_turned, h + 1)
                    if h >= 2:
                        act.wait_ge(s_out, h - 1)
                    nc.scalar.activation(ET[:, h % 2, :], ps[:, 2 + h % 2, 0:3 * P], ACT.Copy).then_inc(s_pT, 1)
                in_steps(MH, ((2, exp), (5, copy)))


def stage_rwkv(kit, rw, low, outT):
    nc, ps, ins = kit.nc, kit.ps, kit.ins
    NT = RWW // P
    sem = lambda n: kit.sem("rw_" + n)
    c3 = 3 * NT
    with ExitStack() as st:
        sb = lambda n, shape: kit.sb("rw_" + n, shape, st)
        kap, bet, kt, rt = (sb(n, [P, NT, S]) for n in ("kap", "bet", "kt", "rt"))
        bonus, gate = sb("bonus", [P, NT, S]), sb("gate", [P, NT, S])
        endG = sb("end_decay", [P, NT, NCH])
        gp = sb("gp", [P, NT, S])
        headstat = sb("head_stat", [P, 2, ST * RWH])

        inner = ExitStack()
        new = kit.sb("rw_new", [P, c3, S], inner)
        lnew = kit.sb("rw_lnew", [P, 4, S], inner)
        wup = kit.sb("rw_wup", [DRANK, RWW], inner)
        aup = kit.sb("rw_aup", [ARANK, RWW], inner)
        gup = kit.sb("rw_gup", [P, 2, RWW], inner)
        t1, t2 = kit.sb("rw_t1", [P, NT, S], inner), kit.sb("rw_t2", [P, NT, S], inner)
        up_ready = kit.loads(3)
        s_new, s_shift, s_code, s_z, s_sw, s_sa = (
            sem(n) for n in ("inputs_shifted", "shifted", "codes", "low_products", "decay_gate", "a_gate"))

        def bank_tile(m, base):
            return ps[:, base + m // 2, (m % 2) * S:(m % 2 + 1) * S]

        r, k, v = (new[:, n * NT:(n + 1) * NT, :] for n in range(3))
        G = bonus

        def head_sums(src, bank):
            for t in range(ST):
                for m in range(NT):
                    a = t * RWH + 2 * m
                    i_ = nc.tensor.matmul(ps[:, bank, a:a + 2], lhsT=src[:, m, t * P:(t + 1) * P],
                                          rhs=kit.c("headsum")[:, 0:P:RWN], start=True, stop=True)
            return i_

        def head_spread(stat, bank):
            for m in range(NT):
                for t in range(ST):
                    for par in range(2):
                        a = t * RWH + 2 * m + par
                        q = (m % 2) * S + t * P
                        i_ = nc.tensor.matmul(ps[RWN * par:RWN * (par + 1), bank + m // 2, q:q + P],
                                              lhsT=stat[:, a:a + 1].broadcast_to([P, RWN]), rhs=kit.c("ident"),
                                              start=True, stop=True)
            return i_

        s_kap, s_ka, s_G, s_Gm, s_eG, s_enG, s_eGm, s_sq, s_ss, s_max, s_nrm, s_rec, s_inv, s_rkk, s_sum = (
            sem(n) for n in ("kap", "k_a_factor", "G", "G_before", "exp_G", "exp_minus_G", "exp_G_before", "kk_sq",
                             "kk_sumsq", "kk_max",
                             "kk_norm", "kk_recip", "kk_inverse", "rk_products", "rk_sums"))
        two = lambda ap: ap.rearrange("p (b a) s -> p b (a s)", b=2)
        with nc.Block() as block:
            @block.sync
            def _(sp):
                sp.dma_start(wup[:, :], ins["rwkv_w_up_2"][0]).then_inc(kit.loaded, 16)
                sp.dma_start(aup[:, :], ins["rwkv_a_up_2"][0]).then_inc(kit.loaded, 16)
                sp.dma_start(gup[:, :, :], ins["rwkv_g_up_2"][0].rearrange("(k p) n -> p k n", p=P)
                             ).then_inc(kit.loaded, 16)

            @block.vector
            def _(dve):
                lows = ((DRANK, 0, 1), (ARANK, 1, 2), (P, 2, 4))
                for m, a, b in lows:
                    nc.vector.tensor_tensor(lnew[0:m, a:b, 1:S], low[0:m, a:b, 0:S - 1], low[0:m, a:b, 1:S],
                                            ALU.subtract)
                    kit.dve(nc.vector.tensor_scalar(lnew[0:m, a:b, 0:1], low[0:m, a:b, 0:1], -1.0, None, ALU.mult))
                for q, (m, name, at) in enumerate(((DRANK, "mu_wd", 0), (ARANK, "mu_wa", 0), (P, "mu_wg", 0),
                                                  (P, "mu_wg", 1))):
                    nc.vector.scalar_tensor_tensor(lnew[0:m, q, :], lnew[0:m, q, :], kit.cols(name, at)[0:m, :],
                                                   low[0:m, q, :], ALU.mult, ALU.add).then_inc(s_shift, 1)
                nc.vector.tensor_tensor(new[:, :, 1:S], rw[:, :, 0:S - 1], rw[:, :, 1:S], ALU.subtract)
                kit.dve(nc.vector.tensor_scalar(new[:, :, 0:1], rw[:, :, 0:1], -1.0, None, ALU.mult))
                for q in range(c3):
                    nc.vector.scalar_tensor_tensor(new[:, q, :], new[:, q, :], kit.cols("mu_rkv", q), rw[:, q, :],
                                                   ALU.mult, ALU.add).then_inc(s_new, 1)
                dve.wait_ge(s_sw, NT)
                kit.dve(nc.vector.tensor_scalar(flat(t1[:, :, :]), flat(t1[:, :, :]), -math.exp(-0.5), None, ALU.mult))
                nc.vector.tensor_tensor_scan(flat(G[:, :, :]), kit.c("carry"), flat(t1[:, :, :]), 0.0, ALU.mult, ALU.add
                                             ).then_inc(s_G, 1)
                dve.wait_ge(s_G, 1)
                dve.wait_ge(s_enG, 1)
                nc.vector.tensor_tensor(flat(t1[:, :, :]), flat(G[:, :, :]), flat(t1[:, :, :]), ALU.subtract
                                        ).then_inc(s_Gm, 1)
                dve.wait_ge(s_sa, NT)
                for m in range(NT):
                    nc.vector.tensor_scalar(gp[:, m, :], t2[:, m, :], -1.0, kit.cols("rwkv_k_a_2", m), ALU.add, ALU.mult
                                            ).then_inc(s_ka, 1)
                dve.wait_ge(s_ss, 1)
                nc.vector.tensor_scalar(headstat[:, 0, :], ps[:, 0, 0:ST * RWH], 1e-24, None, ALU.max
                                        ).then_inc(s_max, 1)
                dve.wait_ge(s_nrm, 1)
                nc.vector.reciprocal(headstat[:, 1, :], headstat[:, 1, :]).then_inc(s_rec, 1)
                dve.wait_ge(s_ka, NT)
                kit.dve(nc.vector.scalar_tensor_tensor(flat(k), flat(gp[:, :, :]), 1.0, flat(k), ALU.add, ALU.mult))
                dve.wait_ge(s_inv, 1)
                kit.dve(nc.vector.tensor_tensor(two(kap[:, :, :]), ps[:, 6:8, :], two(kap[:, :, :]), ALU.mult))
                kit.dve(nc.vector.tensor_tensor(flat(gp[:, :, :]), flat(r), flat(k), ALU.mult))
                for m in range(NT):
                    nc.vector.tensor_scalar(gp[:, m, :], gp[:, m, :], kit.cols("rwkv_r_k_2", m), None,
                                            ALU.mult).then_inc(s_rkk, 1)
                dve.wait_ge(s_enG, 1)
                kit.dve(nc.vector.tensor_tensor(flat(bet[:, :, :]), flat(kap[:, :, :]), flat(t2[:, :, :]), ALU.mult))
                kit.dve(nc.vector.tensor_tensor(flat(bet[:, :, :]), flat(bet[:, :, :]), flat(kt[:, :, :]), ALU.mult))
                kit.dve(nc.vector.tensor_tensor(flat(kt[:, :, :]), flat(k), flat(kt[:, :, :]), ALU.mult))
                dve.wait_ge(s_eG, 1)
                kit.dve(nc.vector.tensor_copy(endG[:, :, :], rt[:, :, :].rearrange("p m (c s) -> p m c s", s=CH)
                                              [:, :, :, CH - 1]))
                kit.dve(nc.vector.tensor_tensor(flat(rt[:, :, :]), flat(r), flat(rt[:, :, :]), ALU.mult))
                dve.wait_ge(s_eGm, 1)
                kit.dve(nc.vector.tensor_tensor(flat(kap[:, :, :]), flat(kap[:, :, :]), flat(t1[:, :, :]), ALU.mult))
                dve.wait_ge(s_sum, 1)
                kit.dve(nc.vector.tensor_tensor(two(bonus[:, :, :]), ps[:, 2:4, :], two(v), ALU.mult))

            @block.scalar
            def _(act):
                nc.scalar.activation(headstat[:, 0, 0:1], kit.c("ones")[:, 0:1], ACT.Tanh)
                act.wait_ge(s_shift, 4)
                nc.scalar.activation(lnew[0:DRANK, 0, :], lnew[0:DRANK, 0, :], ACT.Tanh).then_inc(s_code, 1)
                nc.scalar.activation(lnew[:, 2:4, :], lnew[:, 2:4, :], ACT.Sigmoid).then_inc(s_code, 1)
                act.wait_ge(s_z, 1)
                for m in range(NT):
                    nc.scalar.activation(t1[:, m, :], bank_tile(m, 0), ACT.Sigmoid, bias=kit.cols("rwkv_w0_2", m)
                                         ).then_inc(s_sw, 1)
                act.wait_ge(s_z, 2)
                for m in range(NT):
                    nc.scalar.activation(t2[:, m, :], bank_tile(m, 2), ACT.Sigmoid, bias=kit.cols("rwkv_a0_2", m)
                                         ).then_inc(s_sa, 1)
                act.wait_ge(s_new, c3)
                for m in range(NT):
                    nc.scalar.activation(kap[:, m, :], k[:, m, :], ACT.Copy, scale=kit.cols("rwkv_k_k_2", m)
                                         ).then_inc(s_kap, 1)
                act.wait_ge(s_kap, NT)
                nc.scalar.activation(flat(bet[:, :, :]), flat(kap[:, :, :]), ACT.Square).then_inc(s_sq, 1)
                act.wait_ge(s_z, 3)
                kit.act(nc.scalar.activation(flat(gate[:, :, :]), flat(ps[:, 4:6, :]), ACT.Copy))
                act.wait_ge(s_G, 1)
                nc.scalar.activation(flat(rt[:, :, :]), flat(G[:, :, :]), ACT.Exp).then_inc(s_eG, 1)
                nc.scalar.activation(flat(kt[:, :, :]), flat(G[:, :, :]), ACT.Exp, scale=-1.0).then_inc(s_enG, 1)
                act.wait_ge(s_Gm, 1)
                nc.scalar.activation(flat(t1[:, :, :]), flat(t1[:, :, :]), ACT.Exp).then_inc(s_eGm, 1)
                bring_root(kit)
                act.wait_ge(s_max, 1)
                nc.scalar.activation(headstat[:, 1, :], headstat[:, 0, :], ACT.Sqrt).then_inc(s_nrm, 1)

            @block.tensor
            def _(pe):
                pe.wait_ge(kit.loaded, up_ready)
                pe.wait_ge(s_code, 2)
                for base, w, r, q in ((0, wup, DRANK, 0), (2, aup, ARANK, 1)):
                    for m in range(NT):
                        i_ = nc.tensor.matmul(bank_tile(m, base), lhsT=w[:, m * P:(m + 1) * P], rhs=lnew[0:r, q, :],
                                              start=True, stop=True)
                    i_.then_inc(s_z, 1)
                for m in range(NT):
                    for k in range(2):
                        i_ = nc.tensor.matmul(bank_tile(m, 4), lhsT=gup[:, k, m * P:(m + 1) * P],
                                              rhs=lnew[:, 2 + k, :], start=(k == 0), stop=(k == 1))
                i_.then_inc(s_z, 1)
                pe.wait_ge(s_sq, 1)
                head_sums(bet, 0).then_inc(s_ss, 1)
                pe.wait_ge(s_rec, 1)
                head_spread(headstat[:, 1, :], 6).then_inc(s_inv, 1)
                pe.wait_ge(s_rkk, NT)
                for b in range(2):
                    i_ = nc.tensor.matmul(ps[:, 2 + b, :], lhsT=kit.c("headsum"), rhs=two(gp[:, :, :])[:, b, :],
                                          start=True, stop=True)
                i_.then_inc(s_sum, 1)

        srcs = (kap, bet, kt, v)
        kap_r, bet_r, kt_r, v_r = (rw[:, n * NT:(n + 1) * NT, :] if n < 3 else gp for n in range(4))
        kap_r, bet_r, kt_r, v_r = (x.rearrange("p m s -> p (m s)").rearrange("p (t f) -> p t f", t=ST)
                                   for x in (kap_r, bet_r, kt_r, v_r[:, :, :]))
        dsts = (kap_r, bet_r, kt_r, v_r)
        s_tr, s_rows = sem("turned"), sem("rows")
        with nc.Block() as block:
            @block.tensor
            def _(pe):
                for n in range(8):
                    src, t = srcs[n // 2], n % 2
                    for m in range(NT):
                        i_ = nc.tensor.transpose(ps[:, n, m * P:(m + 1) * P], src[:, m, t * P:(t + 1) * P],
                                                 kit.c("ident"))
                    i_.then_inc(s_tr, 1)

            @block.scalar
            def _(act):
                for n in range(8):
                    act.wait_ge(s_tr, n + 1)
                    nc.scalar.activation(dsts[n // 2][:, n % 2, :], ps[:, n, :], ACT.Copy).then_inc(s_rows, 1)
        inner.close()

        RB, RKm = sb("RB_T", [P, ST, 2, 4 * P]), sb("RK_T", [P, ST, 2, 4 * P])
        KxT = low
        Z = sb("Z", [P, ST, RWW])
        solve = ExitStack()
        AT, X, XT, BT = (kit.sb("rw_" + n, [P, ST, 2, 4 * P], solve) for n in ("A_T", "X", "X_T", "B_T"))
        P1, Off, BV = (x.rearrange("p m s -> p (m s)").rearrange("p (two c) -> p two c", two=2) for x in
                       (kap[:, :, :], bet[:, :, :], kt[:, :, :]))
        blocks = [2 ** n for n in range(1, int(math.log2(CH)))]
        NL = len(blocks)
        N = 4 * NL
        s_pr, s_at, s_ev, s_ready, s_off, s_p1, s_p1c, s_m, s_x, s_bv, s_bvc, s_zk = (
            sem(n) for n in ("products", "A_copied", "masked", "inverse_begun", "between", "offX", "offX_copied",
                             "XoffX", "X_updated", "BV", "BV_copied", "Z_Kx"))
        heads4 = lambda ap: ap.rearrange("p (h c) -> p h c", h=4)
        mask4 = lambda name: kit.c(name).unsqueeze(1).broadcast_to([P, 4, P])
        quads = [slice(m * P, (m + 1) * P) for m in range(4)]
        at_step = lambda n: (n // 4, (n // 2) % 2, n % 2)
        with nc.Block() as block:
            @block.tensor
            def _(pe):
                n = 0
                for t in range(ST):
                    a = t * P
                    for lhs, rhs in ((bet, kap), (kap, bet), (kt, kap), (bet, rt), (kt, rt)):
                        for par in range(2):
                            hb = RWN * par
                            if n >= 8:
                                last = n - 8
                                if last % 10 < 2:
                                    pe.wait_ge(s_at, 2 * (last // 10) + last % 10 + 1)
                                else:
                                    pe.wait_ge(s_ev, 8 * (last // 10) + last % 10 - 1)
                            for m in range(NT):
                                i_ = nc.tensor.matmul(ps[:, n % 8, m * P:(m + 1) * P],
                                                      lhsT=lhs[hb:hb + RWN, m, a:a + P],
                                                      rhs=rhs[hb:hb + RWN, m, a:a + P], start=True, stop=True)
                            i_.then_inc(s_pr, 1)
                            n += 1
                pe.wait_ge(s_at, 2 * ST)
                pe.wait_ge(s_ev, 8 * ST)
                for t in range(ST):
                    for h in range(RWH):
                        f = slice(h * RWN, (h + 1) * RWN)
                        i_ = nc.tensor.matmul(ps[:, 6 + t, f], lhsT=BT[:, t, h % 2, quads[h // 2]], rhs=v_r[:, t, f],
                                              start=True, stop=True)
                    i_.then_inc(s_bv, 1)
                pe.wait_ge(s_ready, 2 * ST)

                def off_x(n):
                    level, t, g = at_step(n)
                    pe.wait_ge(s_off, n + 1)
                    if level:
                        pe.wait_ge(s_x, n - 3)
                    if n >= 2:
                        pe.wait_ge(s_p1c, n - 1)
                    for q in quads:
                        i_ = nc.tensor.matmul(ps[:, n % 2, q], lhsT=Off[:, n % 2, q], rhs=X[:, t, g, q], start=True,
                                              stop=True)
                    i_.then_inc(s_p1, 1)

                def x_off_x(n):
                    level, t, g = at_step(n)
                    pe.wait_ge(s_p1c, n + 1)
                    if n >= 2:
                        pe.wait_ge(s_x, n - 1)
                    if level < NL - 1:
                        for q in quads:
                            nc.tensor.matmul(ps[:, 2 + 2 * (n % 2), q], lhsT=XT[:, t, g, q], rhs=P1[:, n % 2, q],
                                             start=True, stop=True)
                    for q in quads:
                        i_ = nc.tensor.matmul(ps[:, 3 + 2 * (n % 2), q], lhsT=P1[:, n % 2, q], rhs=XT[:, t, g, q],
                                              start=True, stop=True)
                    i_.then_inc(s_m, 1)
                in_steps(N, ((0, off_x), (1, x_off_x)))
                pe.wait_ge(s_x, N)
                pe.wait_ge(s_bvc, ST)
                for t in range(ST):
                    for h in range(RWH):
                        hb = RWN * (h % 2)
                        f = slice(h * RWN, (h + 1) * RWN)
                        i_ = nc.tensor.matmul(ps[hb:hb + RWN, 6 + t, quads[h // 2]], lhsT=kap_r[:, t, f],
                                              rhs=XT[:, t, h % 2, quads[h // 2]], start=True, stop=True)
                    i_.then_inc(s_zk, 1)
                    for h in range(RWH):
                        f = slice(h * RWN, (h + 1) * RWN)
                        i_ = nc.tensor.matmul(ps[:, t, f], lhsT=XT[:, t, h % 2, quads[h // 2]], rhs=BV[:, t, f],
                                              start=True, stop=True)
                    i_.then_inc(s_zk, 1)

            @block.vector
            def _(dve):
                for t in range(ST):
                    for n in range(2, 10):
                        kind, par = n // 2, n % 2
                        dve.wait_ge(s_pr, 10 * t + n + 1)
                        src = ps[:, (10 * t + n) % 8, :]
                        if kind == 1:
                            kit.dve(nc.vector.tensor_tensor(heads4(X[:, t, par, :]), heads4(src), mask4("lvl1"),
                                                            ALU.mult))
                            i_ = nc.vector.tensor_tensor(heads4(X[:, t, par, :]), mask4("ident"),
                                                         heads4(X[:, t, par, :]), ALU.subtract)
                        else:
                            dst, mask = {2: (BT, "strict"), 3: (RB, "incl"), 4: (RKm, "incl")}[kind]
                            i_ = nc.vector.tensor_tensor(heads4(dst[:, t, par, :]), heads4(src), mask4(mask), ALU.mult)
                        i_.then_inc(s_ev, 1)
                for n in range(4):
                    _, t, par = at_step(n)
                    dve.wait_ge(s_at, n + 1)
                    xt = heads4(XT[:, t, par, :])
                    kit.dve(nc.vector.tensor_tensor(xt, heads4(AT[:, t, par, :]), mask4("lvlT1"), ALU.mult))
                    nc.vector.tensor_tensor(xt, mask4("ident"), xt, ALU.subtract).then_inc(s_ready, 1)

                def between(n):
                    level, t, g = at_step(n)
                    if n >= 2:
                        dve.wait_ge(s_p1, n - 1)
                    nc.vector.tensor_tensor(heads4(Off[:, n % 2, :]), heads4(AT[:, t, g, :]),
                                            mask4(f"lvlT{blocks[level]}"), ALU.mult).then_inc(s_off, 1)

                def update(n):
                    level, t, g = at_step(n)
                    dve.wait_ge(s_m, n + 1)
                    if level < NL - 1:
                        nc.vector.tensor_tensor(X[:, t, g, :], X[:, t, g, :], ps[:, 2 + 2 * (n % 2), :], ALU.subtract)
                    nc.vector.tensor_tensor(XT[:, t, g, :], XT[:, t, g, :], ps[:, 3 + 2 * (n % 2), :],
                                            ALU.subtract).then_inc(s_x, 1)
                in_steps(N, ((0, between), (2, update)))

            @block.scalar
            def _(act):
                for n in range(4):
                    _, t, par = at_step(n)
                    act.wait_ge(s_pr, 10 * t + par + 1)
                    nc.scalar.activation(AT[:, t, par, :], ps[:, (10 * t + par) % 8, :], ACT.Copy).then_inc(s_at, 1)
                for t in range(ST):
                    act.wait_ge(s_bv, t + 1)
                    nc.scalar.activation(BV[:, t, :], ps[:, 6 + t, :], ACT.Copy).then_inc(s_bvc, 1)
                for n in range(N):
                    act.wait_ge(s_p1, n + 1)
                    if n >= 2:
                        act.wait_ge(s_m, n - 1)
                    nc.scalar.activation(P1[:, n % 2, :], ps[:, n % 2, :], ACT.Copy).then_inc(s_p1c, 1)
                for t in range(ST):
                    act.wait_ge(s_zk, 2 * t + 1)
                    nc.scalar.activation(KxT[:, :, t * P:(t + 1) * P], heads4(ps[:, 6 + t, :]), ACT.Copy)
                    act.wait_ge(s_zk, 2 * t + 2)
                    nc.scalar.activation(Z[:, t, :], ps[:, t, :], ACT.Copy)
        solve.close()

        U, M, YT = sb("U", [P, ST, RWW]), sb("M", [P, NT, RWN]), sb("Y_T", [P, NT, S])
        s_fold, s_pu, s_u, s_y2, s_y1, s_pm, s_M, s_y2c, s_y = (
            sem(n) for n in ("bonus_gated", "U_products", "U", "Y_chunk", "Y_state", "M_products", "M", "Y_copied",
                             "Y"))
        pairs = lambda ap: ap.rearrange("p (m two n) -> p m two n", two=2, n=RWN)
        with nc.Block() as block:
            @block.tensor
            def _(pe):
                for c in range(NCH):
                    t, pb, b = c // 2, CH * (c % 2), c % 2
                    rows_ = slice(pb, pb + CH)
                    cs = slice(c * CH, (c + 1) * CH)
                    if c:
                        pe.wait_ge(s_M, c)
                        for h in range(RWH):
                            hb, m = RWN * (h % 2), h // 2
                            i_ = nc.tensor.matmul(ps[rows_, h % 2, m * RWN:(m + 1) * RWN],
                                                  lhsT=KxT[hb:hb + RWN, m, cs], rhs=M[hb:hb + RWN, m, :],
                                                  start=True, stop=True)
                        i_.then_inc(s_pu, 1)
                        if c >= 3:
                            pe.wait_ge(s_y, c - 2)
                        for h in range(RWH):
                            hb, m = RWN * (h % 2), h // 2
                            i_ = nc.tensor.matmul(ps[hb:hb + RWN, 4 + b, m * CH:(m + 1) * CH],
                                                  lhsT=M[hb:hb + RWN, m, :], rhs=rt[hb:hb + RWN, m, cs],
                                                  start=True, stop=True)
                        i_.then_inc(s_y1, 1)
                    pe.wait_ge(s_u, c + 1)
                    for h in range(RWH):
                        hb, m = RWN * (h % 2), h // 2
                        f = slice(h * RWN, (h + 1) * RWN)
                        o = ps[hb:hb + RWN, 6 + b, m * RWN:(m + 1) * RWN]
                        nc.tensor.matmul(o, lhsT=bet_r[rows_, t, f], rhs=U[rows_, t, f], start=True, stop=False)
                        i_ = nc.tensor.matmul(o, lhsT=kt_r[rows_, t, f], rhs=v_r[rows_, t, f], start=False,
                                              stop=True)
                    i_.then_inc(s_pm, 1)
                    if c >= 2:
                        pe.wait_ge(s_y2c, c - 1)
                    for h in range(RWH):
                        hb, m = RWN * (h % 2), h // 2
                        f = slice(h * RWN, (h + 1) * RWN)
                        q = slice(m * P + pb, m * P + pb + CH)
                        o = ps[hb:hb + RWN, 2 + b, m * CH:(m + 1) * CH]
                        nc.tensor.matmul(o, lhsT=U[rows_, t, f], rhs=RB[rows_, t, h % 2, q], start=True, stop=False)
                        i_ = nc.tensor.matmul(o, lhsT=v_r[rows_, t, f], rhs=RKm[rows_, t, h % 2, q], start=False,
                                              stop=True)
                    i_.then_inc(s_y2, 1)

            @block.vector
            def _(dve):
                for c in range(NCH):
                    t, pb, b = c // 2, CH * (c % 2), c % 2
                    rows_ = slice(pb, pb + CH)
                    if c == 0:
                        nc.vector.tensor_scalar(U[rows_, t, :], Z[rows_, t, :], -1.0, None, ALU.mult
                                                ).then_inc(s_u, 1)
                    else:
                        dve.wait_ge(s_pu, c)
                        kit.dve(nc.vector.scalar_tensor_tensor(
                            pairs(U[rows_, t, :])[:, :, 0, :], ps[rows_, 0, 0:NT * RWN].rearrange(
                                "p (m n) -> p m n", m=NT), -1.0, pairs(Z[rows_, t, :])[:, :, 0, :], ALU.mult,
                            ALU.subtract))
                        nc.vector.scalar_tensor_tensor(
                            pairs(U[rows_, t, :])[:, :, 1, :], ps[rows_, 1, 0:NT * RWN].rearrange(
                                "p (m n) -> p m n", m=NT), -1.0, pairs(Z[rows_, t, :])[:, :, 1, :], ALU.mult,
                            ALU.subtract).then_inc(s_u, 1)
                    dve.wait_ge(s_pm, c + 1)
                    pm = ps[:, 6 + b, 0:NT * RWN]
                    if c < NCH - 1:
                        if c == 0:
                            kit.dve(nc.vector.tensor_copy(flat(M[:, :, :]), pm))
                        else:
                            dve.wait_ge(s_y1, c)
                            kit.dve(nc.vector.tensor_tensor(flat(M[:, :, :]), flat(M[:, :, :]), pm, ALU.add))
                        nc.vector.tensor_tensor(M[:, :, :], M[:, :, :],
                                                endG[:, :, c:c + 1].broadcast_to([P, NT, RWN]), ALU.mult
                                                ).then_inc(s_M, 1)
                    nc.vector.scalar_tensor_tensor(bonus[:, c, :], bonus[:, c, :], kit.cols("rwkv_ln_b_2", c),
                                                   gate[:, c, :], ALU.add, ALU.mult).then_inc(s_fold, 1)
                    if c:
                        dve.wait_ge(s_y1, c)
                        dve.wait_ge(s_y2c, c + 1)
                        y = YT[:, :, c * CH:(c + 1) * CH]
                        nc.vector.tensor_tensor(y, ps[:, 4 + b, 0:NT * CH].rearrange("p (m s) -> p m s", m=NT), y,
                                                ALU.add).then_inc(s_y, 1)
                    dve.wait_ge(s_fold, c + 1)
                    nc.vector.tensor_scalar(gate[:, c, :], gate[:, c, :], kit.cols("rwkv_ln_w_2", c), None, ALU.mult)

            @block.scalar
            def _(act):
                bring_root(kit)
                for c in range(NCH):
                    act.wait_ge(s_y2, c + 1)
                    nc.scalar.activation(YT[:, :, c * CH:(c + 1) * CH],
                                         ps[:, 2 + c % 2, 0:NT * CH].rearrange("p (m s) -> p m s", m=NT), ACT.Copy
                                         ).then_inc(s_y2c, 1)

        sq = sb("y_sq", [P, NT, S])
        s_mean, s_c, s_var, s_ve, s_sd, s_yrec, s_yinv = (
            sem("y_" + n) for n in ("mean", "squares", "var", "var_eps", "sd", "recip", "inverse"))
        with nc.Block() as block:
            @block.tensor
            def _(pe):
                for b in range(2):
                    i_ = nc.tensor.matmul(ps[:, b, :], lhsT=kit.c("headsum"), rhs=two(YT[:, :, :])[:, b, :],
                                          start=True, stop=True)
                i_.then_inc(s_mean, 1)
                pe.wait_ge(s_c, 1)
                head_sums(sq, 2).then_inc(s_var, 1)
                pe.wait_ge(s_yrec, 1)
                head_spread(headstat[:, 1, :], 4).then_inc(s_yinv, 1)

            @block.vector
            def _(dve):
                dve.wait_ge(s_mean, 1)
                kit.dve(nc.vector.scalar_tensor_tensor(two(YT[:, :, :]), ps[:, 0:2, :], -1.0 / RWN, two(YT[:, :, :]),
                                                       ALU.mult, ALU.add))
                nc.vector.tensor_tensor(flat(sq[:, :, :]), flat(YT[:, :, :]), flat(YT[:, :, :]), ALU.mult
                                        ).then_inc(s_c, 1)
                dve.wait_ge(s_var, 1)
                nc.vector.tensor_scalar(headstat[:, 0, :], ps[:, 2, 0:ST * RWH], 1.0 / RWN, GN_EPS, ALU.mult,
                                        ALU.add).then_inc(s_ve, 1)
                dve.wait_ge(s_sd, 1)
                nc.vector.reciprocal(headstat[:, 1, :], headstat[:, 1, :]).then_inc(s_yrec, 1)
                dve.wait_ge(s_yinv, 1)
                kit.dve(nc.vector.tensor_tensor(two(YT[:, :, :]), ps[:, 4:6, :], two(YT[:, :, :]), ALU.mult))
                kit.dve(nc.vector.tensor_tensor(flat(YT[:, :, :]), flat(YT[:, :, :]), flat(gate[:, :, :]), ALU.mult))
                kit.dve(nc.vector.tensor_tensor(flat(outT), flat(YT[:, :, :]), flat(bonus[:, :, :]), ALU.add))

            @block.scalar
            def _(act):
                act.wait_ge(s_ve, 1)
                nc.scalar.activation(headstat[:, 1, :], headstat[:, 0, :], ACT.Sqrt).then_inc(s_sd, 1)


def stage_conv_glu(kit, norm, w, act_out, head_next):
    nc, ps = kit.nc, kit.ps
    first = kit.units
    uses = list(kit.pairs)
    xbase = kit.x_splits
    kit.x_splits += 4
    turns = F2 // UN
    FT = F2 // P
    s_taps, s_base, s_conv, s_silu, s_glu = (kit.sem("conv_" + n) for n in ("taps", "base", "sums", "silu", "glu"))
    c0 = COLS["conv_w0"]
    taps_all = kit.col[:, c0:c0 + 4 * 2 * FT].rearrange("p (j f) -> p j f", j=4)
    outf = flat(act_out)
    per = 2 * 4 * 2
    col0 = (F2, 0)
    with ExitStack() as st:
        y = kit.sb("conv_y", [P, 2, 4, S], st)
        taps = kit.sb("conv_taps", [P, 2, 4, 4], st)
        tile = lambda j, q: ps[:, 2 * j + q // 2, (q % 2) * S:(q % 2 + 1) * S]

        with nc.Block() as block:
            @block.sync
            def _(sp):
                def body(i):
                    load_block(kit, sp, first // 2 + 4, i, w, col0[1] + UN * i)
                    load_block(kit, sp, first // 2 + 8, i, w, col0[0] + UN + UN * i)
                run_turns(sp, 0, turns - 1, body)
                load_block(kit, sp, first // 2 + 4, turns - 1, w, col0[1] + UN * (turns - 1))
                head_next(sp, first // 2 + 8 * turns)

            @block.tensor
            def _(pe):
                def body(i):
                    for j in range(2):
                        multiply_block(kit, pe, "T", j, first + 8 * j, i, uses[j], None if j else xbase)
                norm.turn(pe)
                run_turns(pe, 0, turns, body)

            @block.scalar
            def _(act):
                norm.root(act)
                split_x_hi(kit, act, norm)

                def body(i):
                    for j in range(2):
                        for u in range(8):
                            split_hi(kit, act, first + AHEAD + 8 * j + u, i)
                            if (j, u) == (1, 3):
                                act.wait_ge(kit.pair_free[0], uses[0] + 2 + i)
                                nc.scalar.activation(flat(y[:, 0, :, :]), flat(y[:, 0, :, :]), ACT.Silu
                                                     ).then_inc(s_silu, 1)
                        act.wait_ge(s_taps, 2 + 2 * i)
                        act.wait_ge(kit.weights_used, first + 8 * (j + 1) + 16 * i)
                        act.wait_ge(s_glu, 1 + i)
                        for q in range(4):
                            nc.scalar.activation(y[:, j, q, :], tile(j, q), ACT.Identity, scale=taps[:, j, 2, q:q + 1],
                                                 bias=taps[:, j, 3, q:q + 1]).then_inc(s_base, 1)
                run_turns(act, 0, turns, body)

            @block.vector
            def _(dve):
                nc.vector.memset(kit.stat[:, 63:64], 0.0).then_inc(s_glu, 1)
                norm.scales(dve)
                split_x_lo(kit, dve, xbase, norm)

                def body(i):
                    dve.wait_ge(s_glu, 1 + i)
                    for j in range(2):
                        nc.vector.tensor_copy(taps[:, j, :, :], taps_all[:, :, ds((FT, 0)[j] + 4 * i, 4)]
                                              ).then_inc(s_taps, 1)
                    dve.wait_ge(s_taps, 2 + 2 * i)
                    for j in range(2):
                        for u in range(8):
                            split_lo(kit, dve, first + AHEAD + 8 * j + u, i)
                        for tap in (1, 0):
                            for q in range(4):
                                dve.wait_ge(s_base, 8 * i + 4 * j + 2 * (q // 2) + 2)
                                if tap == 0:
                                    dve.wait_ge(s_conv, per * i + 8 * j + q + 1)
                                b = 2 - tap
                                nc.vector.scalar_tensor_tensor(y[:, j, q, b:S], tile(j, q)[:, 0:S - b],
                                                               taps[:, j, tap, q:q + 1], y[:, j, q, b:S], ALU.mult,
                                                               ALU.add).then_inc(s_conv, 1)
                        dve.wait_ge(s_conv, per * i + 8 * (j + 1))
                        nc.vector.memset(kit.stat[:, 62:63], 0.0).then_inc(kit.pair_free[j], 1)
                    dve.wait_ge(s_silu, 1 + i)
                    nc.vector.tensor_tensor(outf[:, ds(4 * S * i, 4 * S)], flat(y[:, 0, :, :]), flat(y[:, 1, :, :]),
                                            ALU.mult).then_inc(s_glu, 1)
                run_turns(dve, 0, turns, body)
    kit.units = first + 16 * turns
    kit.pairs = [u + turns for u in uses]


def program(nc, ins, at, out):
    with ExitStack() as ctx:
        kit = Kit(nc, ctx, ins, at)
        mem = {"bias_dram": nc.dram_tensor("bias_rows", (AH, 2 * S), F32, kind="Internal")}

        w_in = ins["w_in"][0]
        q0, k0, v0, gq0, gv0, gr0, lr0 = 0, AW, 2 * AW, 3 * AW, 3 * AW + 2 * GH * GK, 3 * AW + 2 * GH * GK + GH * GV, \
            3 * AW + 2 * GH * GK + 2 * GH * GV
        stage_setup(kit, mem, lambda sp, l: load(kit, sp, l, 0, block_src(w_in, l, q0)))
        mix = ctx.enter_context(ExitStack())
        gqk = kit.sb("gqk_T", [P, 2 * GH, S], mix)
        gv = kit.sb("gv_rows", [P, ST, GH * GV], mix)
        gr = kit.sb("gr_rows", [P, ST, GH * GV], mix)
        glr = kit.sb("glr_T", [GRANK, 2, S], mix)
        gw = kit.sb("gate_w", [GRANK, 2, GH * GK], mix)
        att = ctx.enter_context(ExitStack())
        qkT = kit.sb("qk_T", [P, 2 * AW // P, S], att)
        v = kit.sb("v_rows", [P, ST, AW], att)
        wlr = kit.sb("w_lr", [P, KT, 2 * GRANK], att)
        lr_ready = kit.loads(3)
        s_lr = kit.sem("lowrank_codes")
        lr_rows = kit.sb("lr_rows", [P, ST, 2 * GRANK], att)
        lr_copied = kit.act_steps + ST

        def lr_sync(sp):
            sp.dma_start(wlr[:, :, :], w_in[:, lr0:lr0 + 2 * GRANK].rearrange("(k p) n -> p k n", p=P)
                         ).then_inc(kit.loaded, 16)
            sp.dma_start(gw[:, 0, :], ins["gla_gate_w_fwd"][0]).then_inc(kit.loaded, 16)
            sp.dma_start(gw[:, 1, :], ins["gla_gate_w_bwd"][0]).then_inc(kit.loaded, 16)

        def lr_pe(pe):
            pe.wait_ge(kit.loaded, lr_ready)
            for half in range(2):
                pe.wait_ge(kit.n_out[half], KT // 2)
            for t in range(ST):
                for k in range(KT):
                    ins_ = nc.tensor.matmul(kit.ps[:, 5 + 2 * t, 0:2 * GRANK], lhsT=kit.hT[:, k, t * P:(t + 1) * P],
                                            rhs=wlr[:, k, :], start=(k == 0), stop=(k == KT - 1))
                ins_.then_inc(s_lr, 1)

        def lr_act(act):
            for t in range(ST):
                act.wait_ge(s_lr, t + 1)
                kit.act(nc.scalar.activation(lr_rows[:, t, :], kit.ps[:, 5 + 2 * t, 0:2 * GRANK], ACT.Copy))

        class TurnCodes:

            def spread(self, pe):
                pe.wait_ge(kit.act_order, lr_copied)
                for d in range(2):
                    for t in range(ST):
                        ins_ = nc.tensor.transpose(kit.ps[0:GRANK, 4, d * S + t * P:d * S + (t + 1) * P],
                                                   lr_rows[:, t, d * GRANK:(d + 1) * GRANK], kit.c("ident"))
                ins_.then_inc(s_lr, 1)

            def copy(self, act):
                act.wait_ge(s_lr, ST + 1)
                nc.scalar.activation(flat(glr[:, :, :]), kit.ps[0:GRANK, 4, :], ACT.Copy)

        qk_flat = flat(qkT[:, :, :])
        gqk_flat = flat(gqk[:, :, :])

        def T_blocks(w, col, out, n=2, scale=1.0):
            return [Columns("T", w, col + UN * j, out[:, 4 * S * j:4 * S * (j + 1)], scale) for j in range(n)]

        def row_blocks(w, col, out):
            return [Columns("rows", w, col + UN * j, out[:, :, UN * j:UN * (j + 1)]) for j in range(2)]

        def adds_to_x(w):
            return [Columns("rows", w, n, add_at=n) for n in range(0, D, UN)]

        blocks = (T_blocks(w_in, q0, qk_flat, scale=AD ** -0.5) + T_blocks(w_in, k0, qk_flat[:, 8 * S:])
                  + row_blocks(w_in, v0, v) + T_blocks(w_in, gq0, gqk_flat) + row_blocks(w_in, gv0, gv)
                  + row_blocks(w_in, gr0, gr))
        w_out = ins["w_out"][0]

        def new_ada(name, ctx):
            return Ada(kit, kit.sb(f"ada_w_{name}", [P, 2, 2, 2 * UN], ctx), kit.sb(f"ada_acc_{name}", [P, 2 * UN], ctx
                                                                                   )[:, :])

        with ExitStack() as st:
            kit.x_hi_t = kit.sb("h_hi_1", [P, KT, S], st, R32)
            norm = Norm(kit, st, lambda k: kit.cols("attn_norm_w", k))
            stage_product(kit, blocks, lambda sp, l: load_block(kit, sp, l, 0, w_out, 0), norm, new_ada("1", st),
                          (lr_sync, lr_pe, lr_act), rows=[TurnCodes()])
        gates = flat(kit.hT[:, AW // P:, :]).rearrange("p (d w) -> p d w", d=2)
        stage_attention(kit, qkT[:, 0:AW // P, :], qkT[:, AW // P:, :], v, mem["bias_dram"], kit.hT,
                        GlaGates(kit, gw, glr, gr, gates))
        att.close()

        stage_gla(kit, gates, gqk, gv, gr, kit.hT[:, AW // P:, :])
        mix.close()
        w_gate, w_up, w_down = ins["w_gate"][0], ins["w_up"][0], ins["w_down"][0]
        with ExitStack() as st:
            kit.x_hi_t = kit.sb("h_hi_2", [P, KT, S], st, R32)
            stage_product(kit, adds_to_x(w_out), lambda sp, l: load_block(kit, sp, l, 0, w_gate, 0), None,
                          new_ada("2", st))
        with ExitStack() as st:
            kit.x_hi_t = kit.sb("h_hi_3", [P, KT, S], st, R32)
            norm = Norm(kit, st, lambda k: kit.cols("ffn_norm_w", k))
            fin = kit.sb("final_w", [P, D], st)
            actT = kit.sb("act_T", [P, F1 // P, S], st)
            silu = kit.sb("silu", [P, 4 * S], st)

            def down_head(sp, l):
                for k in range(LOADS):
                    load(kit, sp, l + k, 0, wide_src(w_down, P * k))
            stage_glu(kit, norm, new_ada("3", st), actT[:, :, :], silu[:, :], w_gate, w_up, down_head)
            w2 = ins["w_in_2"][0]
            stage_down(kit, w_down, F1 // P, actT, lambda sp, l: load_block(kit, sp, l, 0, w2, 0), fin,
                       ins["final_norm_w"].partition_broadcast(P))
            stage_final_norm(kit, fin)
        modcols = kit.modcols

        def norm_mod(n, ctx):
            return Norm(kit, ctx, lambda k: kit.modT[:, KT * n + k:KT * n + k + 1],
                        lambda k: modcols[:, 3 * KT * n + k:3 * KT * n + k + 1], n)
        st_rw = ctx.enter_context(ExitStack())
        rw = kit.sb("rw_T", [P, 3 * RWW // P, S], st_rw)
        low = kit.sb("low_T", [P, 4, S], st_rw)
        st_moba = ctx.enter_context(ExitStack())
        mqk = kit.sb("mqk_T", [P, 2 * MH, S], st_moba)
        mv = kit.sb("mv_rows", [P, ST, MH * MD], st_moba)
        st_ret = ctx.enter_context(ExitStack())
        rqk = kit.sb("rqk_T", [P, 4, S], st_ret)
        rvg = kit.sb("rvg_rows", [P, ST, 2 * RH * RV], st_ret)
        with ExitStack() as st:
            LW = DRANK + ARANK + GGRANK
            l0 = RCOLS + 3 * RWW
            spans = ((0, DRANK), (DRANK, DRANK + ARANK), (DRANK + ARANK, DRANK + ARANK + P), (DRANK + ARANK + P, LW))
            rwf, rqkf, mqkf = flat(rw[:, :, :]), flat(rqk[:, :, :]), flat(mqk[:, :, :])
            c1, m0 = RCOLS, RCOLS + WCOLS
            blocks = (T_blocks(w2, 0, rqkf, 1) + T_blocks(w2, c1, rwf, 3) + T_blocks(w2, m0, mqkf, scale=MD ** -0.5)
                      + T_blocks(w2, m0 + MH * MD, mqkf[:, 8 * S:]) + row_blocks(w2, 2 * RH * RK, rvg)
                      + row_blocks(w2, m0 + 2 * MH * MD, mv)
                      + [Columns("T", w2, l0, [low[0:b - a, q, :] for q, (a, b) in enumerate(spans)], spans=spans)])
            wo2 = ins["w_out_2"][0]
            kit.x_hi_t = kit.sb("h_hi_4", [P, KT, S], st, R32)
            stage_product(kit, blocks, lambda sp, l: load_block(kit, sp, l, 0, wo2, 0), norm_mod(0, st),
                          new_ada("4", st))
        stage_retention(kit, rqk, rvg, kit.hT[:, 0:4, :])
        st_ret.close()
        stage_moba(kit, mqk, mv, kit.hT[:, 8:16, :])
        st_moba.close()
        stage_rwkv(kit, rw, low, kit.hT[:, 4:8, :])
        st_rw.close()
        w_up2, w_down2 = ins["w_ffn_up_2"][0], ins["w_ffn_down_2"][0]
        gate2 = kit.sb("gate2_row", [P, D])
        with ExitStack() as st:
            gate1 = kit.sb("gate1_row", [P, D], st)
            kit.x_hi_t = kit.sb("h_hi_5", [P, KT, S], st, R32)
            rows = [Row(kit, 2 * KT, gate1), Row(kit, 5 * KT, gate2)]
            stage_product(kit, adds_to_x(wo2), lambda sp, l: load_block(kit, sp, l, 0, w_up2, F2), rows=rows,
                          gate=gate1)
        with ExitStack() as st:
            kit.x_hi_t = kit.sb("h_hi_6", [P, KT, S], st, R32)
            actT = kit.sb("act2_T", [P, F2 // P, S], st)
            fin = kit.sb("final_w2", [P, D], st)

            def down2_head(sp, l):
                for k in range(LOADS):
                    load(kit, sp, l + k, 0, wide_src(w_down2, P * k))
            stage_conv_glu(kit, norm_mod(1, st), w_up2, actT[:, :, :], down2_head)
            stage_down(kit, w_down2, F2 // P, actT, None, fin, ins["norm_final_2"].partition_broadcast(P), gate2)
            stage_final_norm(kit, fin, out)


INPUTS = ["x", "attn_norm_w", "w_in", "rel_bias_table", "gla_gate_w_fwd", "gla_gate_b_fwd", "gla_gate_w_bwd",
          "gla_gate_b_bwd", "gla_norm_w", "w_out", "ffn_norm_w", "w_gate", "w_up", "w_down", "final_norm_w", "c_2",
          "w_in_2", "w_out_2", "rwkv_mu_2", "rwkv_w0_2", "rwkv_w_up_2", "rwkv_a0_2", "rwkv_a_up_2", "rwkv_g_up_2",
          "rwkv_k_k_2", "rwkv_k_a_2", "rwkv_r_k_2", "rwkv_ln_w_2", "rwkv_ln_b_2", "w_ffn_up_2", "ffn_conv_w_2",
          "ffn_conv_b_2", "w_ffn_down_2", "w_ada_2", "b_ada_2", "norm_mix_2", "norm_ffn_2", "norm_final_2"]


def kernel(**inputs):
    import concourse.bacc as bacc
    from concourse.bass_utils import run_bass_kernel_spmd as run

    nc = bacc.Bacc("TRN2", target_bir_lowering=False, num_devices=1)
    consts, at = constants()
    arrays, aps = {}, {}
    for name in INPUTS + ["consts"]:
        a = np.ascontiguousarray(consts if name == "consts" else inputs[name])
        arrays[f"in_{name}_dram"] = a
        aps[name] = nc.dram_tensor(f"in_{name}_dram", a.shape, mybir.dt.from_np(a.dtype), kind="ExternalInput").ap()
    out = nc.dram_tensor("out_0_dram", (1, S, D), F32, kind="ExternalOutput").ap()
    program(nc, aps, at, out)
    return run(nc, [arrays], core_ids=[0]).results[0]["out_0_dram"]
```
